# Optimizing a Trainium2 kernel written in Bass

```python
import math
import numpy as np
import jax
import jax.numpy as jnp
from jax import lax

D_MODEL = 1024
BATCH = 1
SEQ = 256
DEPTH = 2
DEC_BATCH = 8
DEC_SEQ = 8
PAST_LEN = 256
PAGE_SIZE = 128

MIX_W = D_MODEL // 2
HG_DK = 128
HG_HEADS = MIX_W // HG_DK
HG_DV = MIX_W // HG_HEADS
HG_CHUNK = 64
NSA_HD = 64
NSA_HEADS = MIX_W // NSA_HD
NSA_KV_HEADS = 2
NSA_GROUP = NSA_HEADS // NSA_KV_HEADS
KV_W = NSA_KV_HEADS * NSA_HD
CMP_BLOCK = 32
CMP_STRIDE = 16
SLC_BLOCK = 64
TOP_N = 16
WINDOW = 512
WIN_QBLOCK = 128
SLC_QBLOCK = 64
ROPE_THETA = 500000.0
ROPE_DIM = NSA_HD // 4
D_FF = ((8 * D_MODEL // 3) + 127) // 128 * 128
CONV_W = 3
N_BRANCH = 2
NORM_EPS = 1e-6
NEG_INF = -1e30
LB_FLOOR = 1e-30
FORCE_SCORE = 1e9
IN_SIZES = (MIX_W, MIX_W, MIX_W, MIX_W, MIX_W, KV_W, KV_W, KV_W, KV_W, KV_W, KV_W, 3 * NSA_HEADS, N_BRANCH * D_MODEL)

kernel_name = 'hgrn2_nsa_convffn_hybrid_step'

def rmsnorm(x, g):
    x32 = x.astype(jnp.float32)
    y = x32 * lax.rsqrt(jnp.mean(x32 * x32, axis=-1, keepdims=True) + NORM_EPS)
    return (y * g.astype(jnp.float32)).astype(x.dtype)

def rope_partial(x, pos):
    half = ROPE_DIM // 2
    inv = jnp.float32(ROPE_THETA) ** (-jnp.arange(half, dtype=jnp.float32) * 2.0 / ROPE_DIM)
    ang = pos.astype(jnp.float32)[:, None] * inv[None, :]
    cos = jnp.cos(ang)[:, None, :]
    sin = jnp.sin(ang)[:, None, :]
    x32 = x.astype(jnp.float32)
    x1 = x32[..., :half]
    x2 = x32[..., half:ROPE_DIM]
    out = jnp.concatenate([x1 * cos - x2 * sin, x1 * sin + x2 * cos, x32[..., ROPE_DIM:]], axis=-1)
    return out.astype(x.dtype)

def masked_softmax(s, mask):
    s = jnp.where(mask, s.astype(jnp.float32), NEG_INF)
    m = jnp.max(s, axis=-1, keepdims=True)
    e = jnp.where(mask, jnp.exp(s - m), 0.0)
    return e / jnp.maximum(jnp.sum(e, axis=-1, keepdims=True), 1e-30)

def gla_chunked(q, k, v, log_f, s0, chunk):
    B, L, H, DK = q.shape
    DV = v.shape[-1]
    n = L // chunk

    def to_chunks(a):
        return a.reshape(B, n, chunk, H, a.shape[-1]).transpose(1, 0, 3, 2, 4)

    causal = jnp.tril(jnp.ones((chunk, chunk), dtype=bool))[None, None, :, :, None]

    def step(S, inp):
        qc, kc, vc, gc = inp
        b = jnp.cumsum(gc, axis=2)
        inter = jnp.einsum('bhtd,bhde->bhte', qc * jnp.exp(b), S)
        diff = b[:, :, :, None, :] - b[:, :, None, :, :]
        decay = jnp.exp(jnp.where(causal, diff, NEG_INF))
        attn = jnp.einsum('bhtd,bhsd,bhtsd->bhts', qc, kc, decay)
        intra = jnp.einsum('bhts,bhse->bhte', attn, vc)
        b_last = b[:, :, -1, :]
        S_new = jnp.exp(b_last)[..., None] * S + jnp.einsum('bhsd,bhse->bhde', kc * jnp.exp(b_last[:, :, None, :] - b), vc)
        return S_new, inter + intra

    S, o = lax.scan(step, s0, (to_chunks(q), to_chunks(k), to_chunks(v), to_chunks(log_f)))
    return o.transpose(1, 0, 3, 2, 4).reshape(B, L, H, DV), S

def hgrn2_mixer(q_raw, f_raw, i_raw, g_raw, lb, norm_g, s0):
    B, L = q_raw.shape[:2]
    q = jax.nn.silu(q_raw.astype(jnp.float32)) * (HG_DK ** -0.5)
    fr = f_raw.astype(jnp.float32)
    log_f = jnp.logaddexp(jnp.log(jnp.maximum(lb, LB_FLOOR)), jnp.log1p(-lb) + jax.nn.log_sigmoid(fr))
    k = (1.0 - lb) * jax.nn.sigmoid(-fr)
    v = i_raw.astype(jnp.float32)
    o, s_final = gla_chunked(q, k, v, log_f, s0, math.gcd(HG_CHUNK, L))
    o = rmsnorm(o, norm_g) * jax.nn.silu(g_raw.astype(jnp.float32))
    return o.reshape(B, L, HG_HEADS * HG_DV).astype(q_raw.dtype), s_final

def compress_blocks(rows, pe, w1, w2):
    T = rows.shape[1]
    n_cmp = (T - CMP_BLOCK) // CMP_STRIDE + 1
    idx = (jnp.arange(n_cmp) * CMP_STRIDE)[:, None] + jnp.arange(CMP_BLOCK)[None, :]
    blk = rows[:, idx] + pe[None, None, :, None, :].astype(rows.dtype)
    h = jax.nn.gelu(jnp.einsum('bnjgd,jde->bnge', blk, w1))
    return jnp.einsum('bnge,ef->bngf', h, w2)

def nsa_cmp_slc(q, pos, cmp_rows, slc_rows, cmp_pe, cmp_w1, cmp_w2):
    B, L = q.shape[:2]
    T = cmp_rows.shape[1]
    scale = NSA_HD ** -0.5
    qg = q.reshape(B, L, NSA_KV_HEADS, NSA_GROUP, NSA_HD)
    k_cmp = compress_blocks(cmp_rows[:, :, 0], cmp_pe[0], cmp_w1[0], cmp_w2[0])
    v_cmp = compress_blocks(cmp_rows[:, :, 1], cmp_pe[1], cmp_w1[1], cmp_w2[1])
    n_cmp = k_cmp.shape[1]
    c_start = jnp.arange(n_cmp, dtype=jnp.int32) * CMP_STRIDE
    c_end = c_start + CMP_BLOCK - 1
    k_cmp = rope_partial(k_cmp, c_end)
    s = jnp.einsum('blgrd,bngd->blgrn', qg, k_cmp) * scale
    cmask = (c_end[None, :] <= pos[:, None])[None, :, None, None, :]
    p_cmp = masked_softmax(s, cmask)
    o_cmp = jnp.einsum('blgrn,bngd->blgrd', p_cmp.astype(v_cmp.dtype), v_cmp).reshape(B, L, NSA_HEADS, NSA_HD)
    n_slc = -(-T // SLC_BLOCK)
    s_start = jnp.arange(n_slc, dtype=jnp.int32) * SLC_BLOCK
    cover = ((c_start[:, None] < s_start[None, :] + SLC_BLOCK) & (c_start[:, None] + CMP_BLOCK > s_start[None, :])).astype(jnp.float32)
    imp = jnp.einsum('blgrn,ns->blgs', p_cmp, cover)
    blk = jnp.arange(n_slc, dtype=jnp.int32)[None, :]
    cur = (pos // SLC_BLOCK)[:, None]
    forced = ((blk == 0) | (blk == cur) | (blk == cur - 1))[None, :, None, :]
    allowed = (s_start[None, :] <= pos[:, None])[None, :, None, :]
    score = jnp.where(allowed, jnp.where(forced, FORCE_SCORE, imp), NEG_INF)
    n_top = min(TOP_N, n_slc)
    top_val, top_idx = lax.top_k(score, n_top)
    top_ok = top_val > 0.5 * NEG_INF
    pad = n_slc * SLC_BLOCK - T
    rows = jnp.pad(slc_rows, ((0, 0), (0, pad), (0, 0), (0, 0), (0, 0)))
    rows = rows.reshape(B, n_slc, SLC_BLOCK, 2, NSA_KV_HEADS, NSA_HD).transpose(3, 0, 4, 1, 2, 5)
    k_blk, v_blk = rows[0], rows[1]
    bi = jnp.arange(B)[:, None, None, None]
    gi = jnp.arange(NSA_KV_HEADS)[None, :, None, None]
    qb = SLC_QBLOCK if L % SLC_QBLOCK == 0 else L
    nb = L // qb

    def attend_selected(args):
        q_b, pos_b, idx_b, ok_b = args
        idx_t = idx_b.transpose(0, 2, 1, 3)
        kg = k_blk[bi, gi, idx_t]
        vg = v_blk[bi, gi, idx_t]
        sc = jnp.einsum('bqgrd,bgqnkd->bgqrnk', q_b, kg) * scale
        kpos = idx_t[..., None] * SLC_BLOCK + jnp.arange(SLC_BLOCK, dtype=jnp.int32)
        m = (kpos <= pos_b[None, None, :, None, None]) & ok_b.transpose(0, 2, 1, 3)[..., None]
        m = m[:, :, :, None].reshape(B, NSA_KV_HEADS, qb, 1, n_top * SLC_BLOCK)
        p = masked_softmax(sc.reshape(B, NSA_KV_HEADS, qb, NSA_GROUP, n_top * SLC_BLOCK), m)
        p = p.reshape(B, NSA_KV_HEADS, qb, NSA_GROUP, n_top, SLC_BLOCK).astype(vg.dtype)
        return jnp.einsum('bgqrnk,bgqnkd->bqgrd', p, vg)

    def to_blocks(a):
        return a.reshape(B, nb, qb, *a.shape[2:]).swapaxes(0, 1)

    o_slc = lax.map(attend_selected, (to_blocks(qg), pos.reshape(nb, qb), to_blocks(top_idx), to_blocks(top_ok)))
    o_slc = o_slc.swapaxes(0, 1).reshape(B, L, NSA_HEADS, NSA_HD)
    return o_cmp, o_slc

def band_attend(q, qpos, k, v, kpos):
    B, Q = q.shape[:2]
    qg = q.reshape(B, Q, NSA_KV_HEADS, NSA_GROUP, NSA_HD)
    s = jnp.einsum('bqgrd,bkgd->bgrqk', qg, k) * (NSA_HD ** -0.5)
    d = qpos[:, None] - kpos[None, :]
    mask = (d >= 0) & (d <= WINDOW) & (kpos[None, :] >= 0)
    p = masked_softmax(s, mask).astype(v.dtype)
    o = jnp.einsum('bgrqk,bkgd->bqgrd', p, v)
    return o.reshape(B, Q, NSA_HEADS, NSA_HD)

def window_prompt(q, pos, kw, vw):
    B, L = q.shape[:2]
    qb = WIN_QBLOCK if L % WIN_QBLOCK == 0 else L
    nb = L // qb
    idx = jnp.arange(nb, dtype=jnp.int32)[:, None] * qb + jnp.arange(WINDOW + qb, dtype=jnp.int32)[None, :]
    kpad = jnp.pad(kw, ((0, 0), (WINDOW, 0), (0, 0), (0, 0)))
    vpad = jnp.pad(vw, ((0, 0), (WINDOW, 0), (0, 0), (0, 0)))
    kb = kpad[:, idx]
    vb = vpad[:, idx]
    kpos = idx - WINDOW + pos[0]
    qblk = q.reshape(B, nb, qb, NSA_HEADS, NSA_HD)
    o = jax.vmap(band_attend, in_axes=(1, 0, 1, 1, 0), out_axes=1)(qblk, pos.reshape(nb, qb), kb, vb, kpos)
    return o.reshape(B, L, NSA_HEADS, NSA_HD)

def window_sample(q, pos, kw, vw, buf):
    wb = buf.shape[1]
    keys = jnp.concatenate([buf[:, :, 0], kw.astype(buf.dtype)], axis=1)
    vals = jnp.concatenate([buf[:, :, 1], vw.astype(buf.dtype)], axis=1)
    kpos = jnp.concatenate([pos[0] - wb + jnp.arange(wb, dtype=jnp.int32), pos])
    o = band_attend(q, pos, keys, vals, kpos)
    new_buf = jnp.stack([keys[:, -wb:], vals[:, -wb:]], axis=2)
    return o, new_buf

def token_mixer(h, pos, past, w_in, lb, hg_norm, cmp_pe, cmp_w1, cmp_w2, w_branch, w_out):
    B, L, _ = h.shape
    splits = np.cumsum(IN_SIZES)[:-1].tolist()
    hq, hf, hi, hg, nq, kc, vc, ks, vs, kw, vw, ngate, mgate = jnp.split(h @ w_in, splits, axis=-1)

    def heads(a, n):
        return a.reshape(B, L, n, -1)

    if past is None:
        s0 = jnp.zeros((B, HG_HEADS, HG_DK, HG_DV), jnp.float32)
    else:
        s0 = past[3].astype(jnp.float32)
    o_hg, s_hg = hgrn2_mixer(heads(hq, HG_HEADS), heads(hf, HG_HEADS), heads(hi, HG_HEADS), heads(hg, HG_HEADS), lb, hg_norm, s0)
    q = rope_partial(heads(nq, NSA_HEADS), pos)
    new_cmp = jnp.stack([heads(kc, NSA_KV_HEADS), heads(vc, NSA_KV_HEADS)], axis=2)
    new_slc = jnp.stack([rope_partial(heads(ks, NSA_KV_HEADS), pos), heads(vs, NSA_KV_HEADS)], axis=2)
    kw = rope_partial(heads(kw, NSA_KV_HEADS), pos)
    vw = heads(vw, NSA_KV_HEADS)
    if past is None:
        cmp_rows, slc_rows = new_cmp, new_slc
        o_win = window_prompt(q, pos, kw, vw)
        new_win = jnp.stack([kw, vw], axis=2)[:, -min(WINDOW, L):]
    else:
        cmp_rows = jnp.concatenate([past[0], new_cmp.astype(past[0].dtype)], axis=1)
        slc_rows = jnp.concatenate([past[1], new_slc.astype(past[1].dtype)], axis=1)
        o_win, new_win = window_sample(q, pos, kw, vw, past[2])
    o_cmp, o_slc = nsa_cmp_slc(q, pos, cmp_rows, slc_rows, cmp_pe, cmp_w1, cmp_w2)
    g = jax.nn.sigmoid(ngate.astype(jnp.float32)).reshape(B, L, 3, NSA_HEADS, 1)
    o_nsa = g[:, :, 0] * o_cmp + g[:, :, 1] * o_slc + g[:, :, 2] * o_win
    o_nsa = o_nsa.reshape(B, L, MIX_W).astype(h.dtype)
    branches = jnp.einsum('blnc,ncd->blnd', jnp.stack([o_hg, o_nsa], axis=2), w_branch)
    mg = jax.nn.sigmoid(mgate.astype(jnp.float32)).reshape(B, L, N_BRANCH, D_MODEL).astype(h.dtype)
    merged = jnp.sum(mg * branches, axis=2)
    return merged @ w_out, (new_cmp, new_slc, new_win, s_hg)

def conv_ffn(h, conv_past, w_gate_up, conv_w, conv_b, w_down):
    B, L, _ = h.shape
    g, u = jnp.split(h @ w_gate_up, 2, axis=-1)
    if conv_past is None:
        prev = jnp.zeros((B, CONV_W - 1, D_FF), g.dtype)
    else:
        prev = conv_past.astype(g.dtype)
    gfull = jnp.concatenate([prev, g], axis=1)
    conv = lax.conv_general_dilated(gfull, conv_w[:, None, :].astype(gfull.dtype), window_strides=(1,), padding='VALID',
                                    dimension_numbers=('NWC', 'WIO', 'NWC'), feature_group_count=D_FF) + conv_b
    out = (jax.nn.gelu(conv) * u) @ w_down
    return out, gfull[:, -(CONV_W - 1):]

def gather_pages(pool, page_table):
    pages = pool[page_table]
    return pages.reshape(pages.shape[0], pages.shape[1] * pages.shape[2], *pages.shape[3:])

def trunk(x, pos, caches, page_table, weights):
    (norm_mix, w_in, hg_lower, hg_norm, cmp_pe, cmp_w1, cmp_w2, w_branch, w_out,
     norm_ffn, w_gate_up, conv_w, conv_b, w_down, norm_final) = weights
    lbs = jax.nn.softmax(hg_lower.astype(jnp.float32), axis=0)
    lbs = jnp.cumsum(lbs, axis=0) - lbs[0:1]
    out_cmp, out_slc, out_win, out_hg, out_conv = [], [], [], [], []
    for l in range(DEPTH):
        if caches is None:
            past, conv_past = None, None
        else:
            cache_cmp_kv, cache_slc_kv, cache_win_kv, state_hgrn, state_conv = caches
            past = (gather_pages(cache_cmp_kv[l], page_table), gather_pages(cache_slc_kv[l], page_table),
                    cache_win_kv[l], state_hgrn[l])
            conv_past = state_conv[l]
        mix, (c_kv, s_kv, w_kv, s_hg) = token_mixer(rmsnorm(x, norm_mix[l]), pos, past, w_in[l],
                                                     lbs[l].reshape(HG_HEADS, HG_DK), hg_norm[l], cmp_pe[l],
                                                     cmp_w1[l], cmp_w2[l], w_branch[l], w_out[l])
        x = x + mix.astype(x.dtype)
        ff, c_st = conv_ffn(rmsnorm(x, norm_ffn[l]), conv_past, w_gate_up[l], conv_w[l], conv_b[l], w_down[l])
        x = x + ff.astype(x.dtype)
        out_cmp.append(c_kv)
        out_slc.append(s_kv)
        out_win.append(w_kv)
        out_hg.append(s_hg)
        out_conv.append(c_st)
    return rmsnorm(x, norm_final), (jnp.stack(out_cmp), jnp.stack(out_slc), jnp.stack(out_win),
                                    jnp.stack(out_hg), jnp.stack(out_conv))

def setup_inputs(seed: int = 0) -> dict:
    key = jax.random.key(seed)
    k = jax.random.split(key, 24)
    n_pages = PAST_LEN // PAGE_SIZE
    n_pool = (DEC_BATCH * n_pages * 5) // 4
    win_buf = min(WINDOW, PAST_LEN)
    d_in = sum(IN_SIZES)

    def nrm(kk, shape, scale):
        return jax.random.normal(kk, shape, jnp.float32) * scale

    perm = jax.random.permutation(k[0], n_pool)
    page_table = perm[:DEC_BATCH * n_pages].reshape(DEC_BATCH, n_pages).astype(jnp.int32)
    return {
        'x_prompt': nrm(k[1], (BATCH, SEQ, D_MODEL), 1.0),
        'x_sample': nrm(k[2], (DEC_BATCH, DEC_SEQ, D_MODEL), 1.0),
        'cache_cmp_kv': nrm(k[3], (DEPTH, n_pool, PAGE_SIZE, 2, NSA_KV_HEADS, NSA_HD), 1.0),
        'cache_slc_kv': nrm(k[4], (DEPTH, n_pool, PAGE_SIZE, 2, NSA_KV_HEADS, NSA_HD), 1.0),
        'cache_win_kv': nrm(k[5], (DEPTH, DEC_BATCH, win_buf, 2, NSA_KV_HEADS, NSA_HD), 1.0),
        'state_hgrn': nrm(k[6], (DEPTH, DEC_BATCH, HG_HEADS, HG_DK, HG_DV), 0.5),
        'state_conv': nrm(k[7], (DEPTH, DEC_BATCH, CONV_W - 1, D_FF), 1.0),
        'page_table': page_table,
        'norm_mix': 1.0 + nrm(k[8], (DEPTH, D_MODEL), 0.02),
        'w_in': nrm(k[9], (DEPTH, D_MODEL, d_in), D_MODEL ** -0.5),
        'hg_lower': nrm(k[10], (DEPTH, HG_HEADS * HG_DK), 1.0),
        'hg_norm': 1.0 + nrm(k[11], (DEPTH, HG_DV), 0.02),
        'cmp_pe': nrm(k[12], (DEPTH, 2, CMP_BLOCK, NSA_HD), 0.1),
        'cmp_w1': nrm(k[13], (DEPTH, 2, CMP_BLOCK, NSA_HD, NSA_HD), (CMP_BLOCK * NSA_HD) ** -0.5),
        'cmp_w2': nrm(k[14], (DEPTH, 2, NSA_HD, NSA_HD), NSA_HD ** -0.5),
        'w_branch': nrm(k[15], (DEPTH, N_BRANCH, MIX_W, D_MODEL), MIX_W ** -0.5),
        'w_out': nrm(k[16], (DEPTH, D_MODEL, D_MODEL), 0.5 * D_MODEL ** -0.5),
        'norm_ffn': 1.0 + nrm(k[17], (DEPTH, D_MODEL), 0.02),
        'w_gate_up': nrm(k[18], (DEPTH, D_MODEL, 2 * D_FF), D_MODEL ** -0.5),
        'conv_w': nrm(k[19], (DEPTH, CONV_W, D_FF), CONV_W ** -0.5),
        'conv_b': nrm(k[20], (DEPTH, D_FF), 0.02),
        'w_down': nrm(k[21], (DEPTH, D_FF, D_MODEL), 0.5 * D_FF ** -0.5),
        'norm_final': 1.0 + nrm(k[22], (D_MODEL,), 0.02),
    }

def reference(x_prompt, x_sample, cache_cmp_kv, cache_slc_kv, cache_win_kv, state_hgrn, state_conv, page_table,
              norm_mix, w_in, hg_lower, hg_norm, cmp_pe, cmp_w1, cmp_w2, w_branch, w_out,
              norm_ffn, w_gate_up, conv_w, conv_b, w_down, norm_final):
    weights = (norm_mix, w_in, hg_lower, hg_norm, cmp_pe, cmp_w1, cmp_w2, w_branch, w_out,
               norm_ffn, w_gate_up, conv_w, conv_b, w_down, norm_final)
    past_len = page_table.shape[1] * PAGE_SIZE
    pos_p = jnp.arange(x_prompt.shape[1], dtype=jnp.int32)
    pos_s = past_len + jnp.arange(x_sample.shape[1], dtype=jnp.int32)
    y_prompt, st_p = trunk(x_prompt, pos_p, None, None, weights)
    y_sample, st_s = trunk(x_sample, pos_s, (cache_cmp_kv, cache_slc_kv, cache_win_kv, state_hgrn, state_conv),
                           page_table, weights)
    return (y_prompt, y_sample, st_p[0], st_s[0], st_p[1], st_s[1], st_p[2], st_s[2], st_p[3], st_s[3], st_p[4], st_s[4])


_drawn_inputs = setup_inputs


def setup_inputs(seed=0):
    import zlib

    import numpy as np

    out = dict(_drawn_inputs(seed))
    spreads = {}
    factors = {'hg_norm': 8.0,
     'cmp_pe': 4.649,
     'conv_b': 6.484,
     'norm_final': 8.023,
     'cache_slc_kv': 4.069,
     'norm_ffn': 2.72}
    for name, (base, spread) in spreads.items():
        noise = np.random.default_rng([zlib.crc32(name.encode()), seed]).standard_normal(out[name].shape)
        drawn = base * np.exp(spread * noise) if base else spread * noise
        out[name] = jnp.asarray(drawn.astype(out[name].dtype))
    for name, factor in factors.items():
        out[name] = (out[name] * factor).astype(out[name].dtype)
    return out
```

```python
from contextlib import ExitStack

import concourse.bass as bass
from concourse import mybir

F32 = mybir.dt.float32
F32R = mybir.dt.float32r
I32 = mybir.dt.int32
ALU = mybir.AluOpType
ACT = mybir.ActivationFunctionType
AX = mybir.AxisListType

P = 128
D, DEPTH, SEQ, NSEQ, STEPS, PAST = 1024, 2, 256, 8, 8, 256
PAGE, NPAGE, POOLN = 128, 2, 20
MIX, HH, HD = 512, 4, 128
NH, KVH, GRP, ND = 8, 2, 4, 64
KD = D // P
SMP = NSEQ * STEPS
T = SEQ + SMP
DFF = 2816
NJ = DFF // P
JPB = 2
NCB = 15
NCS = NSEQ + 1
CHUNK = 64
NEG = -1e30
EPS = 1e-6
SCALE = ND ** -0.5
DIN = 5400
C_HQ, C_HF, C_HI, C_HG, C_NQ, C_KC, C_KS, C_GT, C_MG = 0, 512, 1024, 1536, 2048, 2560, 2816, 3328, 3352
TM = [P, P, SMP]
LEVELS = [0, 1, 2, 4, 8, 16, 32]
SLOT = 4096
NSLOT = 4
MGB = 6
DOWN = [[6, 6, 5, 5], [8, 8, 6]]

BLOCKS = (["par", "cmp", "w_kvc", "w_kvn", "w_nq", "w_hf", "w_hq", "w_cmp", "w_hi", "w_hg", "kv0", "kv1", "mg0", "mg1",
           "st0", "st1", "br0", "mg2", "br1", "mg3", "wo0", "wo1"] + [f"ff{n}" for n in range(NJ // JPB)]
          + [f"dn{mh}_{n}" for mh in range(2) for n in range(len(DOWN[mh]))])
NBLK = len(BLOCKS)
assert NBLK % NSLOT == 0
BNO = {b: n for n, b in enumerate(BLOCKS)}
DMAS = {b: 1 for b in BLOCKS}
DMAS.update(par=7, cmp=2 * NSEQ, w_kvc=2, w_cmp=4, kv0=4 * NPAGE + 4, kv1=4 * NPAGE + 4, st0=2, st1=2, br0=3,
            br1=3)
for _n in range(4):
    DMAS[f"mg{_n}"] = 2
for _n in range(NJ // JPB):
    DMAS[f"ff{_n}"] = 2
SLOT_TOTAL = [16 * sum(DMAS[b] for b in BLOCKS[s::NSLOT]) for s in range(NSLOT)]
LANDED = {b: 16 * sum(DMAS[c] for c in BLOCKS[n % NSLOT:n + 1:NSLOT]) for b, n in BNO.items()}
LAST_USE = {"par": "cst", "w_kvc": "kvc2", "w_kvn": "kvn2", "w_nq": "nq3", "w_hf": "hf3",
            "w_hq": "hq3", "w_cmp": "vc2", "w_hi": "hi2", "kv0": "ov5", "kv1": "ov7", "w_hg": "hg3"}
LAST_USE.update({f"mg{n}": f"mgb{2 * n + 1}" for n in range(4)})
LAST_USE.update({f"{b}{n}": f"{u}{4 * n + 3}" for b, u in (("br", "brb"), ("wo", "wo")) for n in range(2)})
LAST_USE.update({f"ff{n}": f"u{JPB * n + JPB - 1}" for n in range(NJ // JPB)})
LAST_USE.update({f"dn{mh}_{len(DOWN[mh]) - 1}": f"dn{mh}_3" for mh in range(2)})
SPLIT = [(f"ff{j // JPB}", j % JPB, KD) for j in range(NJ)]
for _mh in range(2):
    for _n, _kn in enumerate(DOWN[_mh]):
        SPLIT += [(f"dn{_mh}_{_n}", 0, (_kn + 1) // 2), (f"dn{_mh}_{_n}", (_kn + 1) // 2, _kn // 2)]
UNIT_COLS = 2048

UNITS = [(i, g) for i in range(2) for g in range(KVH)]


def mm_plan():
    out = [(f"kvc{i}", "A") for i in range(3)] + [(f"kvn{i}", "A") for i in range(3)]
    out += [(f"nq{m}", "A") for m in range(4)] + [(f"hf{h}", "A") for h in range(HH)]
    out += [(f"hq{h}", "V") for h in range(HH)] + [(f"hi{i}", "A") for i in range(3)]
    out += [(f"hg{h}", "V") for h in range(HH)]
    for m in range(KD):
        out += [(f"mga{m}", "A"), (f"mgb{m}", "A")]
    out += [(f"wo{m}", "V") for m in range(KD)]
    for j in range(NJ):
        out += [(f"g{j}", "A"), (f"u{j}", "V")]
    return out + [(f"dn0_{m}", "V") for m in range(4)]


def ax_plan():
    out = [("par", "V"), ("cst", "V"), ("norm1", "A")]
    out += [(f"cc{s}", "AV"[s % 2]) for s in range(NSEQ)]
    out += [("cp", "A"), ("kt0", "A"), ("kt1", "V")]
    out += [(f"nqr{m}", "V") for m in range(4)]
    out += [("hidk", "A"), ("hidv", "A"), ("kcm", "A"), ("kcr", "V")] + [(f"vc{n}", "A") for n in range(3)]
    for n in range(4):
        out += level_plan(2 * n)
        out += [(f"sc{n}_{r}", "V") for r in range(GRP)] + [(f"scc{n}", "V")]
        out += level_plan(2 * n + 1) if 2 * n + 1 < len(LEVELS) else []
        i = UNITS[n][0]
        out += [(f"tp{n}_{x}", "AV"[x % 2]) for x in range(2 * (i + 1))] + [(f"tpc{n}", "A"), (f"ov{n}", "V")]
    out += [("gsel0", "V"), ("gsel1", "V")]
    out += [(f"krt{h}", "AV"[h % 2]) for h in range(HH)]
    for hb in range(2):
        out += [(f"skt{hb}_{x}", "AV"[x % 2]) for x in range(4)]
        out += [(f"ds{c}", "V") for c in (2 * hb, 2 * hb + 1)]
        for g in range(KVH):
            n = 4 + 2 * hb + g
            out += [(f"ssa{n}", "A"), (f"ssb{n}", "A"), (f"tps{n}", "V"), (f"tpn{n}", "A"), (f"ov{n}", "V")]
    for h in range(HH):
        out += [(f"o{h}", "V"), (f"oo{h}", "V"), (f"dsa{h}", "V"), (f"dsb{h}", "V")]
    out += [(f"on{h}", "A") for h in range(HH)]
    for m in range(KD):
        out += [(f"bra{m}", "V"), (f"brb{m}", "V")]
    out += [("norm2", "A")]
    out += [(f"cv{n}", "V") for n in range(6)]
    return out + [(f"dn1_{m}", "V") for m in range(4)]


def level_plan(k):
    return [(f"lv{k}", "V")] + ([(f"lvs{k}", "V")] if LEVELS[k] < STEPS else [])


MM_PLAN, AX_PLAN = mm_plan(), ax_plan()


class Banks:

    def __init__(self, plan, banks, full, emptied):
        self.no = {name: n for n, (name, _) in enumerate(plan)}
        self.plan, self.banks, self.full, self.emptied = plan, banks, full, emptied

    def bank(self, name):
        return self.banks[self.no[name] % len(self.banks)]

    def filled(self, name):
        return self.full, self.no[name] + 1

    def emptied_at(self, name):
        n = self.no[name]
        who = self.plan[n][1]
        return self.emptied[who], sum(1 for _, e in self.plan[:n + 1] if e == who)

    def vacant(self, name):
        n = self.no[name] - len(self.banks)
        return self.emptied_at(self.plan[n][0]) if n >= 0 else None


class Steps:

    def __init__(self, eng):
        self.eng, self.count, self.last = eng, {}, None

    def up(self, sem):
        self.count[sem.name] = self.count.get(sem.name, 0) + 1
        self.last = (sem, self.count[sem.name])
        return sem, 1

    def settled(self):
        return self.last


CONST = {}
_at = 0
for _name, _w in (("ident", P), ("ones", P), ("perm", P), ("cosq", T), ("sinq", T), ("cosk", 48), ("sink", 48),
                  ("ccmp", NCB), ("scmp", NCB), ("causal", 2 * P), ("cneg", 2 * NCB), ("c01", 2 * NCB),
                  ("newneg", 2 * SMP), ("level", 7 * CHUNK), ("sel", 2 * P), ("seqrow", NSEQ), ("rrow", GRP)):
    CONST[_name] = (_at, _at + _w)
    _at += _w
NCONST = _at


def hybrid_step(nc, x_prompt, x_sample, cache_cmp, cache_slc, cache_win, state_hgrn, state_conv, page_table, norm_mix,
                w_in, hg_lower, hg_norm, cmp_pe, cmp_w1, cmp_w2, w_branch, w_out, norm_ffn, w_gate_up, conv_w, conv_b,
                w_down, norm_final, consts, y_p, y_s, cmp_p, cmp_s, slc_p, slc_s, win_p, win_s, hg_p, hg_s, cv_p,
                cv_s):
    ctx = ExitStack()
    with ctx:
        def sb(name, cols, dt=F32):
            return ctx.enter_context(nc.sbuf_tensor(name, [P, cols], dt))

        def sem(name):
            return ctx.enter_context(nc.semaphore(name))

        ring_at = (nc.sbuf_base + 31) // 32 * 32
        ring = sb("ring", NSLOT * SLOT)
        xT = sb("xT", KD * T)[:, :].rearrange("p (k t) -> p k t", k=KD)
        hT_at = (nc.sbuf_base + 31) // 32 * 32
        hT = sb("hT", KD * T)[:, :].rearrange("p (k t) -> p k t", k=KD)
        cst_all = sb("consts", NCONST)
        mixb_at = (nc.sbuf_base + 31) // 32 * 32
        mixb = sb("mixb", 14592)
        attb = sb("attb", 4608)
        work_at = (nc.sbuf_base + 31) // 32 * 32
        work = sb("work", 7048)
        kvb = sb("kvb", 2 * 4 * PAST)
        kvT = kvb[:, :].rearrange("p (w b t) -> p w b t", w=2, b=4)
        qT = work[:, 0:4 * T].rearrange("p (m t) -> p m t", m=4)
        qS = work[:, 1280:1536].rearrange("p (b r s) -> p b r s", b=NSEQ, r=GRP)
        ktn = work[:, 1536:1536 + 2 * T].rearrange("p (w t) -> p w t", w=2)
        vc = work[:, 2176:2176 + NCS * 2 * ND].rearrange("p (s g d) -> p s g d", s=NCS, g=2)
        kcT = work[:, 3328:3328 + NCS * NCB].rearrange("p (s n) -> p s n", s=NCS)
        ctok = work[:, 5000:5768].rearrange("p (i c) -> p i c", i=3)
        stok = work[:, 3464:5000].rearrange("p (i c) -> p i c", i=3)
        oN = work[:, 5768:5768 + 4 * T].rearrange("p (m t) -> p m t", m=4)
        gts = sb("gts", 3 * 24)[:, :].rearrange("p (i c) -> p i c", i=3)
        gsel = sb("gsel", 12)[:, :].rearrange("p (h c) -> p h c", h=2)
        gtmp = sb("gtmp", 24)
        prm = sb("prm", 160)
        cstT = sb("cstT", NJ * 16)[:, :].rearrange("p (j c) -> p j c", j=NJ)
        glast = kvb[:, 512:512 + NJ * 18].rearrange("p (j c) -> p j c", j=NJ)
        lbs = sb("lbs", 8 * 6)
        lbl = sb("lbl", 8)
        pro = sb("pro", 16)
        rs = kvb[:, 0:T]
        pcs = sb("pcs", 64)
        mx = sb("mx", 16)
        nm = sb("nm", 16)
        sm = sb("sm", 16)
        wt = sb("wt", 16)
        rtmp = sb("rtmp", 128)
        hbias = sb("hbias", 2)
        epsb = sb("epsb", 1)
        pages = sb("pages", 16, I32)

        def con(name, rows=P):
            a, b = CONST[name]
            return cst_all[0:rows, a:b]

        ident, ones = con("ident"), con("ones")

        def part(buf, at, cols):
            return buf[:, at:at + cols]

        def heads(at):
            return part(mixb, at, HH * T).rearrange("p (h t) -> p h t", h=HH)

        qH, kH, pH, rH, qL, kL = (heads(1280 * n) for n in range(6))
        oS, sqH, rsH, sgq, oH = rH, kH, qL, kL, qH
        qraw = qL
        vH = part(mixb, 7680, 3 * MIX).rearrange("p (i c) -> p i c", i=3)
        acc = part(mixb, 9216, 3 * 256).rearrange("p (i h t) -> p i h t", i=3, h=HH)
        gH = heads(9984)
        krP = part(mixb, 0, HH * 2 * P).rearrange("p (h i d) -> p h i d", h=HH, i=2)
        krS = part(mixb, 1280 * 5, HH * P).rearrange("p (h d) -> p h d", h=HH)
        craw = part(mixb, 7680, NCS * 512).rearrange("p (s c) -> p s c", s=NCS)
        sP = part(mixb, 11520, 4 * 512).rearrange("p (c h v) -> p c h v", c=4, h=HH)
        vX = part(mixb, 13568, NSEQ * P).rearrange("p (b v) -> p b v", b=NSEQ)
        sq = part(mixb, 0, KD * T).rearrange("p (k t) -> p k t", k=KD)
        ring_r = nc.alloc_sbuf_tensor_at("ring_low", [P, NSLOT * SLOT], F32R, offset=ring_at)
        work_r = nc.alloc_sbuf_tensor_at("high_parts", [P, 2 * UNIT_COLS + KD * T], F32R, offset=work_at)
        act_r = nc.alloc_sbuf_tensor_at("act_parts", [P, 2 * NJ * T], F32R, offset=mixb_at)
        h_low = nc.alloc_sbuf_tensor_at("h_low", [P, KD * T], F32R, offset=hT_at)[:, :].rearrange(
            "p (k t) -> p k t", k=KD)
        h_high = part(work_r, 2 * UNIT_COLS, KD * T).rearrange("p (k t) -> p k t", k=KD)
        act_high, act_low = (part(act_r, NJ * T * n, NJ * T).rearrange("p (j t) -> p j t", j=NJ) for n in range(2))
        xin = part(mixb, 4096, 3 * D).rearrange("p (i c) -> p i c", i=3)
        yout = part(mixb, 4096, 3 * D).rearrange("p (i c) -> p i c", i=3)
        cmpT = attb[:, :].rearrange("p (v g s t) -> p v g s t", v=2, g=2, s=NCS)
        hid = part(attb, 0, 2 * NCS * NCB).rearrange("p (g s n) -> p g s n", g=2, s=NCS)
        kraw = part(attb, 512, NCS * NCB).rearrange("p (s n) -> p s n", s=NCS)
        kt1, kt2 = (part(attb, 1024 + 256 * n, NCS * NCB).rearrange("p (s n) -> p s n", s=NCS) for n in range(2))
        prob = part(attb, 0, 4 * 512).rearrange("p (r w k) -> p r w k", r=GRP, w=2)
        probT = part(attb, 2048, 4 * 512).rearrange("p (x c) -> p x c", x=4)
        probTc = part(attb, 4096, 512)
        sprob = part(attb, 1280, 512).rearrange("p (w k) -> p w k", w=2)
        snew = part(attb, 1792, 2 * SMP).rearrange("p (w k) -> p w k", w=2)
        sprobT = part(attb, 1920, 512).rearrange("p (x c) -> p x c", x=4)
        snewT = part(attb, 2560 + 4 * T, 384).rearrange("p (x c) -> p x c", x=3)
        merged = part(attb, 0, KD * T).rearrange("p (k t) -> p k t", k=KD)
        mgs = part(attb, 2560, MGB * T).rearrange("p (b t) -> p b t", b=MGB)
        GX = SEQ + 2 + NSEQ * (STEPS + 2)
        gext = [part(attb, GX * n, GX) for n in range(2)]
        cvt = [part(attb, 680 + T * n, T) for n in range(2)]
        cvo = part(attb, 1320, DFF)
        S1 = CHUNK

        def slot(b):
            s = BNO[b] % NSLOT
            return ring[:, s * SLOT:(s + 1) * SLOT]

        def unit_of(u, buf):
            b, a, n = SPLIT[u]
            s = (BNO[b] % NSLOT) * SLOT
            if b[:2] == "ff":
                return buf[:, s:s + SLOT].rearrange("p (k h c) -> p k h c", k=KD, h=4)[:, :, a::2, :]
            return buf[:, s + 512 * a:s + 512 * (a + n)].rearrange("p (k h c) -> p k h c", k=n, h=4)

        def unit_high(u):
            b, _, n = SPLIT[u]
            at = UNIT_COLS * (u % 2)
            h = 2 if b[:2] == "ff" else 4
            return work_r[:, at:at + n * h * P].rearrange("p (k h c) -> p k h c", k=n, h=h)

        def kt_of(b, n, width):
            return slot(b)[:, 0:n * width].rearrange("p (k c) -> p k c", k=n)

        mmb = [ctx.enter_context(nc.psum_tensor(f"mm{n}", [P, 512], F32)) for n in range(4)]
        axb = [ctx.enter_context(nc.psum_tensor(f"ax{n}", [P, 512], F32)) for n in range(4)]

        landed = [sem(f"ring_landed{s}") for s in range(NSLOT)]
        arrived, cleared = sem("arrived"), sem("cleared")
        spare = sem("spare")
        consts_in, copied = sem("consts_in"), sem("window_copied")
        first = {}

        def lsem(name):
            s = sem(name)
            first.setdefault("range", []).append(s)
            return s

        down_read = lsem("down_unit_read")
        kv_stored = lsem("keys_and_values_stored")
        w_high, w_low, h_hi, h_lo = lsem("weights_high"), lsem("weights_low"), lsem("h_high"), lsem("h_low_ready")
        stored = lsem("outputs_stored")
        state_stored = [lsem("state_stored0"), lsem("state_stored1")]
        mm_full, mm_act, mm_dve = lsem("mm_full"), lsem("mm_emptied_by_act"), lsem("mm_emptied_by_dve")
        ax_full, ax_act, ax_dve = lsem("ax_full"), lsem("ax_emptied_by_act"), lsem("ax_emptied_by_dve")
        dve_step, act_step, pool_step = lsem("dve_step"), lsem("act_step"), lsem("pool_step")
        squares_dve, squares_act, rs_ready, h_ready = (lsem("squares_dve"), lsem("squares_act"), lsem("rs_ready"),
                                                       lsem("h_ready"))
        x_ready = lsem("x_ready")
        prm_ready = lsem("params_ready")
        k_roped = lsem("k_roped")
        rows_ready = lsem("compressor_rows_ready")
        qraw_ready, q_ready, qs_ready = lsem("qraw_ready"), lsem("q_ready"), lsem("q_sample_ready")
        hid_ready, kraw_ready, kc_ready, hb_ready = (lsem("hidden_ready"), lsem("kcmp_raw_ready"), lsem("kcmp_ready"),
                                                     lsem("hbias_ready"))
        sig_ready, mul_ready = lsem("sigmoid_ready"), lsem("hgrn_inputs_ready")
        ql_ready, kl_ready, r_done = lsem("q_level_ready"), lsem("k_level_ready"), lsem("r_updated")
        p_done = lsem("p_updated")
        max_ready, exp_ready, scaled = lsem("max_ready"), lsem("exp_ready"), lsem("probs_scaled")
        o_ready, vx_ready, s_ready, sn_ready = lsem("o_ready"), lsem("vx_ready"), lsem("state_ready"), lsem("new_state")
        sqo_ready, rso_ready, oh_ready = lsem("o_squares"), lsem("o_rs"), lsem("oh_ready")
        gate_ready, prod_ready, merged_ready = lsem("gate_ready"), lsem("product_ready"), lsem("merged_ready")
        pre_ready, tap_ready, conv_ready, gelu_ready, act_ready = (lsem("prefix_ready"), lsem("tap_ready"),
                                                                   lsem("conv_ready"), lsem("gelu_ready"),
                                                                   lsem("act_ready"))
        glast_ready, cvo_ready, xin_in, y_ready = lsem("glast_ready"), lsem("cvo_ready"), lsem("x_in"), lsem("y_ready")
        reset = first["range"]
        nums = sorted(s.num for s in reset)
        assert nums == list(range(nums[0], nums[0] + len(nums)))

        MM = Banks(MM_PLAN, mmb, mm_full, {"A": mm_act, "V": mm_dve})
        AXR = Banks(AX_PLAN, axb, ax_full, {"A": ax_act, "V": ax_dve})

        down_units = [u for u, (b, _, _) in enumerate(SPLIT) if b[:2] == "dn"]
        down_inner = [u for u in down_units if u + 1 < len(SPLIT) and SPLIT[u + 1][0][:3] == SPLIT[u][0][:3]]

        def unit_read(u):
            if u < NJ:
                return MM.filled(f"u{u}")
            if u in down_inner:
                return down_read, down_inner.index(u) + 1
            return (MM if SPLIT[u][0][2] == "0" else AXR).filled(f"{SPLIT[u][0][:3]}_3")

        def landed_at(b, l):
            return landed[BNO[b] % NSLOT], l * SLOT_TOTAL[BNO[b] % NSLOT] + LANDED[b]

        def depart(eng, l):
            eng.sem_inc(arrived, 1)
            eng.wait_ge(cleared, l + 1)

        block = ctx.enter_context(nc.Block())

        @block.sync
        def _(sp):
            def ld(b, out, in_):
                sp.dma_start(out, in_).then_inc(landed[BNO[b] % NSLOT], 16)

            def page(n, lay):
                pg = sp.value_load(pages[0:1, n:n + 1], min_val=0, max_val=POOLN - 1)
                return lay * POOLN + pg

            def lay1(x, lay):
                return x[bass.DynSlice(lay, 1)] if not isinstance(lay, int) else x[lay:lay + 1]

            def load(b, lay):
                s = slot(b)
                if b == "par":
                    for at, x in ((0, norm_mix), (8, norm_ffn), (16, hg_norm), (17, conv_b)):
                        n = x.shape[1] // P
                        ld(b, s[at:at + n, 0:P], lay1(x, lay).rearrange("o (k p) -> (o k) p", p=P))
                    ld(b, s[39:105, 0:P], lay1(conv_w, lay).rearrange("o w (k p) -> (o w k) p", p=P))
                    ld(b, s[0:32, P:2 * P], lay1(cmp_pe, lay).rearrange("o v (j a) d -> (o v j) (a d)", a=2))
                    ld(b, s[0:16, 256:256 + DFF], lay1(state_conv, lay).rearrange("o b w c -> (o b w) c"))
                elif b == "cmp":
                    v = s.rearrange("p (s c) -> p s c", s=NSEQ)
                    pool = cache_cmp.rearrange("l n (p a) v g d -> (l n) p (a v g d)", a=2)
                    for q in range(NSEQ):
                        for k in range(NPAGE):
                            row = page(q * NPAGE + k, lay)
                            ld(b, v[64 * k:64 * k + 64, q, :],
                               pool[bass.DynSlice(row, 1)].rearrange("o p c -> (o p) c"))
                elif b in ("kv0", "kv1"):
                    hb = int(b[2])
                    v = s.rearrange("p (w s c) -> p w s c", w=2, s=4)
                    pool = cache_slc.rearrange("l n (p a) v g d -> (l n) p (a v g d)", a=2)
                    win = cache_win.rearrange("l b (p a) v g d -> (l b) p (a v g d)", a=2)
                    for q in range(4):
                        for k in range(NPAGE):
                            row = page((4 * hb + q) * NPAGE + k, lay)
                            ld(b, v[64 * k:64 * k + 64, 0, q, :],
                               pool[bass.DynSlice(row, 1)].rearrange("o p c -> (o p) c"))
                        ld(b, v[:, 1, q, :],
                           win[bass.DynSlice(lay * NSEQ + 4 * hb + q, 1)].rearrange("o p c -> (o p) c"))
                elif b in ("st0", "st1"):
                    v = s[:, 0:4 * NSEQ * P // 2].rearrange("p (h b v) -> p h b v", h=2, b=NSEQ)
                    for h in range(2):
                        ld(b, v[:, h], lay1(state_hgrn, lay)[:, :, 2 * int(b[2]) + h].rearrange(
                            "o b p v -> p (o b) v"))
                elif b == "w_cmp":
                    for v in range(2):
                        ld(b, s[:, 1024 * v:1024 * (v + 1)].rearrange("p (j e) -> p j e", e=ND),
                           lay1(cmp_w1, lay)[:, v].rearrange("o (j a) d e -> (a d) (o j) e", a=2))
                        ld(b, s[64 * v:64 * v + 64, 2048:2048 + ND],
                           lay1(cmp_w2, lay)[:, v].rearrange("o e f -> (o e) f"))
                elif b in ("br0", "br1"):
                    c = 512 * int(b[2])
                    va, vb = (s[:, 2048 * n:2048 * (n + 1)].rearrange("p (k c) -> p k c", k=4) for n in range(2))
                    wb = lay1(w_branch, lay)[:, :, :, c:c + 512]
                    ld(b, va, wb[:, 0].rearrange("o (k p) c -> p (o k) c", p=P))
                    for g in range(KVH):
                        ld(b, vb[64 * g:64 * g + 64], wb[:, 1, 256 * g:256 * g + 256].rearrange(
                            "o (k p) c -> p (o k) c", p=ND))
                elif b.startswith("mg") or b.startswith("ff"):
                    n = int(b[2:])
                    v = s.rearrange("p (k c) -> p k c", k=KD)
                    w, a0, a1 = ((w_in, C_MG, C_MG + D) if b[0] == "m" else (w_gate_up, 0, DFF))
                    for h, a in enumerate((a0, a1)):
                        ld(b, v[:, :, 256 * h:256 * h + 256], lay1(w, lay)[:, :, a + 256 * n:a + 256 * n + 256]
                           .rearrange("o (k p) c -> p (o k) c", p=P))
                elif b.startswith("dn"):
                    mh, n = int(b[2]), int(b[4:])
                    k0, kn = sum(DOWN[mh][:n]), DOWN[mh][n]
                    ld(b, kt_of(b, kn, 512), lay1(w_down, lay)[:, k0 * P:(k0 + kn) * P, 512 * mh:512 * mh + 512]
                       .rearrange("o (k p) c -> p (o k) c", p=P))
                else:
                    w, c, n = {"w_kvc": (w_in, C_KC, 256), "w_kvn": (w_in, C_KS, 512), "w_nq": (w_in, C_NQ, 512),
                               "w_hf": (w_in, C_HF, 512), "w_hq": (w_in, C_HQ, 512), "w_hi": (w_in, C_HI, 512),
                               "w_hg": (w_in, C_HG, 512), "wo0": (w_out, 0, 512), "wo1": (w_out, 512, 512)}[b]
                    tot = 280 if b == "w_kvc" else n
                    v = kt_of(b, KD, tot)
                    ld(b, v[:, :, 0:n], lay1(w, lay)[:, :, c:c + n].rearrange("o (k p) c -> p (o k) c", p=P))
                    if b == "w_kvc":
                        ld(b, v[:, :, 256:280], lay1(w, lay)[:, :, C_GT:C_GT + 24].rearrange(
                            "o (k p) c -> p (o k) c", p=P))

            def store(out, in_, s=stored):
                sp.dma_start(out, in_).then_inc(s, 16)

            def flat3(x, lay):
                return lay1(x, lay).rearrange("o b s v g d -> (o b s) (v g d)")

            def stores_before(b, lay):
                if b == "w_nq":
                    for q in range(NSEQ):
                        sp.dma_start(lay1(win_s, lay)[:, q, 0:PAST - STEPS].rearrange(
                            "o (a t) v g d -> (o a) (t v g d)", a=8),
                            lay1(cache_win, lay)[:, q, STEPS:PAST].rearrange(
                                "o (a t) v g d -> (o a) (t v g d)", a=8)).then_inc(copied, 16)
                if b == "w_hi":
                    sp.wait_ge(mm_act, 3)
                    store(lay1(cmp_p, lay).rearrange("o b (p a) v g d -> (o b p) a (v g d)", a=2), ctok[:, 0:2, :], kv_stored)
                    store(flat3(cmp_s, lay), ctok[0:SMP, 2, :], kv_stored)
                    sp.wait_ge(k_roped, 3)
                    for w, (op, os) in enumerate(((slc_p, slc_s), (win_p, None))):
                        store(lay1(op, lay).rearrange("o b (i p) v g d -> (o b p) i (v g d)", p=P),
                              stok[:, 0:2, 256 * w:256 * w + 256], kv_stored)
                        if os is not None:
                            store(flat3(os, lay), stok[0:SMP, 2, 256 * w:256 * w + 256], kv_stored)
                    store(lay1(win_s, lay)[:, :, PAST - STEPS:PAST].rearrange("o b s v g d -> (o b) s (v g d)"),
                          stok[0:SMP, 2, 256:512], kv_stored)
                if b == BLOCKS[-1]:
                    sp.wait_ge(cvo_ready, 6)
                    store(lay1(cv_p, lay).rearrange("o b w c -> (o b w) c"), cvo[0:2, :])
                    store(lay1(cv_s, lay).rearrange("o b w c -> (o b w) c"), cvo[2:18, :])
                if b == "st0":
                    sp.wait_ge(s_ready, 4)
                    store(lay1(hg_p, lay).rearrange("o b h p v -> p (o b h) v"), sP[:, 3])
                if b in ("st0", "st1"):
                    n = int(b[2])
                    v = slot(b)[:, 0:2048].rearrange("p (h b v) -> p h b v", h=2, b=NSEQ)
                    for h in range(2):
                        sp.wait_ge(sn_ready, 2 * n + h + 1)
                        store(lay1(hg_s, lay)[:, :, 2 * n + h].rearrange("o b p v -> p (o b) v"), v[:, h],
                              state_stored[n])
                    sp.wait_ge(state_stored[n], 32)

            sp.dma_start(cst_all[:, :], consts).then_inc(consts_in, 16)
            sp.dma_start(pages[0:1, :], page_table.rearrange("b n -> (b n)").unsqueeze(0)).then_inc(consts_in, 16)
            sp.dma_start(xin[:, 0:2, :], x_prompt.rearrange("b (i p) c -> p (b i) c", p=P)).then_inc(xin_in, 16)
            sp.dma_start(xin[0:SMP, 2, :], x_sample.rearrange("b s c -> (b s) c")).then_inc(xin_in, 16)
            sp.dma_start(attb[0:8, 0:P], hg_lower.rearrange("l (h p) -> (l h) p", p=P)).then_inc(xin_in, 16)
            sp.dma_start(attb[8:16, 0:P], norm_final.rearrange("(k p) -> k p", p=P)).then_inc(xin_in, 16)
            sp.wait_ge(consts_in, 32)
            for b in BLOCKS[:NSLOT]:
                load(b, 0)

            def clear(l):
                sp.wait_ge(arrived, 4 * (l + 1))
                sp.sem_inc(spare, 1)
                sp.sem_clear(range(nums[0], nums[-1] + 1))
                sp.sem_inc(cleared, 1)

            def layer(lay, last):
                for n, b in enumerate(BLOCKS):
                    stores_before(b, lay)
                    if n + NSLOT < NBLK or not last:
                        if b == "cmp":
                            sp.wait_ge(rows_ready, NSEQ)
                        elif b in LAST_USE:
                            R = MM if LAST_USE[b] in MM.no else AXR
                            sp.wait_ge(*R.filled(LAST_USE[b]))
                        elif b.startswith("dn"):
                            sp.wait_ge(*unit_read(max(u for u in down_units if SPLIT[u][0] == b)))
                        load(BLOCKS[(n + NSLOT) % NBLK], lay + (n + NSLOT) // NBLK)
                sp.wait_ge(stored, 16 * NSTORE)
                clear(lay + 1)

            NSTORE = 1 + 2
            clear(0)
            with sp.Fori(0, DEPTH - 1) as lay:
                layer(lay, False)
            layer(DEPTH - 1, True)
            sp.wait_ge(y_ready, 1)
            store(y_p.rearrange("b (i p) c -> p (b i) c", p=P), yout[:, 0:2, :])
            store(y_s.rearrange("b s c -> (b s) c"), yout[0:SMP, 2, :])
            sp.wait_ge(stored, 32)
            sp.wait_ge(copied, 16 * DEPTH * NSEQ)

        @block.tensor
        def _(pe):
            def begin(R, name):
                w = R.vacant(name)
                if w:
                    pe.wait_ge(*w)
                return R.bank(name)

            def mm(out, lhsT, rhs, start, stop):
                return nc.tensor.matmul(out, lhsT, rhs, start=start, stop=stop)

            def tr(out, in_):
                return nc.tensor.transpose(out, in_, ident[0:in_.shape[0], 0:in_.shape[0]])

            pe.wait_ge(consts_in, 32)
            pe.wait_ge(xin_in, 64)
            for k in range(KD + 1):
                if k >= 4:
                    pe.wait_ge(x_ready, k - 3)
                if k < KD:
                    for i in range(3):
                        last = tr(axb[k % 4][:, P * i:P * i + TM[i]], xin[0:TM[i], i, P * k:P * k + P])
                else:
                    last = tr(axb[k % 4][:, 0:16], attb[0:16, 0:P])
                last.then_inc(ax_full, 1)
            pe.wait_ge(x_ready, KD + 1)
            depart(pe, 0)

            def norm(name, l_sq):
                bank = begin(AXR, name)
                for k in range(KD):
                    if k == 0:
                        pe.wait_ge(squares_dve, l_sq)
                    if k == 4:
                        pe.wait_ge(squares_act, l_sq)
                    last = mm(bank[:, 0:T], ones, sq[:, k, :], k == 0, k == KD - 1)
                last.then_inc(ax_full, 1)

            def feature_tile(name, w, cols, need_h=None):
                bank = begin(MM, name)
                for k in range(KD):
                    if need_h is not None:
                        pe.wait_ge(h_ready, need_h + k + 1)
                    last = mm(bank[:, 0:T], cols(w, k), hT[:, k, :], k == 0, k == KD - 1)
                last.then_inc(mm_full, 1)

            def split_products(out, high, low, x_high, x_low, start, stop):
                mm(out, high, x_high, start, False)
                mm(out, high, x_low, False, False)
                return mm(out, low, x_high, False, stop)

            def split_tile(name, u, h, need_h):
                bank = begin(MM, name)
                for k in range(KD):
                    if need_h:
                        pe.wait_ge(h_lo, k + 1)
                    last = split_products(bank[:, 0:T], unit_high(u)[:, k, h, :], unit_of(u, ring_r)[:, k, h, :],
                                          h_high[:, k, :], h_low[:, k, :], k == 0, k == KD - 1)
                last.then_inc(mm_full, 1)

            def plain(w, c0):
                return lambda v, k: v[:, k, c0:c0 + P]

            def hgrn_values(i, l):
                if i == 0:
                    pe.wait_ge(*landed_at("w_hi", l))
                w = kt_of("w_hi", KD, 512)
                bank = begin(MM, f"hi{i}")
                for k in range(KD):
                    last = mm(bank[0:TM[i], :], hT[:, k, P * i:P * i + TM[i]], w[:, k, :], k == 0, k == KD - 1)
                last.then_inc(mm_full, 1)

            def out_gate(h, l):
                if h == 0:
                    pe.wait_ge(*landed_at("w_hg", l))
                w = kt_of("w_hg", KD, 512)
                feature_tile(f"hg{h}", w, plain(w, P * h))

            def merge_gates(m, l):
                mg = f"mg{m // 2}"
                if m % 2 == 0:
                    pe.wait_ge(*landed_at(mg, l))
                w = kt_of(mg, KD, 512)
                feature_tile(f"mga{m}", w, plain(w, P * (m % 2)))
                feature_tile(f"mgb{m}", w, plain(w, 256 + P * (m % 2)))

            def level(kk):
                m = LEVELS[kk]
                pe.wait_ge(ql_ready, kk + 1)
                pe.wait_ge(kl_ready, kk + 1)
                qs, ks = (qH, kH) if m == 0 else (qL, kL)
                if m == 1:
                    ks = kH
                bank = begin(AXR, f"lv{kk}")
                for h in range(HH):
                    for c in range(4):
                        at = (c // 2) * 256 + h * S1
                        last = mm(bank[64 * (c % 2):64 * (c % 2) + 64, at:at + S1], ks[:, h, S1 * c:S1 * c + S1],
                                  qs[:, h, S1 * c:S1 * c + S1], True, True)
                last.then_inc(ax_full, 1)
                if m < STEPS:
                    bank = begin(AXR, f"lvs{kk}")
                    for h in range(HH):
                        last = mm(bank[0:64, h * S1:h * S1 + S1], ks[:, h, SEQ:T], qs[:, h, SEQ:T], True, True)
                    last.then_inc(ax_full, 1)

            def scores(n):
                i, g = UNITS[n]
                gs = slice(64 * g, 64 * g + 64)
                nk = P * (i + 1)
                for r in range(GRP):
                    bank = begin(AXR, f"sc{n}_{r}")
                    for w in range(2):
                        last = mm(bank[:, 256 * w:256 * w + nk], qT[gs, r, P * i:P * i + P], ktn[gs, w, 0:nk], True,
                                  True)
                    last.then_inc(ax_full, 1)
                bank = begin(AXR, f"scc{n}")
                for r in range(GRP):
                    last = mm(bank[:, NCB * r:NCB * r + NCB], qT[gs, r, P * i:P * i + P], kcT[gs, NSEQ, :], True, True)
                last.then_inc(ax_full, 1)

            def values(n):
                i, g = UNITS[n]
                pe.wait_ge(scaled, n + 1)
                for x in range(2 * (i + 1)):
                    w, kt = x % 2, x // 2
                    bank = begin(AXR, f"tp{n}_{x}")
                    for r in range(GRP):
                        last = tr(bank[:, P * r:P * r + P], prob[:, r, w, P * kt:P * kt + P])
                    last.then_inc(ax_full, 1)
                bank = begin(AXR, f"tpc{n}")
                for r in range(GRP):
                    last = tr(bank[0:NCB, P * r:P * r + P], pcs[:, NCB * r:NCB * r + NCB])
                last.then_inc(ax_full, 1)
                bank = begin(AXR, f"ov{n}")
                out = bank[64 * g:64 * g + 64, :]
                pe.wait_ge(*AXR.emptied_at(f"tpc{n}"))
                pe.wait_ge(*AXR.emptied_at(f"tp{n}_{2 * i + 1}"))
                mm(out, vc[0:NCB, NSEQ, g, :], probTc[0:NCB, :], True, False)
                for x in range(2 * (i + 1)):
                    w, kt = x % 2, x // 2
                    last = mm(out, stok[:, kt, 256 * w + P + 64 * g:256 * w + P + 64 * g + 64], probT[:, x, :], False,
                              x == 2 * i + 1)
                last.then_inc(ax_full, 1)

            def sample_scores(n, hb, g):
                gs = slice(64 * g, 64 * g + 64)
                bank = begin(AXR, f"ssa{n}")
                for w in range(2):
                    for b in range(4):
                        last = mm(bank[32 * b:32 * b + 32, 256 * w:256 * w + 256],
                                  qS[gs, 4 * hb + b].rearrange("p r s -> p (r s)"), kvT[gs, w, b, :], True, True)
                last.then_inc(ax_full, 1)
                bank = begin(AXR, f"ssb{n}")
                q4 = qS[gs, 4 * hb:4 * hb + 4].rearrange("p b r s -> p (b r s)")
                for w in range(2):
                    mm(bank[:, SMP * w:SMP * w + SMP], q4, ktn[gs, w, SEQ:T], True, True)
                for b in range(4):
                    last = mm(bank[32 * b:32 * b + 32, P:P + NCB], qS[gs, 4 * hb + b].rearrange("p r s -> p (r s)"),
                              kcT[gs, 4 * hb + b, :], True, True)
                last.then_inc(ax_full, 1)

            def sample_values(n, hb, g):
                pe.wait_ge(scaled, n + 1)
                bank = begin(AXR, f"tps{n}")
                for x in range(4):
                    w, kt = x // 2, x % 2
                    last = tr(bank[:, P * x:P * x + P], sprob[:, w, P * kt:P * kt + P])
                last.then_inc(ax_full, 1)
                bank = begin(AXR, f"tpn{n}")
                for w in range(2):
                    tr(bank[0:SMP, P * w:P * w + P], snew[:, w, :])
                tr(bank[0:NCB, 2 * P:3 * P], pcs[:, 0:NCB]).then_inc(ax_full, 1)
                bank = begin(AXR, f"ov{n}")
                pe.wait_ge(*AXR.emptied_at(f"tps{n}"))
                pe.wait_ge(*AXR.emptied_at(f"tpn{n}"))
                kv = slot(f"kv{hb}").rearrange("p (w s a v g d) -> p w s a v g d", w=2, s=4, a=2, v=2, g=2)
                for b in range(4):
                    out = bank[64 * g:64 * g + 64, 32 * b:32 * b + 32]
                    cs = slice(32 * b, 32 * b + 32)
                    mm(out, vc[0:NCB, 4 * hb + b, g, :], snewT[0:NCB, 2, cs], True, False)
                    for w in range(2):
                        mm(out, stok[0:SMP, 2, 256 * w + P + 64 * g:256 * w + P + 64 * g + 64], snewT[0:SMP, w, cs],
                           False, False)
                    for x in range(4):
                        last = mm(out, kv[:, x // 2, b, x % 2, 1, g, :], sprobT[:, x, cs], False, x == 3)
                last.then_inc(ax_full, 1)

            def layer(l):
                pe.wait_ge(*landed_at("par", l))
                s = slot("par")
                bank = begin(AXR, "par")
                tr(bank[:, 0:105], s[0:105, 0:P])
                tr(bank[:, P:P + 32], s[0:32, P:2 * P]).then_inc(ax_full, 1)
                bank = begin(AXR, "cst")
                for j in range(NJ):
                    last = tr(bank[:, 16 * j:16 * j + 16], s[0:16, 256 + P * j:256 + P * j + P])
                last.then_inc(ax_full, 1)
                norm("norm1", 1)
                for q in range(NSEQ):
                    bank = begin(AXR, f"cc{q}")
                    pe.wait_ge(rows_ready, q + 1)
                    for x in range(4):
                        last = tr(bank[:, P * x:P * x + P], craw[:, q, P * x:P * x + P])
                    last.then_inc(ax_full, 1)
                pe.wait_ge(*landed_at("w_kvc", l))
                w = kt_of("w_kvc", KD, 280)
                for i in range(3):
                    bank = begin(MM, f"kvc{i}")
                    for k in range(KD):
                        if i == 0:
                            pe.wait_ge(h_ready, k + 1)
                        lhs = hT[:, k, i:SEQ:2] if i < 2 else hT[:, k, SEQ:T]
                        mm(bank[0:TM[i], 0:256], lhs, w[:, k, 0:256], k == 0, k == KD - 1)
                    for k in range(KD):
                        last = mm(bank[0:TM[i], 256:280], hT[:, k, P * i:P * i + TM[i]], w[:, k, 256:280], k == 0,
                                  k == KD - 1)
                    last.then_inc(mm_full, 1)
                pe.wait_ge(*landed_at("w_kvn", l))
                w = kt_of("w_kvn", KD, 512)
                for i in range(3):
                    bank = begin(MM, f"kvn{i}")
                    for k in range(KD):
                        last = mm(bank[0:TM[i], :], hT[:, k, P * i:P * i + TM[i]], w[:, k, :], k == 0, k == KD - 1)
                    last.then_inc(mm_full, 1)
                bank = begin(AXR, "cp")
                pe.wait_ge(rows_ready, NCS)
                for x in range(4):
                    last = tr(bank[:, P * x:P * x + P], craw[:, NSEQ, P * x:P * x + P])
                last.then_inc(ax_full, 1)
                pe.wait_ge(*landed_at("w_nq", l))
                w = kt_of("w_nq", KD, 512)
                for m in range(4):
                    bank = begin(MM, f"nq{m}")
                    for k in range(KD):
                        for g in range(KVH):
                            last = mm(bank[64 * g:64 * g + 64, 0:T], w[:, k, 256 * g + 64 * m:256 * g + 64 * m + 64],
                                      hT[:, k, :], k == 0, k == KD - 1)
                    last.then_inc(mm_full, 1)
                pe.wait_ge(*landed_at("w_hf", l))
                w = kt_of("w_hf", KD, 512)
                feature_tile("hf0", w, plain(w, 0))
                for x in range(2):
                    bank = begin(AXR, f"kt{x}")
                    if x == 0:
                        pe.wait_ge(k_roped, 3)
                    for i in range(3):
                        last = tr(bank[:, P * i:P * i + TM[i]], stok[0:TM[i], i, 256 * x:256 * x + P])
                    last.then_inc(ax_full, 1)
                for h in range(1, HH):
                    feature_tile(f"hf{h}", w, plain(w, P * h))
                for m in range(4):
                    bank = begin(AXR, f"nqr{m}")
                    pe.wait_ge(qraw_ready, m + 1)
                    mm(bank[:, 0:T], con("perm"), qraw[:, m, :], True, True).then_inc(ax_full, 1)
                pe.wait_ge(*landed_at("w_hq", l))
                w = kt_of("w_hq", KD, 512)
                for h in range(HH):
                    feature_tile(f"hq{h}", w, plain(w, P * h))
                pe.wait_ge(*landed_at("w_cmp", l))
                w1 = slot("w_cmp")[:, 0:2048].rearrange("p (v j e) -> p v j e", v=2, e=ND)
                banks = [begin(AXR, "hidk"), begin(AXR, "hidv")]
                pe.wait_ge(prm_ready, 1)
                pe.wait_ge(*AXR.emptied_at(f"cc{NSEQ - 1}"))
                pe.wait_ge(*AXR.emptied_at("cp"))
                for j in range(16):
                    for v in range(2):
                        mm(banks[v][64 * v:64 * v + 64, 300:301], w1[:, v, j, :], prm[:, P + 16 * v + j:P + 16 * v + j + 1],
                           j == 0, j == 15)
                for j in range(16):
                    for v in range(2):
                        rows = cmpT[:, v].rearrange("p g s t -> p (g s) t")[:, :, j:j + 8 * NCB - 7:8]
                        last = mm(banks[v][64 * v:64 * v + 64, 0:2 * NCS * NCB], w1[:, v, j, :], rows, j == 0, j == 15)
                        if j == 15:
                            last.then_inc(ax_full, 1)
                hgrn_values(0, l)
                bank = begin(AXR, "kcm")
                pe.wait_ge(hid_ready, 2)
                w2 = slot("w_cmp")
                for g in range(KVH):
                    last = mm(bank[64 * g:64 * g + 64, 0:NCS * NCB], w2[0:64, 2048:2048 + ND],
                              hid[0:64, g].rearrange("p s n -> p (s n)"), True, True)
                last.then_inc(ax_full, 1)
                bank = begin(AXR, "kcr")
                pe.wait_ge(kraw_ready, 1)
                mm(bank[:, 0:NCS * NCB], con("perm"), kraw.rearrange("p s n -> p (s n)"), True, True).then_inc(
                    ax_full, 1)
                for n in range(3):
                    bank = begin(AXR, f"vc{n}")
                    for y in range(6):
                        q, g = (6 * n + y) // 2, (6 * n + y) % 2
                        last = mm(bank[0:NCB, ND * y:ND * y + ND], hid[64:128, g, q, :], w2[64:128, 2048:2048 + ND], True,
                                  True)
                    last.then_inc(ax_full, 1)
                for n in range(4):
                    level(2 * n)
                    if n == 0:
                        pe.wait_ge(q_ready, 4)
                        pe.wait_ge(*AXR.emptied_at("kt1"))
                        pe.wait_ge(*AXR.emptied_at("vc2"))
                        pe.wait_ge(kc_ready, 1)
                    scores(n)
                    if n == 0:
                        hgrn_values(1, l)
                    else:
                        out_gate(n, l)
                    if 2 * n + 1 < len(LEVELS):
                        level(2 * n + 1)
                    values(n)
                    if n == 0:
                        hgrn_values(2, l)
                        out_gate(0, l)
                for hb in range(2):
                    bank = begin(AXR, f"gsel{hb}")
                    mm(bank[:, 0:24], con("sel", SMP)[:, P * hb:P * hb + P], gts[0:SMP, 2, :], True, True).then_inc(
                        ax_full, 1)
                pe.wait_ge(kl_ready, len(LEVELS) + 1)
                for h in range(HH):
                    bank = begin(AXR, f"krt{h}")
                    for i in range(3):
                        last = tr(bank[0:TM[i], P * i:P * i + P], kL[:, h, P * i:P * i + TM[i]])
                    last.then_inc(ax_full, 1)
                pe.wait_ge(qs_ready, 1)
                for hb in range(2):
                    pe.wait_ge(*landed_at(f"kv{hb}", l))
                    kv = slot(f"kv{hb}").rearrange("p (w s a c) -> p w s a c", w=2, s=4, a=2)
                    for x in range(4):
                        w, bp = x // 2, x % 2
                        bank = begin(AXR, f"skt{hb}_{x}")
                        for y in range(4):
                            last = tr(bank[:, P * y:P * y + P], kv[:, w, 2 * bp + y // 2, y % 2, 0:P])
                        last.then_inc(ax_full, 1)
                    for c in (2 * hb, 2 * hb + 1):
                        bank = begin(AXR, f"ds{c}")
                        if c == 0:
                            pe.wait_ge(*AXR.emptied_at("krt3"))
                            pe.wait_ge(*AXR.emptied_at("krt2"))
                        rows = slice(64 * (c % 2), 64 * (c % 2) + 64)
                        for h in range(HH):
                            last = mm(bank[:, P * h:P * h + P], krP[rows, h, c // 2, :], vH[rows, c // 2, P * h:P * h + P],
                                      True, True)
                        last.then_inc(ax_full, 1)
                    pe.wait_ge(*AXR.emptied_at(f"skt{hb}_3"))
                    pe.wait_ge(*AXR.emptied_at(f"skt{hb}_2"))
                    for g in range(KVH):
                        sample_scores(4 + 2 * hb + g, hb, g)
                        merge_gates(2 * hb + g, l)
                        sample_values(4 + 2 * hb + g, hb, g)
                pe.wait_ge(s_ready, 3)
                pe.wait_ge(ql_ready, len(LEVELS) + 1)
                for h in range(HH):
                    if h % 2 == 0:
                        pe.wait_ge(*landed_at(f"st{h // 2}", l))
                    s0 = slot(f"st{h // 2}")[:, 0:2048].rearrange("p (h b v) -> p h b v", h=2, b=NSEQ)
                    for c in (0, 2, 4, 1, 3):
                        if c < 2:
                            bank = begin(AXR, ("o", "oo")[c] + str(h))
                        rows = slice(64 * (c % 2), 64 * (c % 2) + 64)
                        cols = slice(S1 * c, S1 * c + S1)
                        last = mm(bank[:, cols], vH[rows, c // 2, P * h:P * h + P], acc[rows, c // 2, h, :], True, c == 0)
                        if 1 <= c <= 3:
                            last = mm(bank[:, cols], sP[:, c - 1, h, :], qL[:, h, cols], False, True)
                        for b in range(NSEQ if c == 4 else 0):
                            cols = slice(SEQ + STEPS * b, SEQ + STEPS * (b + 1))
                            last = mm(bank[:, cols], s0[:, h % 2, b, :], qL[:, h, cols], False, b == NSEQ - 1)
                        if c >= 3:
                            last.then_inc(ax_full, 1)
                    pe.wait_ge(vx_ready, h + 1)
                    for y, name in enumerate((f"dsa{h}", f"dsb{h}")):
                        bank = begin(AXR, name)
                        mm(bank[:, :], krS[0:SMP, h, :], vX[0:SMP, 4 * y:4 * y + 4, :].rearrange("p b v -> p (b v)"),
                           True, True).then_inc(ax_full, 1)
                merge_gates(4, l)
                for h in range(HH):
                    bank = begin(AXR, f"on{h}")
                    pe.wait_ge(sqo_ready, h + 1)
                    mm(bank[:, 0:T], ones, sqH[:, h, :], True, True).then_inc(ax_full, 1)
                merge_gates(5, l)
                for m in range(KD):
                    br = f"br{m // 4}"
                    if m % 4 == 0:
                        pe.wait_ge(*landed_at(br, l))
                    if m == 0:
                        pe.wait_ge(oh_ready, 4)
                        pe.wait_ge(*AXR.emptied_at("ov7"))
                    for y, (name, src) in enumerate(((f"bra{m}", oH), (f"brb{m}", oN))):
                        w = slot(br)[:, 2048 * y:2048 * (y + 1)].rearrange("p (k c) -> p k c", k=4)
                        bank = begin(AXR, name)
                        for k in range(4):
                            last = mm(bank[:, 0:T], w[:, k, P * (m % 4):P * (m % 4) + P], src[:, k, :], k == 0, k == 3)
                        last.then_inc(ax_full, 1)
                    if m in (3, 4):
                        merge_gates(m + 3, l)
                for m in range(KD):
                    if m % 4 == 0:
                        pe.wait_ge(*landed_at(f"wo{m // 4}", l))
                    w = kt_of(f"wo{m // 4}", KD, 512)
                    bank = begin(MM, f"wo{m}")
                    for k in range(KD):
                        if m == 0:
                            pe.wait_ge(merged_ready, k + 1)
                        last = mm(bank[:, 0:T], w[:, k, P * (m % 4):P * (m % 4) + P], merged[:, k, :], k == 0, k == KD - 1)
                    last.then_inc(mm_full, 1)
                norm("norm2", 2)
                for j in range(NJ):
                    pe.wait_ge(w_low, j + 1)
                    split_tile(f"g{j}", j, 0, j == 0)
                    split_tile(f"u{j}", j, 1, False)
                for u in down_units:
                    b, a, kn = SPLIT[u]
                    mh, n = int(b[2]), int(b[4:])
                    R = (MM, AXR)[mh]
                    if u == NJ + 2:
                        pe.wait_ge(glast_ready, 1)
                        for c in range(6):
                            bank = begin(AXR, f"cv{c}")
                            for y in range(4 if c < 5 else 2):
                                last = tr(bank[0:18, P * y:P * y + P], glast[:, 4 * c + y, :])
                            last.then_inc(ax_full, 1)
                    pe.wait_ge(w_low, u + 1)
                    for kk in range(kn):
                        k = sum(DOWN[mh][:n]) + a + kk
                        for m in range(4):
                            bank = begin(R, f"dn{mh}_{m}") if k == 0 else R.bank(f"dn{mh}_{m}")
                            if mh == 0 and m == 0:
                                pe.wait_ge(act_ready, k + 1)
                            last = split_products(bank[:, 0:T], unit_high(u)[:, kk, m, :], unit_of(u, ring_r)[:, kk, m, :],
                                                  act_high[:, k, :], act_low[:, k, :], k == 0, k == NJ - 1)
                            if k == NJ - 1:
                                last.then_inc(R.full, 1)
                    if u in down_inner:
                        last.then_inc(down_read, 1)
                pe.wait_ge(x_ready, 2 * KD)

            with pe.Fori(0, DEPTH) as l:
                layer(l)
                depart(pe, l + 1)
            for k in range(KD):
                if k == 0:
                    pe.wait_ge(squares_dve, 1)
                if k == 4:
                    pe.wait_ge(squares_act, 1)
                last = mm(axb[0][:, 0:T], ones, sq[:, k, :], k == 0, k == KD - 1)
            last.then_inc(ax_full, 1)
            n = 0
            for k0 in range(0, KD, 4):
                for i in range(3):
                    if n >= 4:
                        pe.wait_ge(mm_dve, n - 3)
                    for k in range(k0, k0 + 4):
                        if i == 0:
                            pe.wait_ge(h_ready, k + 1)
                        last = tr(mmb[n % 4][0:TM[i], P * (k - k0):P * (k - k0) + P], hT[:, k, P * i:P * i + TM[i]])
                    last.then_inc(mm_full, 1)
                    n += 1

        @block.scalar
        def _(sc):
            def A(out, in_, f, **kw):
                return nc.scalar.activation(out, in_, f, **kw)

            sc.wait_ge(mul_ready, 1)
            A(lbs[:, 12:20], lbs[:, 12:20], ACT.Exp).then_inc(exp_ready, 1)
            sc.wait_ge(exp_ready, 1)
            depart(sc, 0)

            def norm(st, src_wait, n, bank):
                if src_wait:
                    sc.wait_ge(*src_wait)
                A(sq[:, 4:8, :], xT[:, 4:8, :], ACT.Square).then_inc(*st.up(squares_act))
                sc.wait_ge(*bank[1])
                A(rs[:, 0:T], bank[0][:, 0:T], ACT.Ln, bias=epsb[:, 0:1], scale=1.0 / D).then_inc(*st.up(ax_act))
                sc.wait_ge(*st.settled())
                A(rs[:, 0:T], rs[:, 0:T], ACT.Exp, scale=-0.5).then_inc(*st.up(rs_ready))

            def layer(l):
                st = Steps(sc)
                AB, MB = AXR.bank, MM.bank

                def take(R, name):
                    sc.wait_ge(*R.filled(name))
                    return R.bank(name)

                norm(st, None, 1, (AB("norm1"), AXR.filled("norm1")))
                for q in range(0, NSEQ, 2):
                    bank = take(AXR, f"cc{q}")
                    A(cmpT[:, :, :, q, :].rearrange("p v g t -> p (v g) t"), bank[:, :].rearrange("p (x t) -> p x t", x=4),
                      ACT.Copy).then_inc(*st.up(ax_act))
                for i in range(3):
                    bank = take(MM, f"kvc{i}")
                    A(gts[0:TM[i], i, :], bank[0:TM[i], 256:280], ACT.Sigmoid)
                    A(ctok[0:TM[i], i, :], bank[0:TM[i], 0:256], ACT.Copy).then_inc(*st.up(mm_act))
                for i in range(3):
                    bank = take(MM, f"kvn{i}")
                    A(stok[0:TM[i], i, :], bank[0:TM[i], :], ACT.Copy).then_inc(*st.up(mm_act))
                bank = take(AXR, "cp")
                A(cmpT[:, :, :, NSEQ, :].rearrange("p v g t -> p (v g) t"), bank[:, :].rearrange("p (x t) -> p x t", x=4),
                  ACT.Copy).then_inc(*st.up(ax_act))
                for m in range(4):
                    bank = take(MM, f"nq{m}")
                    A(qraw[:, m, :], bank[:, 0:T], ACT.Copy).then_inc(*st.up(qraw_ready))
                    sc.wait_ge(*st.settled())
                    sc.sem_inc(*st.up(mm_act))
                for h in range(HH):
                    bank = take(MM, f"hf{h}")
                    A(pH[:, h, :], bank[:, 0:T], ACT.Sigmoid).then_inc(*st.up(sig_ready))
                    A(kH[:, h, :], bank[:, 0:T], ACT.Sigmoid, scale=-1.0).then_inc(*st.up(mm_act))
                    if h == 0:
                        bank = take(AXR, "kt0")
                        A(ktn[:, 0, :], bank[:, 0:T], ACT.Copy).then_inc(*st.up(ax_act))
                for h in range(HH):
                    bank = take(MM, f"hq{h}")
                    A(sgq[:, h, :], bank[:, 0:T], ACT.Sigmoid).then_inc(*st.up(sig_ready))
                take(AXR, "hidk")
                bank = take(AXR, "hidv")
                for v, name in enumerate(("hidk", "hidv")):
                    rows = slice(64 * v, 64 * v + 64)
                    A(hbias[rows, 0:1], AB(name)[rows, 300:301], ACT.Copy).then_inc(*st.up(act_step))
                sc.wait_ge(*st.settled())
                for v, name in enumerate(("hidk", "hidv")):
                    rows = slice(64 * v, 64 * v + 64)
                    A(hid[rows].rearrange("p g s n -> p (g s n)"), AB(name)[rows, 0:2 * NCS * NCB],
                      ACT.Gelu_apprx_tanh, bias=hbias[rows, 0:1]).then_inc(*st.up(hid_ready))
                sc.wait_ge(*st.settled())
                sc.sem_inc(ax_act, 2)
                st.count[ax_act.name] += 2
                def hgrn_values(i):
                    bank = take(MM, f"hi{i}")
                    A(vH[0:TM[i], i, :], bank[0:TM[i], :], ACT.Copy).then_inc(*st.up(mm_act))

                def out_gate(h):
                    bank = take(MM, f"hg{h}")
                    A(gH[:, h, :], bank[:, 0:T], ACT.Sigmoid).then_inc(*st.up(sig_ready))

                def merge_gates(m):
                    for dst, name in ((merged[:, m, :], f"mga{m}"), (mgs[:, m % MGB, :], f"mgb{m}")):
                        bank = take(MM, name)
                        if m >= MGB and name[2] == "b":
                            sc.wait_ge(merged_ready, m - MGB + 1)
                        A(dst, bank[:, 0:T], ACT.Sigmoid).then_inc(*st.up(mm_act))

                hgrn_values(0)
                bank = take(AXR, "kcm")
                A(kraw.rearrange("p s n -> p (s n)"), bank[:, 0:NCS * NCB], ACT.Copy).then_inc(*st.up(kraw_ready))
                sc.wait_ge(*st.settled())
                sc.sem_inc(*st.up(ax_act))
                for n in range(3):
                    bank = take(AXR, f"vc{n}")
                    A(vc[0:NCB, 3 * n:3 * n + 3].rearrange("p s g d -> p (s g d)"), bank[0:NCB, 0:6 * ND],
                      ACT.Copy).then_inc(*st.up(ax_act))
                for n, (i, g) in enumerate(UNITS):
                    nk = P * (i + 1)
                    sc.wait_ge(max_ready, n + 1)
                    A(pcs[:, 0:60], pcs[:, 0:60], ACT.Exp, scale=SCALE)
                    for r in range(GRP):
                        for w in range(2):
                            c = 4 * (w + 1) + r
                            last = A(prob[:, r, w, 0:nk], prob[:, r, w, 0:nk], ACT.Exp, bias=nm[:, c:c + 1],
                                     scale=SCALE, accum_out=sm[:, c:c + 1])
                    last.then_inc(*st.up(exp_ready))
                    if n == 0:
                        hgrn_values(1)
                    else:
                        out_gate(n)
                    for x in range(0, 2 * (i + 1), 2):
                        bank = take(AXR, f"tp{n}_{x}")
                        A(probT[:, x, :], bank[:, :], ACT.Copy).then_inc(*st.up(ax_act))
                    bank = take(AXR, f"tpc{n}")
                    A(probTc[0:NCB, :], bank[0:NCB, :], ACT.Copy).then_inc(*st.up(ax_act))
                    if n == 0:
                        hgrn_values(2)
                        out_gate(0)
                sc.wait_ge(ql_ready, len(LEVELS) + 1)
                for h in (0, 2):
                    bank = take(AXR, f"krt{h}")
                    A(krP[:, h].rearrange("p i d -> p (i d)"), bank[:, 0:256], ACT.Copy)
                    A(krS[0:SMP, h, :], bank[0:SMP, 256:384], ACT.Copy).then_inc(*st.up(ax_act))
                for hb in range(2):
                    for x in (0, 2):
                        bank = take(AXR, f"skt{hb}_{x}")
                        A(kvT[:, x // 2, 2 * (x % 2):2 * (x % 2) + 2, :].rearrange("p b t -> p (b t)"), bank[:, :],
                          ACT.Copy).then_inc(*st.up(ax_act))
                    for g in range(KVH):
                        n = 4 + 2 * hb + g
                        sc.wait_ge(max_ready, n + 1)
                        A(pcs[:, 0:NCB], AB(f"ssb{n}")[:, P:P + NCB], ACT.Exp, bias=nm[:, 0:1], scale=SCALE,
                          accum_out=sm[:, 0:1])
                        for w in range(2):
                            A(snew[:, w, :], snew[:, w, :], ACT.Exp, bias=nm[:, w + 1:w + 2], scale=SCALE,
                              accum_out=sm[:, w + 3:w + 4])
                        for w in range(2):
                            last = A(sprob[:, w, :], AB(f"ssa{n}")[:, 256 * w:256 * w + 256], ACT.Exp,
                                     bias=nm[:, w + 1:w + 2], scale=SCALE, accum_out=sm[:, w + 1:w + 2])
                        last.then_inc(*st.up(exp_ready))
                        sc.wait_ge(*st.settled())
                        sc.sem_inc(ax_act, 2)
                        st.count[ax_act.name] += 2
                        merge_gates(2 * hb + g)
                        bank = take(AXR, f"tpn{n}")
                        A(snewT[0:SMP, 0:2, :].rearrange("p x c -> p (x c)"), bank[0:SMP, 0:256], ACT.Copy)
                        A(snewT[0:NCB, 2, :], bank[0:NCB, 256:384], ACT.Copy).then_inc(*st.up(ax_act))
                sc.wait_ge(kl_ready, len(LEVELS) + 1)
                for h in range(HH):
                    sc.wait_ge(*AXR.emptied_at(f"oo{h}"))
                    A(sqH[:, h, :], oS[:, h, :], ACT.Square).then_inc(*st.up(sqo_ready))
                merge_gates(4)
                for h in range(HH):
                    bank = take(AXR, f"on{h}")
                    A(rsH[:, h, :], bank[:, 0:T], ACT.Ln, bias=epsb[:, 0:1], scale=1.0 / HD).then_inc(*st.up(ax_act))
                sc.wait_ge(*st.settled())
                A(rsH[:, :, :], rsH[:, :, :], ACT.Exp, scale=-0.5).then_inc(*st.up(rso_ready))
                for m in range(5, KD):
                    merge_gates(m)
                def split(u):
                    if u == 0:
                        sc.wait_ge(kv_stored, 16 * 6)
                    if u == 0 or SPLIT[u][0] != SPLIT[u - 1][0]:
                        sc.wait_ge(*landed_at(SPLIT[u][0], l))
                        sc.sem_inc(spare, 1)
                    if u >= 2:
                        sc.wait_ge(*unit_read(u - 2))
                    A(unit_high(u), unit_of(u, ring), ACT.Copy).then_inc(*st.up(w_high))

                split(0)
                split(1)
                norm(st, (x_ready, KD), 2, (AB("norm2"), AXR.filled("norm2")))
                for k in range(KD):
                    sc.wait_ge(h_ready, KD + k + 1)
                    A(h_high[:, k, :], hT[:, k, :], ACT.Copy).then_inc(*st.up(h_hi))
                for j in range(NJ):
                    if j:
                        split(j + 1)
                    bank = take(MM, f"g{j}")
                    gx, cv = gext[j % 2], cvt[j % 2]
                    if j == 0:
                        sc.wait_ge(pre_ready, 1)
                    if j >= 2:
                        sc.wait_ge(conv_ready, j - 1)
                        sc.wait_ge(pre_ready, j + 1)
                        sc.wait_ge(act_ready, j - 1)
                    A(gx[:, 2:2 + SEQ], bank[:, 0:SEQ], ACT.Copy)
                    A(gx[:, 2 + SEQ:GX].rearrange("p (b s) -> p b s", b=NSEQ)[:, :, 2:2 + STEPS],
                      bank[:, SEQ:T].rearrange("p (b s) -> p b s", b=NSEQ), ACT.Copy)
                    A(cv, bank[:, 0:T], ACT.Identity, bias=prm[:, 17 + j:18 + j],
                      scale=prm[:, 39 + 2 * NJ + j:40 + 2 * NJ + j]).then_inc(*st.up(mm_act))
                    sc.wait_ge(conv_ready, j + 1)
                    A(cv, cv, ACT.Gelu_apprx_tanh).then_inc(*st.up(gelu_ready))
                for u in range(NJ + 1, len(SPLIT)):
                    split(u)
                sc.wait_ge(*st.settled())

            with sc.Fori(0, DEPTH) as l:
                layer(l)
                depart(sc, l + 1)
            norm(Steps(sc), None, 1, (axb[0], (ax_full, 1)))

        @block.vector
        def _(ve):
            V = nc.vector

            st = Steps(ve)
            V.memset(epsb[:, :], EPS)
            for k in range(KD + 1):
                ve.wait_ge(ax_full, k + 1)
                if k < KD:
                    V.tensor_copy(xT[:, k, :], axb[k % 4][:, 0:T]).then_inc(*st.up(x_ready))
                else:
                    V.tensor_copy(pro[:, :], axb[k % 4][:, 0:16]).then_inc(*st.up(x_ready))
            ve.wait_ge(*st.settled())

            def link(ins):
                ins.then_inc(*st.up(dve_step))
                ve.wait_ge(*st.settled())

            big = lbs[:, 0:4]
            link(V.tensor_tensor(big, pro[:, 0:4], pro[:, 4:8], ALU.max))
            link(V.tensor_tensor(lbs[:, 4:12].rearrange("p (l h) -> p l h", l=2),
                                 pro[:, 0:8].rearrange("p (l h) -> p l h", l=2),
                                 big.unsqueeze(1).to_broadcast([P, 2, 4]), ALU.subtract))
            V.tensor_copy(lbs[:, 12:20], lbs[:, 4:12]).then_inc(*st.up(mul_ready))
            ve.wait_ge(exp_ready, 1)
            link(V.tensor_tensor(lbs[:, 20:24], lbs[:, 12:16], lbs[:, 16:20], ALU.add))
            link(V.reciprocal(lbs[:, 24:28], lbs[:, 20:24]))
            link(V.tensor_tensor(lbs[:, 12:20].rearrange("p (l h) -> p l h", l=2),
                                 lbs[:, 12:20].rearrange("p (l h) -> p l h", l=2),
                                 lbs[:, 24:28].unsqueeze(1).to_broadcast([P, 2, 4]), ALU.mult))
            link(V.tensor_tensor(lbs[:, 28:32], lbs[:, 12:16], lbs[:, 16:20], ALU.add))
            link(V.tensor_tensor(lbs[:, 32:36], lbs[:, 12:16], lbs[:, 12:16], ALU.subtract))
            link(V.tensor_tensor(lbs[:, 36:40], lbs[:, 28:32], lbs[:, 12:16], ALU.subtract))
            depart(ve, 0)

            def make_h(st, n, gain):
                ve.wait_ge(rs_ready, n)
                for k in range(KD):
                    V.scalar_tensor_tensor(hT[:, k, :], xT[:, k, :], gain[:, k:k + 1], rs[:, 0:T], ALU.mult,
                                           ALU.mult).then_inc(*st.up(h_ready))

            def layer(l):
                st = Steps(ve)

                def link(ins):
                    ins.then_inc(*st.up(dve_step))
                    ve.wait_ge(*st.settled())

                def take(R, name):
                    ve.wait_ge(*R.filled(name))
                    return R.bank(name)

                V.tensor_tensor(sq[:, 0:4, :], xT[:, 0:4, :], xT[:, 0:4, :], ALU.mult).then_inc(*st.up(squares_dve))
                link(V.tensor_copy(lbl[:, 0:4], lbs[:, bass.DynSlice(32 + 4 * l, 4)]))
                link(V.tensor_scalar(lbl[:, 4:8], lbl[:, 0:4], -1.0, 1.0, ALU.mult, ALU.add))
                link(V.tensor_scalar(lbl[:, 0:4], lbl[:, 0:4], 1e-30, None, ALU.max))
                bank = take(AXR, "par")
                V.tensor_copy(prm[:, 0:105], bank[:, 0:105])
                V.tensor_copy(prm[:, P:P + 32], bank[:, P:P + 32]).then_inc(*st.up(ax_dve))
                ve.wait_ge(*st.settled())
                ve.sem_inc(prm_ready, 1)
                bank = take(AXR, "cst")
                V.tensor_copy(cstT[:, :, :].rearrange("p j c -> p (j c)"), bank[:, 0:16 * NJ]).then_inc(*st.up(ax_dve))
                make_h(st, 1, prm[:, 0:8])
                for q in range(1, NSEQ, 2):
                    bank = take(AXR, f"cc{q}")
                    V.tensor_copy(cmpT[:, :, :, q, :].rearrange("p v g t -> p (v g) t"),
                                  bank[:, :].rearrange("p (x t) -> p x t", x=4)).then_inc(*st.up(ax_dve))
                bank = take(AXR, "kt1")
                V.tensor_copy(ktn[:, 1, :], bank[:, 0:T]).then_inc(*st.up(ax_dve))
                for h in range(HH):
                    ve.wait_ge(mm_act, 10 + h + 1)
                    V.tensor_scalar(pH[:, h, :], pH[:, h, :], lbl[:, 4 + h:5 + h], lbl[:, h:h + 1], ALU.mult, ALU.add)
                    V.tensor_scalar(kH[:, h, :], kH[:, h, :], lbl[:, 4 + h:5 + h], None, ALU.mult).then_inc(
                        *st.up(mul_ready))
                for m in range(4):
                    bank = take(AXR, f"nqr{m}")
                    V.tensor_tensor(qT[:, m, :], bank[:, 0:T], con("sinq"), ALU.mult).then_inc(*st.up(ax_dve))
                    link(V.tensor_tensor(qraw[:, m, :], qraw[:, m, :], con("cosq"), ALU.mult))
                    V.tensor_tensor(qT[:, m, :], qT[:, m, :], qraw[:, m, :], ALU.add).then_inc(*st.up(q_ready))
                for h in range(HH):
                    ve.wait_ge(sig_ready, HH + h + 1)
                    V.scalar_tensor_tensor(qH[:, h, :], MM.bank(f"hq{h}")[:, 0:T], HD ** -0.5, sgq[:, h, :], ALU.mult,
                                           ALU.mult).then_inc(*st.up(mul_ready))
                    ve.wait_ge(*st.settled())
                    ve.sem_inc(*st.up(mm_dve))
                ve.sem_inc(*st.up(ql_ready))
                bank = take(AXR, "kcr")
                rot = bank[:, 0:NCS * NCB].rearrange("p (s n) -> p s n", s=NCS)
                V.tensor_tensor(kt1, rot, con("scmp").unsqueeze(1).to_broadcast([P, NCS, NCB]), ALU.mult).then_inc(
                    *st.up(ax_dve))
                link(V.tensor_tensor(kt2, kraw, con("ccmp").unsqueeze(1).to_broadcast([P, NCS, NCB]), ALU.mult))
                V.tensor_tensor(kcT[:, :, :], kt1, kt2, ALU.add).then_inc(*st.up(kc_ready))

                def level_q(kk):
                    m = LEVELS[kk]
                    if m == 0:
                        return
                    if kk >= 2:
                        ve.wait_ge(*AXR.filled(f"lvs{kk - 1}" if LEVELS[kk - 1] < STEPS else f"lv{kk - 1}"))
                    ts = T if m < STEPS else SEQ
                    V.tensor_tensor(qL[:, :, 0:ts], qH[:, :, 0:ts], pH[:, :, 0:ts], ALU.mult).then_inc(
                        *st.up(ql_ready))
                    ve.wait_ge(r_done, kk)
                    ve.wait_ge(*st.settled())
                    if m < STEPS:
                        v = pH[:, :, :].rearrange("p h t -> p (h t)").rearrange("p (n u m) -> p n u m", u=2, m=m)
                        V.tensor_tensor(v[:, :, 1, :], v[:, :, 1, :],
                                        v[:, :, 0, m - 1:m].to_broadcast([P, HH * T // (2 * m), m]),
                                        ALU.mult).then_inc(*st.up(p_done))
                    else:
                        v = pH[:, :, 0:SEQ].rearrange("p h (n u m) -> p h n u m", u=2, m=m)
                        V.tensor_tensor(v[:, :, :, 1, :], v[:, :, :, 1, :],
                                        v[:, :, :, 0, m - 1:m].to_broadcast([P, HH, SEQ // (2 * m), m]),
                                        ALU.mult).then_inc(*st.up(p_done))
                    ve.wait_ge(*st.settled())

                def level_take(kk):
                    bank = take(AXR, f"lv{kk}")
                    a, b = CONST["level"]
                    mask = cst_all[:, a + S1 * kk:a + S1 * kk + S1].bitcast(I32)
                    V.copy_predicated(acc[:, 0:2].rearrange("p i h t -> p (i h) t"),
                                      mask.unsqueeze(1).to_broadcast([P, 8, S1]),
                                      bank[:, :].rearrange("p (x t) -> p x t", t=S1)).then_inc(*st.up(ax_dve))
                    if LEVELS[kk] < STEPS:
                        bank = take(AXR, f"lvs{kk}")
                        V.copy_predicated(acc[0:64, 2], mask[0:64].unsqueeze(1).to_broadcast([64, HH, S1]),
                                          bank[0:64, 0:256].rearrange("p (x t) -> p x t", t=S1)).then_inc(
                                              *st.up(ax_dve))
                    ve.wait_ge(*st.settled())

                def normalise(n, cols):
                    link(V.tensor_scalar(sm[:, cols], sm[:, cols], 1e-30, None, ALU.max))
                    link(V.reciprocal(sm[:, cols], sm[:, cols]))

                def out_gate(h):
                    ve.wait_ge(sig_ready, 2 * HH + h + 1)
                    V.tensor_tensor(gH[:, h, :], MM.bank(f"hg{h}")[:, 0:T], gH[:, h, :], ALU.mult).then_inc(
                        *st.up(mul_ready))
                    ve.wait_ge(*st.settled())
                    ve.sem_inc(*st.up(mm_dve))

                link(V.memset(acc[:, :, :, :], 0.0))
                for n, (i, g) in enumerate(UNITS):
                    nk = P * (i + 1)
                    if 2 * n:
                        level_q(2 * n)
                    level_take(2 * n)
                    if n == 1:
                        out_gate(0)
                    if n == 0:
                        ve.wait_ge(*AXR.filled("vc2"))
                    else:
                        ve.wait_ge(*AXR.filled(f"tpc{n - 1}"))
                    a, b = CONST["causal"]
                    mask = cst_all[:, b - nk:b]
                    for r in range(GRP):
                        bank = take(AXR, f"sc{n}_{r}")
                        for w in range(2):
                            c = 4 * (w + 1) + r
                            last = V.tensor_tensor_reduce(prob[:, r, w, 0:nk], bank[:, 256 * w:256 * w + nk], mask, 1.0,
                                                          -3e38, ALU.add, ALU.max, mx[:, c:c + 1])
                        last.then_inc(*st.up(ax_dve))
                    bank = take(AXR, f"scc{n}")
                    a, b = CONST["cneg"]
                    neg = cst_all[:, a + NCB * i:a + NCB * i + NCB]
                    a, b = CONST["c01"]
                    one = cst_all[:, a + NCB * i:a + NCB * i + NCB]
                    pc = pcs[:, 0:60].rearrange("p (r n) -> p r n", r=GRP)
                    V.tensor_tensor(pc, bank[:, 0:60].rearrange("p (r n) -> p r n", r=GRP),
                                    neg.unsqueeze(1).to_broadcast([P, GRP, NCB]), ALU.add).then_inc(*st.up(ax_dve))
                    ve.wait_ge(*st.settled())
                    link(V.tensor_reduce(mx[:, 0:4], pc, AX.X, ALU.max))
                    V.tensor_tensor(pc, pc, mx[:, 0:4].unsqueeze(2).to_broadcast([P, GRP, NCB]), ALU.subtract)
                    V.tensor_scalar(nm[:, 0:12], mx[:, 0:12], -SCALE, None, ALU.mult).then_inc(*st.up(max_ready))
                    if 2 * n + 1 < len(LEVELS):
                        level_q(2 * n + 1)
                        level_take(2 * n + 1)
                    else:
                        ve.wait_ge(*AXR.filled(f"lv{len(LEVELS) - 1}"))
                        link(V.tensor_tensor(qL[:, :, :], qH[:, :, :], pH[:, :, :], ALU.mult))
                        ve.sem_inc(*st.up(ql_ready))
                    if n:
                        out_gate(n)
                    ve.wait_ge(exp_ready, n + 1)
                    link(V.tensor_tensor(pc, pc, one.unsqueeze(1).to_broadcast([P, GRP, NCB]), ALU.mult))
                    link(V.tensor_reduce(sm[:, 0:4], pc, AX.X, ALU.add))
                    normalise(n, slice(0, 12))
                    gate = gts[:, i, :].rearrange("p (b h) -> p b h", b=3)[:, :, 4 * g:4 * g + 4]
                    link(V.tensor_tensor(wt[:, 0:12].rearrange("p (b r) -> p b r", b=3), gate,
                                         sm[:, 0:12].rearrange("p (b r) -> p b r", b=3), ALU.mult))
                    V.tensor_tensor(pc, pc, wt[:, 0:4].unsqueeze(2).to_broadcast([P, GRP, NCB]), ALU.mult)
                    for r in range(GRP):
                        for w in range(2):
                            c = 4 * (w + 1) + r
                            last = V.tensor_scalar(prob[:, r, w, 0:nk], prob[:, r, w, 0:nk], wt[:, c:c + 1], None,
                                                   ALU.mult)
                    last.then_inc(*st.up(scaled))
                    for x in range(1, 2 * (i + 1), 2):
                        bank = take(AXR, f"tp{n}_{x}")
                        V.tensor_copy(probT[:, x, :], bank[:, :]).then_inc(*st.up(ax_dve))
                    bank = take(AXR, f"ov{n}")
                    V.tensor_copy(oN[64 * g:64 * g + 64, :, P * i:P * i + P],
                                  bank[64 * g:64 * g + 64, :].rearrange("p (r q) -> p r q", r=GRP)).then_inc(
                                      *st.up(ax_dve))
                for hb in range(2):
                    bank = take(AXR, f"gsel{hb}")
                    t3 = gtmp[:, 0:24].rearrange("p (x r) -> p x r", r=GRP)
                    V.tensor_tensor(t3, bank[:, 0:24].rearrange("p (x r) -> p x r", r=GRP),
                                    con("rrow").unsqueeze(1).to_broadcast([P, 6, GRP]), ALU.mult).then_inc(
                                        *st.up(ax_dve))
                    ve.wait_ge(*st.settled())
                    link(V.tensor_reduce(gsel[:, hb, :], t3, AX.X, ALU.add))
                for h in (1, 3):
                    bank = take(AXR, f"krt{h}")
                    V.tensor_copy(krP[:, h].rearrange("p i d -> p (i d)"), bank[:, 0:256])
                    V.tensor_copy(krS[0:SMP, h, :], bank[0:SMP, 256:384]).then_inc(*st.up(ax_dve))
                for hb in range(2):
                    for x in (1, 3):
                        bank = take(AXR, f"skt{hb}_{x}")
                        V.tensor_copy(kvT[:, x // 2, 2 * (x % 2):2 * (x % 2) + 2, :].rearrange("p b t -> p (b t)"),
                                      bank[:, :]).then_inc(*st.up(ax_dve))
                    for c in (2 * hb, 2 * hb + 1):
                        bank = take(AXR, f"ds{c}")
                        if c == 0:
                            V.tensor_copy(sP[:, 0].rearrange("p h v -> p (h v)"), bank[:, :]).then_inc(*st.up(s_ready))
                        else:
                            for h in range(HH):
                                end = pH[:, h, S1 * c + S1 - 1:S1 * c + S1]
                                last = V.scalar_tensor_tensor(sP[:, c, h, :], sP[:, c - 1, h, :], end,
                                                              bank[:, P * h:P * h + P], ALU.mult, ALU.add)
                            last.then_inc(*st.up(s_ready))
                        ve.wait_ge(*st.settled())
                        ve.sem_inc(*st.up(ax_dve))
                    for g in range(KVH):
                        n = 4 + 2 * hb + g
                        a, b = CONST["newneg"]
                        mask = cst_all[:, a + SMP * hb:a + SMP * hb + SMP]
                        bank = take(AXR, f"ssb{n}")
                        m1 = mx[:, 4:6]
                        V.tensor_reduce(m1, AXR.bank(f"ssa{n}")[:, :].rearrange("p (w k) -> p w k", w=2), AX.X, ALU.max)
                        for w in range(2):
                            V.tensor_tensor_reduce(snew[:, w, :], bank[:, SMP * w:SMP * w + SMP], mask, 1.0, -3e38,
                                                   ALU.add, ALU.max, mx[:, 6 + w:7 + w])
                        link(V.tensor_reduce(mx[:, 0:1], bank[:, P:P + NCB], AX.X, ALU.max))
                        link(V.tensor_tensor(mx[:, 1:3], mx[:, 4:6], mx[:, 6:8], ALU.max))
                        V.tensor_scalar(nm[:, 0:3], mx[:, 0:3], -SCALE, None, ALU.mult).then_inc(*st.up(max_ready))
                        ve.wait_ge(exp_ready, n + 1)
                        link(V.tensor_tensor(sm[:, 1:3], sm[:, 1:3], sm[:, 3:5], ALU.add))
                        normalise(n, slice(0, 3))
                        gate = gsel[:, hb, :].rearrange("p (b g) -> p b g", b=3)[:, :, g]
                        link(V.tensor_tensor(wt[:, 0:3], gate, sm[:, 0:3], ALU.mult))
                        V.tensor_scalar(pcs[:, 0:NCB], pcs[:, 0:NCB], wt[:, 0:1], None, ALU.mult)
                        for w in range(2):
                            V.tensor_scalar(snew[:, w, :], snew[:, w, :], wt[:, w + 1:w + 2], None, ALU.mult)
                            last = V.tensor_scalar(sprob[:, w, :], sprob[:, w, :], wt[:, w + 1:w + 2], None, ALU.mult)
                        last.then_inc(*st.up(scaled))
                        bank = take(AXR, f"tps{n}")
                        V.tensor_copy(sprobT[:, :, :].rearrange("p x c -> p (x c)"), bank[:, :]).then_inc(
                            *st.up(ax_dve))
                        bank = take(AXR, f"ov{n}")
                        for b in range(4):
                            t0 = SEQ + STEPS * (4 * hb + b)
                            last = V.tensor_copy(oN[64 * g:64 * g + 64, :, t0:t0 + STEPS],
                                                 bank[64 * g:64 * g + 64, 32 * b:32 * b + 32].rearrange(
                                                     "p (r s) -> p r s", r=GRP))
                        last.then_inc(*st.up(ax_dve))
                ve.wait_ge(r_done, len(LEVELS) + 1)
                for h in range(HH):
                    s0 = slot(f"st{h // 2}")[:, 0:2048].rearrange("p (h b v) -> p h b v", h=2, b=NSEQ)
                    bank = take(AXR, f"o{h}")
                    for c in (0, 2):
                        V.tensor_copy(oS[:, h, S1 * c:S1 * c + S1], bank[:, S1 * c:S1 * c + S1])
                    V.tensor_copy(oS[:, h, SEQ:T], bank[:, SEQ:T]).then_inc(*st.up(ax_dve))
                    bank = take(AXR, f"oo{h}")
                    for c in (1, 3):
                        last = V.tensor_copy(oS[:, h, S1 * c:S1 * c + S1], bank[:, S1 * c:S1 * c + S1])
                    last.then_inc(*st.up(ax_dve))
                    for y, name in enumerate((f"dsa{h}", f"dsb{h}")):
                        bank = take(AXR, name)
                        for b in range(4):
                            q = 4 * y + b
                            end = pH[:, h, SEQ + STEPS * q + STEPS - 1:SEQ + STEPS * q + STEPS]
                            last = V.scalar_tensor_tensor(s0[:, h % 2, q, :], s0[:, h % 2, q, :], end,
                                                          bank[:, P * b:P * b + P], ALU.mult, ALU.add)
                        last.then_inc(*st.up(ax_dve))
                    ve.wait_ge(*st.settled())
                    ve.sem_inc(*st.up(sn_ready))
                ve.wait_ge(rso_ready, 1)
                link(V.scalar_tensor_tensor(oS[:, :, :].rearrange("p h t -> p (h t)"),
                                            oS[:, :, :].rearrange("p h t -> p (h t)"), prm[:, 16:17],
                                            rsH[:, :, :].rearrange("p h t -> p (h t)"), ALU.mult, ALU.mult))
                link(V.tensor_tensor(oH[:, :, :], oS[:, :, :], gH[:, :, :], ALU.mult))
                ve.sem_inc(oh_ready, 4)
                for m in range(KD):
                    ve.wait_ge(mm_act, 17 + 2 * m + 2)
                    for buf, name in ((merged[:, m, :], f"bra{m}"), (mgs[:, m % MGB, :], f"brb{m}")):
                        bank = take(AXR, name)
                        V.tensor_tensor(buf, bank[:, 0:T], buf, ALU.mult).then_inc(*st.up(ax_dve))
                def split(u):
                    ve.wait_ge(w_high, u + 1)
                    V.tensor_tensor(unit_of(u, ring_r), unit_of(u, ring), unit_high(u).bitcast(F32),
                                    ALU.subtract).then_inc(*st.up(w_low))

                for m in range(KD):
                    if m >= KD - 2:
                        split(m - KD + 2)
                    bank = take(MM, f"wo{m}")
                    V.tensor_tensor(xT[:, m, :], xT[:, m, :], bank[:, 0:T], ALU.add).then_inc(*st.up(x_ready))
                    ve.wait_ge(*st.settled())
                    ve.sem_inc(*st.up(mm_dve))
                V.tensor_tensor(sq[:, 0:4, :], xT[:, 0:4, :], xT[:, 0:4, :], ALU.mult).then_inc(*st.up(squares_dve))
                ve.wait_ge(rs_ready, 2)
                for k in range(KD + 2):
                    if k < KD:
                        V.scalar_tensor_tensor(hT[:, k, :], xT[:, k, :], prm[:, 8 + k:9 + k], rs[:, 0:T], ALU.mult,
                                               ALU.mult).then_inc(*st.up(h_ready))
                    if k >= 2:
                        ve.wait_ge(h_hi, k - 1)
                        V.tensor_tensor(h_low[:, k - 2, :], hT[:, k - 2, :], h_high[:, k - 2, :].bitcast(F32),
                                        ALU.subtract).then_inc(*st.up(h_lo))
                for j in range(NJ):
                    if j:
                        split(j + 1)
                    gx, cv = gext[j % 2], cvt[j % 2]
                    ve.wait_ge(mm_act, 33 + j + 1)
                    ve.wait_ge(pre_ready, j + 1)
                    gs3 = gx[:, 2 + SEQ:GX].rearrange("p (b s) -> p b s", b=NSEQ)
                    cs3 = cv[:, SEQ:T].rearrange("p (b s) -> p b s", b=NSEQ)
                    for tap in (1, 0):
                        c = 39 + NJ * tap + j
                        V.scalar_tensor_tensor(cv[:, 0:SEQ], gx[:, tap:tap + SEQ], prm[:, c:c + 1], cv[:, 0:SEQ],
                                               ALU.mult, ALU.add)
                        last = V.scalar_tensor_tensor(cs3, gs3[:, :, tap:tap + STEPS], prm[:, c:c + 1], cs3, ALU.mult,
                                                      ALU.add)
                        if tap:
                            link(last)
                    last.then_inc(*st.up(conv_ready))
                    ve.wait_ge(gelu_ready, j + 1)
                    bank = take(MM, f"u{j}")
                    V.tensor_tensor(cv, cv, bank[:, 0:T], ALU.mult).then_inc(*st.up(mm_dve))
                    ve.wait_ge(*st.settled())
                    link(V.tensor_copy(act_high[:, j, :], cv))
                    V.tensor_tensor(act_low[:, j, :], cv, act_high[:, j, :].bitcast(F32), ALU.subtract).then_inc(
                        *st.up(act_ready))
                for u in range(NJ + 1, len(SPLIT)):
                    if u == NJ + 3:
                        for n in range(6):
                            bank = take(AXR, f"cv{n}")
                            w = P * (4 if n < 5 else 2)
                            V.tensor_copy(cvo[0:18, 512 * n:512 * n + w], bank[0:18, 0:w]).then_inc(*st.up(cvo_ready))
                            ve.wait_ge(*st.settled())
                            ve.sem_inc(*st.up(ax_dve))
                    split(u)
                    if u == NJ + 10:
                        for m in range(4):
                            bank = take(MM, f"dn0_{m}")
                            V.tensor_tensor(xT[:, m, :], xT[:, m, :], bank[:, 0:T], ALU.add).then_inc(*st.up(x_ready))
                for m in range(4):
                    bank = take(AXR, f"dn1_{m}")
                    V.tensor_tensor(xT[:, 4 + m, :], xT[:, 4 + m, :], bank[:, 0:T], ALU.add).then_inc(*st.up(x_ready))
                ve.wait_ge(*st.settled())

            with ve.Fori(0, DEPTH) as l:
                layer(l)
                depart(ve, l + 1)
            st = Steps(ve)
            V.tensor_tensor(sq[:, 0:4, :], xT[:, 0:4, :], xT[:, 0:4, :], ALU.mult).then_inc(*st.up(squares_dve))
            make_h(st, 1, pro[:, 8:16])
            n = 0
            for k0 in range(0, KD, 4):
                for i in range(3):
                    ve.wait_ge(mm_full, n + 1)
                    last = V.tensor_copy(yout[0:TM[i], i, P * k0:P * k0 + 512], mmb[n % 4][0:TM[i], :])
                    last.then_inc(*st.up(mm_dve))
                    n += 1
            ve.wait_ge(*st.settled())
            ve.sem_inc(y_ready, 1)

        @block.gpsimd
        def _(po):
            G = nc.gpsimd
            po.wait_ge(consts_in, 32)
            depart(po, 0)

            def layer(l):
                st = Steps(po)

                def link(ins):
                    ins.then_inc(*st.up(pool_step))
                    po.wait_ge(*st.settled())

                def pair_rows(q, src):
                    G.tensor_copy(craw[:, q, :].rearrange("p (x a d) -> p x a d", x=4, a=2),
                                  src.rearrange("p a (x d) -> p x a d", x=4)).then_inc(*st.up(rows_ready))

                po.wait_ge(*landed_at("cmp", l))
                po.sem_inc(spare, 1)
                for q in range(NSEQ):
                    pair_rows(q, slot("cmp").rearrange("p (s a c) -> p s a c", s=NSEQ, a=2)[:, q])
                po.wait_ge(mm_act, 3)
                pair_rows(NSEQ, ctok[:, 0:2, :])
                for i in range(3):
                    n = TM[i]
                    po.wait_ge(mm_act, 3 + i + 1)
                    for w in range(2):
                        x = stok[0:n, i, 256 * w:256 * w + P].rearrange("p (g d) -> p g d", g=2)[:, :, 0:16]
                        tc, ts = (rtmp[0:n, 64 * y:64 * y + 32].rearrange("p (g d) -> p g d", g=2) for y in range(2))
                        a, b = CONST["cosk"]
                        link(G.tensor_tensor(tc, x, cst_all[0:n, a + 16 * i:a + 16 * i + 16].unsqueeze(1).to_broadcast(
                            [n, 2, 16]), ALU.mult))
                        a, b = CONST["sink"]
                        link(G.tensor_tensor(ts, x, cst_all[0:n, a + 16 * i:a + 16 * i + 16].unsqueeze(1).to_broadcast(
                            [n, 2, 16]), ALU.mult))
                        link(G.tensor_tensor(x[:, :, 0:8], tc[:, :, 0:8], ts[:, :, 8:16], ALU.subtract))
                        link(G.tensor_tensor(x[:, :, 8:16], ts[:, :, 0:8], tc[:, :, 8:16], ALU.add))
                    po.sem_inc(*st.up(k_roped))
                po.wait_ge(squares_dve, 1)
                po.wait_ge(*AXR.filled("norm1"))
                link(G.memset(rH[:, :, :], 1.0))
                po.wait_ge(q_ready, 4)
                for b in range(NSEQ):
                    last = G.tensor_copy(qS[:, b], qT[:, :, SEQ + STEPS * b:SEQ + STEPS * (b + 1)])
                last.then_inc(*st.up(qs_ready))
                po.wait_ge(mul_ready, 2 * HH)
                po.sem_inc(*st.up(kl_ready))
                for kk in range(1, len(LEVELS)):
                    m = LEVELS[kk]
                    if m == 1:
                        po.sem_inc(*st.up(kl_ready))
                    else:
                        if m > 2:
                            po.wait_ge(*AXR.filled(f"lvs{kk - 1}" if LEVELS[kk - 1] < STEPS else f"lv{kk - 1}"))
                        ts = T if m < STEPS else SEQ
                        G.tensor_tensor(kL[:, :, 0:ts], kH[:, :, 0:ts], rH[:, :, 0:ts], ALU.mult).then_inc(
                            *st.up(kl_ready))
                    po.wait_ge(*st.settled())
                    if kk > 1:
                        po.wait_ge(p_done, kk - 1)
                    if m < STEPS:
                        r = rH[:, :, :].rearrange("p h t -> p (h t)").rearrange("p (n u m) -> p n u m", u=2, m=m)
                        p_ = pH[:, :, :].rearrange("p h t -> p (h t)").rearrange("p (n u m) -> p n u m", u=2, m=m)
                        link(G.tensor_tensor(r[:, :, 0, :], r[:, :, 0, :],
                                             p_[:, :, 1, m - 1:m].to_broadcast([P, HH * T // (2 * m), m]), ALU.mult))
                    else:
                        for h in range(HH):
                            r = rH[:, h, 0:SEQ].rearrange("p (n u m) -> p n u m", u=2, m=m)
                            p_ = pH[:, h, 0:SEQ].rearrange("p (n u m) -> p n u m", u=2, m=m)
                            last = G.tensor_tensor(r[:, :, 0, :], r[:, :, 0, :],
                                                   p_[:, :, 1, m - 1:m].to_broadcast([P, SEQ // (2 * m), m]), ALU.mult)
                        link(last)
                    po.sem_inc(*st.up(r_done))
                po.wait_ge(*AXR.filled(f"lv{len(LEVELS) - 1}"))
                G.tensor_tensor(kL[:, :, :], kH[:, :, :], rH[:, :, :], ALU.mult).then_inc(*st.up(kl_ready))
                po.wait_ge(*st.settled())
                po.sem_inc(*st.up(r_done))
                po.sem_inc(*st.up(r_done))
                po.wait_ge(mm_act, 17)
                for h in range(HH):
                    if h:
                        po.wait_ge(*AXR.filled(f"dsb{h - 1}"))
                    v = vH[0:SMP, 2, P * h:P * h + P].unsqueeze(1).to_broadcast([SMP, NSEQ, P])
                    G.tensor_tensor(vX[0:SMP], v, con("seqrow", SMP).unsqueeze(2).to_broadcast([SMP, NSEQ, P]),
                                    ALU.mult).then_inc(*st.up(vx_ready))
                for m in range(KD):
                    po.wait_ge(*AXR.emptied_at(f"brb{m}"))
                    G.tensor_tensor(merged[:, m, :], merged[:, m, :], mgs[:, m % MGB, :], ALU.add).then_inc(
                        *st.up(merged_ready))
                po.wait_ge(*MM.filled("wo7"))
                for n in range(2):
                    G.memset(gext[n][:, 0:2], 0.0)
                for j in range(NJ + 1):
                    gx = gext[j % 2]
                    if j < NJ:
                        if j >= 2:
                            po.wait_ge(conv_ready, j - 1)
                        G.tensor_copy(gx[:, 2 + SEQ:GX].rearrange("p (b s) -> p b s", b=NSEQ)[:, :, 0:2],
                                      cstT[:, j, :].rearrange("p (b w) -> p b w", b=NSEQ)).then_inc(*st.up(pre_ready))
                    if j:
                        gp = gext[(j - 1) % 2]
                        po.wait_ge(mm_act, 33 + j)
                        G.tensor_copy(glast[:, j - 1, 0:2], gp[:, SEQ:SEQ + 2])
                        link(G.tensor_copy(glast[:, j - 1, 2:18].rearrange("p (b w) -> p b w", b=NSEQ),
                                           gp[:, 2 + SEQ:GX].rearrange("p (b s) -> p b s", b=NSEQ)[:, :,
                                                                                                STEPS:STEPS + 2]))
                po.sem_inc(glast_ready, 1)

            with po.Fori(0, DEPTH) as l:
                layer(l)
                depart(po, l + 1)


def shape_constants(np):
    out = np.zeros((P, NCONST), np.float32)

    def put(name, v):
        a, b = CONST[name]
        v = np.asarray(v, np.float32)
        out[:v.shape[0], a:b] = v.reshape(v.shape[0], -1)

    put("ident", np.eye(P))
    put("ones", np.ones((P, P)))
    half = ND // 8
    perm = np.zeros((P, P))
    for g in range(2):
        for d in range(half):
            perm[64 * g + half + d, 64 * g + d] = -1
            perm[64 * g + d, 64 * g + half + d] = 1
    put("perm", perm)
    inv = np.float32(500000.0) ** (-np.arange(half, dtype=np.float32) * np.float32(2.0) / np.float32(2 * half))

    def angles(pos):
        return pos.astype(np.float32)[:, None] * inv[None, :].astype(np.float32)

    pos = np.concatenate([np.arange(SEQ), PAST + np.tile(np.arange(STEPS), NSEQ)])

    def table(pos):
        ang = angles(pos)
        c, s = np.ones((ND, len(pos)), np.float32), np.zeros((ND, len(pos)), np.float32)
        c[:half] = c[half:2 * half] = np.cos(ang).T
        s[:half] = s[half:2 * half] = np.sin(ang).T
        return np.tile(c, (2, 1)), np.tile(s, (2, 1))

    for (cn, sn), ps in ((("cosq", "sinq"), pos), (("ccmp", "scmp"), np.arange(NCB) * 16 + 31)):
        c, s = table(ps)
        put(cn, c)
        put(sn, s)
    ang = angles(np.concatenate([pos, np.zeros(64)])).reshape(3, P, half).transpose(1, 0, 2)
    put("cosk", np.concatenate([np.cos(ang), np.cos(ang)], 2))
    put("sink", np.concatenate([np.sin(ang), np.sin(ang)], 2))
    q = np.arange(P)
    put("causal", np.concatenate([np.zeros((P, P)), np.where(q[None, :] <= q[:, None], 0, NEG)], 1))
    end = np.arange(NCB) * 16 + 31
    ok = np.stack([end[None, :] <= (q[:, None] + P * i) for i in range(2)], 1)
    put("cneg", np.where(ok, 0, NEG))
    put("c01", ok)
    b4, s = q // 32, q % 8
    key = np.arange(SMP)
    put("newneg", np.stack([np.where((key[None, :] // 8 == 4 * hb + b4[:, None]) & (key[None, :] % 8 <= s[:, None]), 0,
                                     NEG) for hb in range(2)], 1))
    ks, qs = np.arange(P)[:, None] % CHUNK, np.arange(CHUNK)[None, :]
    lev = []
    for m in LEVELS:
        if m == 0:
            lev.append(ks == qs)
        else:
            lev.append((ks // (2 * m) == qs // (2 * m)) & (ks % (2 * m) < m) & (qs % (2 * m) >= m))
    put("level", np.stack(lev, 1))
    tok = np.arange(SMP)[:, None]
    put("sel", np.stack([(tok == (4 * hb + b4[None, :]) * 8 + s[None, :]) for hb in range(2)], 1))
    put("seqrow", tok // 8 == np.arange(NSEQ)[None, :])
    put("rrow", (q[:, None] % 32) // 8 == np.arange(GRP)[None, :])
    return out


_INS = ["x_prompt", "x_sample", "cache_cmp_kv", "cache_slc_kv", "cache_win_kv", "state_hgrn", "state_conv", "page_table",
        "norm_mix", "w_in", "hg_lower", "hg_norm", "cmp_pe", "cmp_w1", "cmp_w2", "w_branch", "w_out", "norm_ffn",
        "w_gate_up", "conv_w", "conv_b", "w_down", "norm_final"]
_KV = (2, KVH, ND)
_OUTS = [(1, SEQ, D), (NSEQ, STEPS, D), (DEPTH, 1, SEQ) + _KV, (DEPTH, NSEQ, STEPS) + _KV, (DEPTH, 1, SEQ) + _KV,
         (DEPTH, NSEQ, STEPS) + _KV, (DEPTH, 1, SEQ) + _KV, (DEPTH, NSEQ, PAST) + _KV, (DEPTH, 1, HH, HD, HD),
         (DEPTH, NSEQ, HH, HD, HD), (DEPTH, 1, 2, DFF), (DEPTH, NSEQ, 2, DFF)]


def kernel(**inputs):
    import numpy as np
    import concourse.bacc as bacc
    from concourse.bass_utils import run_bass_kernel_spmd

    nc = bacc.Bacc("TRN2", target_bir_lowering=False, num_devices=1)
    arrays, args = {}, []
    for name in _INS:
        a = np.ascontiguousarray(inputs[name])
        arrays[f"in_{name}"] = a
        args.append(nc.dram_tensor(f"in_{name}", a.shape, mybir.dt.from_np(a.dtype), kind="ExternalInput").ap())
    a = shape_constants(np)
    arrays["in_constants"] = a
    args.append(nc.dram_tensor("in_constants", a.shape, F32, kind="ExternalInput").ap())
    for i, shape in enumerate(_OUTS):
        args.append(nc.dram_tensor(f"out_{i}", shape, F32, kind="ExternalOutput").ap())
    hybrid_step(nc, *args)
    r = run_bass_kernel_spmd(nc, [arrays], core_ids=[0])
    return tuple(r.results[0][f"out_{i}"] for i in range(len(_OUTS)))
```

```python
from contextlib import ExitStack

import concourse.bass as bass
from concourse import mybir

F32 = mybir.dt.float32
F32R = mybir.dt.float32r
I32 = mybir.dt.int32
ALU = mybir.AluOpType
ACT = mybir.ActivationFunctionType
AX = mybir.AxisListType

P = 128
D, DEPTH, SEQ, NSEQ, STEPS, PAST = 1024, 2, 256, 8, 8, 256
PAGE, NPAGE, POOLN = 128, 2, 20
MIX, HH, HD = 512, 4, 128
NH, KVH, GRP, ND = 8, 2, 4, 64
KD = D // P
SMP = NSEQ * STEPS
T = SEQ + SMP
DFF = 2816
NJ = DFF // P
JPB = 2
NCB = 15
NCS = NSEQ + 1
CHUNK = 64
NEG = -1e30
EPS = 1e-6
SCALE = ND ** -0.5
C_HQ, C_HF, C_HI, C_HG, C_NQ, C_KC, C_KS, C_GT, C_MG = 0, 512, 1024, 1536, 2048, 2560, 2816, 3328, 3352
TM = [P, P, SMP]
LEVELS = [0, 1, 2, 4, 8, 16, 32]
SLOT = 4096
NSLOT = 4
MGB = 6
DOWN = [[6, 6, 5, 5], [8, 8, 6]]

BLOCKS = (["par", "cmp", "w_kvc", "w_kvn", "w_nq", "w_hf", "w_hq", "w_cmp", "w_hi", "w_hg", "kv0", "kv1", "mg0", "mg1",
           "st0", "st1", "mg2", "br0", "mg3", "br1", "wo0", "wo1"] + [f"ff{n}" for n in range(NJ // JPB)]
          + [f"dn{mh}_{n}" for mh in range(2) for n in range(len(DOWN[mh]))])
NBLK = len(BLOCKS)
assert NBLK % NSLOT == 0
BNO = {b: n for n, b in enumerate(BLOCKS)}
DMAS = {b: 1 for b in BLOCKS}
DMAS.update(par=7, cmp=2 * NSEQ, w_kvc=2, w_cmp=4, kv0=4 * NPAGE + 4, kv1=4 * NPAGE + 4, st0=2, st1=2, br0=3,
            br1=3)
for _n in range(4):
    DMAS[f"mg{_n}"] = 2
for _n in range(NJ // JPB):
    DMAS[f"ff{_n}"] = 2
SLOT_TOTAL = [16 * sum(DMAS[b] for b in BLOCKS[s::NSLOT]) for s in range(NSLOT)]
LANDED = {b: 16 * sum(DMAS[c] for c in BLOCKS[n % NSLOT:n + 1:NSLOT]) for b, n in BNO.items()}
LAST_USE = {"par": "cst", "w_kvc": "kvc2", "w_kvn": "kvn2", "w_nq": "nq3", "w_hf": "hf3",
            "w_hq": "hq3", "w_cmp": "vc2", "w_hi": "hi2", "kv0": "ov5", "kv1": "ov7", "w_hg": "hg3"}
LAST_USE.update({f"mg{n}": f"mgb{2 * n + 1}" for n in range(4)})
LAST_USE.update({f"{b}{n}": f"{u}{4 * n + 3}" for b, u in (("br", "bra"), ("wo", "wo")) for n in range(2)})
LAST_USE.update({f"ff{n}": f"u{JPB * n + JPB - 1}" for n in range(NJ // JPB)})
LAST_USE.update({f"dn{mh}_{len(DOWN[mh]) - 1}": f"dn{mh}_3" for mh in range(2)})
SPLIT = []
for _n in range(2):
    SPLIT += [(f"mg{_n + 2}", 0, KD), (f"mg{_n + 2}", 1, KD), (f"br{_n}", 4, 4), (f"br{_n}", 0, 4)]
SPLIT += [(f"wo{_n // 2}", _n % 2, KD) for _n in range(4)]
FFU = len(SPLIT)
SPLIT += [(f"ff{j // JPB}", j % JPB, KD) for j in range(NJ)]
DNU = len(SPLIT)
for _mh in range(2):
    for _n, _kn in enumerate(DOWN[_mh]):
        SPLIT += [(f"dn{_mh}_{_n}", 0, (_kn + 1) // 2), (f"dn{_mh}_{_n}", (_kn + 1) // 2, _kn // 2)]
UNIT_COLS = 2048

UNITS = [(i, g) for i in range(2) for g in range(KVH)]


def mm_plan():
    out = [(f"kvc{i}", "A") for i in range(3)] + [(f"kvn{i}", "A") for i in range(3)]
    out += [(f"nq{m}", "A") for m in range(4)] + [(f"hf{h}", "A") for h in range(HH)]
    out += [(f"hq{h}", "V") for h in range(HH)] + [(f"hi{i}", "A") for i in range(3)]
    out += [(f"hg{h}", "V") for h in range(HH)]
    for m in range(KD):
        out += [(f"mga{m}", "A"), (f"mgb{m}", "A")]
    out += [(f"wo{m}", "V") for m in range(KD)]
    for j in range(NJ):
        out += [(f"g{j}", "A"), (f"u{j}", "V")]
    return out + [(f"dn0_{m}", "V") for m in range(4)]


def ax_plan():
    out = [("par", "V"), ("norm1", "A"), ("cst", "V")]
    out += [(f"cc{s}", "AV"[s % 2]) for s in range(NSEQ)]
    out += [("cp", "A"), ("kt0", "A"), ("kt1", "V")]
    out += [(f"nqr{m}", "V") for m in range(4)]
    out += [("hidk", "A"), ("hidv", "A"), ("kcm", "A"), ("kcr", "V")] + [(f"vc{n}", "A") for n in range(3)]
    def turned(n):
        return [(f"tp{n}_{x}", "AV"[x % 2]) for x in range(2 * (UNITS[n][0] + 1))] + [(f"tpc{n}", "A"), (f"ov{n}", "V")]

    for n in range(4):
        out += level_plan(2 * n)
        out += [(f"sc{n}_{r}", "V") for r in range(GRP)] + [(f"scc{n}", "V")]
        out += turned(n - 1) if n else []
        out += level_plan(2 * n + 1) if 2 * n + 1 < len(LEVELS) else []
        out += [("gsel0", "V"), ("gsel1", "V")] if n == 0 else []
    out += [(f"krt{h}", "AV"[h % 2]) for h in range(HH)]
    for hb in range(2):
        out += [(f"skt{hb}_{x}", "AV"[x % 2]) for x in range(4)]
        out += turned(3) if hb == 0 else []
        out += [(f"ds{c}", "V") for c in (2 * hb, 2 * hb + 1)]
        for g in range(KVH):
            n = 4 + 2 * hb + g
            out += [(f"ssa{n}", "A"), (f"ssb{n}", "A"), (f"tps{n}", "V"), (f"tpn{n}", "A"), (f"ov{n}", "V")]
    for h in range(HH):
        out += [(f"o{h}", "V"), (f"oo{h}", "V"), (f"dsa{h}", "V"), (f"dsb{h}", "V")]
    out += [(f"on{h}", "A") for h in range(HH)]
    for n in range(2):
        out += [(f"br{x}{m}", "V") for x in "ba" for m in range(4 * n, 4 * n + 4)]
    out += [("norm2", "A")]
    out += [(f"cv{n}", "V") for n in range(6)]
    return out + [(f"dn1_{m}", "V") for m in range(4)]


def level_plan(k):
    return [(f"lv{k}", "V")] + ([(f"lvs{k}", "V")] if LEVELS[k] < STEPS else [])


MM_PLAN, AX_PLAN = mm_plan(), ax_plan()


class Banks:

    def __init__(self, plan, banks, full, emptied):
        self.no = {name: n for n, (name, _) in enumerate(plan)}
        self.plan, self.banks, self.full, self.emptied = plan, banks, full, emptied

    def bank(self, name):
        return self.banks[self.no[name] % len(self.banks)]

    def filled(self, name):
        return self.full, self.no[name] + 1

    def emptied_at(self, name):
        n = self.no[name]
        who = self.plan[n][1]
        return self.emptied[who], sum(1 for _, e in self.plan[:n + 1] if e == who)

    def vacant(self, name):
        n = self.no[name] - len(self.banks)
        return self.emptied_at(self.plan[n][0]) if n >= 0 else None


class Steps:

    def __init__(self, eng):
        self.eng, self.count, self.last = eng, {}, None

    def up(self, sem):
        self.count[sem.name] = self.count.get(sem.name, 0) + 1
        self.last = (sem, self.count[sem.name])
        return sem, 1

    def settled(self):
        return self.last


CONST = {}
_at = 0
for _name, _w in (("ident", P), ("ones", P), ("perm", P), ("cosq", T), ("sinq", T), ("cosk", 48), ("sink", 48),
                  ("ccmp", NCB), ("scmp", NCB), ("causal", 2 * P), ("cneg", 2 * NCB), ("c01", 2 * NCB),
                  ("newneg", 2 * SMP), ("level", 7 * CHUNK), ("sel", 2 * P), ("seqrow", NSEQ), ("rrow", GRP)):
    CONST[_name] = (_at, _at + _w)
    _at += _w
NCONST = _at
NFIRST = CONST["perm"][1]


def hybrid_step(nc, x_prompt, x_sample, cache_cmp, cache_slc, cache_win, state_hgrn, state_conv, page_table, norm_mix,
                w_in, hg_lower, hg_norm, cmp_pe, cmp_w1, cmp_w2, w_branch, w_out, norm_ffn, w_gate_up, conv_w, conv_b,
                w_down, norm_final, consts, y_p, y_s, cmp_p, cmp_s, slc_p, slc_s, win_p, win_s, hg_p, hg_s, cv_p,
                cv_s):
    ctx = ExitStack()
    with ctx:
        def sb(name, cols, dt=F32):
            return ctx.enter_context(nc.sbuf_tensor(name, [P, cols], dt))

        def sem(name):
            return ctx.enter_context(nc.semaphore(name))

        ring_at = (nc.sbuf_base + 31) // 32 * 32
        ring = sb("ring", NSLOT * SLOT)
        xT = sb("xT", KD * T)[:, :].rearrange("p (k t) -> p k t", k=KD)
        hT_at = (nc.sbuf_base + 31) // 32 * 32
        hT = sb("hT", KD * T)[:, :].rearrange("p (k t) -> p k t", k=KD)
        cst_all = sb("consts", NCONST)
        mixb_at = (nc.sbuf_base + 31) // 32 * 32
        mixb = sb("mixb", 14592)
        attb_at = (nc.sbuf_base + 31) // 32 * 32
        attb = sb("attb", 4608)
        work_at = (nc.sbuf_base + 31) // 32 * 32
        work = sb("work", 9096)
        oN = work[:, 0:4 * T].rearrange("p (m t) -> p m t", m=4)
        qT = work[:, 1280:2560].rearrange("p (m t) -> p m t", m=4)
        qS = work[:, 2560:2816].rearrange("p (b r s) -> p b r s", b=NSEQ, r=GRP)
        ktn = work[:, 2816:3456].rearrange("p (w t) -> p w t", w=2)
        vc = work[:, 3456:4608].rearrange("p (s g d) -> p s g d", s=NCS, g=2)
        kcT = work[:, 4608:4608 + NCS * NCB].rearrange("p (s n) -> p s n", s=NCS)
        stok = work[:, 4744:6280].rearrange("p (i c) -> p i c", i=3)
        ctok = work[:, 6280:7048].rearrange("p (i c) -> p i c", i=3)
        kvT = work[:, 7048:9096].rearrange("p (w b t) -> p w b t", w=2, b=4)
        gts = sb("gts", 3 * 24)[:, :].rearrange("p (i c) -> p i c", i=3)
        gsel = sb("gsel", 12)[:, :].rearrange("p (h c) -> p h c", h=2)
        gtmp = sb("gtmp", 24)
        prm = sb("prm", 160)
        cstT = sb("cstT", NJ * 16)[:, :].rearrange("p (j c) -> p j c", j=NJ)
        glast = work[:, 8256:8256 + NJ * 18].rearrange("p (j c) -> p j c", j=NJ)
        lbs = sb("lbs", 8 * 6)
        lbl = sb("lbl", 8)
        pro = sb("pro", 16)
        rs = work[:, 7936:7936 + T]
        pcb = [sb(f"pcs{n}", 64) for n in range(2)]
        mxb = [sb(f"mx{n}", 16) for n in range(2)]
        nmb = [sb(f"nm{n}", 16) for n in range(2)]
        smb = [sb(f"sm{n}", 16) for n in range(2)]
        wt = sb("wt", 16)
        pcs, mx, nm, sm = pcb[0], mxb[0], nmb[0], smb[0]
        rtmp = sb("rtmp", 128)
        hbias = sb("hbias", 2)
        epsb = sb("epsb", 1)
        pages = sb("pages", 16, I32)

        def con(name, rows=P):
            a, b = CONST[name]
            return cst_all[0:rows, a:b]

        ident, ones = con("ident"), con("ones")

        def part(buf, at, cols):
            return buf[:, at:at + cols]

        def heads(at):
            return part(mixb, at, HH * T).rearrange("p (h t) -> p h t", h=HH)

        qH, kH, pH, rH, qL, kL = (heads(1280 * n) for n in range(6))
        oS, sqH, rsH, sgq, oH = rH, kH, qL, kL, qH
        qraw = qL
        vH = part(mixb, 7680, 3 * MIX).rearrange("p (i c) -> p i c", i=3)
        acc = part(mixb, 9216, 3 * 256).rearrange("p (i h t) -> p i h t", i=3, h=HH)
        gH = heads(9984)
        krP = part(mixb, 0, HH * 2 * P).rearrange("p (h i d) -> p h i d", h=HH, i=2)
        krS = part(mixb, 1280 * 5, HH * P).rearrange("p (h d) -> p h d", h=HH)
        craw = part(mixb, 7680, NCS * 512).rearrange("p (s c) -> p s c", s=NCS)
        sP = part(mixb, 11520, 4 * 512).rearrange("p (c h v) -> p c h v", c=4, h=HH)
        vX = part(mixb, 13568, NSEQ * P).rearrange("p (b v) -> p b v", b=NSEQ)
        sq = part(mixb, 0, KD * T).rearrange("p (k t) -> p k t", k=KD)
        ring_r = nc.alloc_sbuf_tensor_at("ring_low", [P, NSLOT * SLOT], F32R, offset=ring_at)
        work_r = nc.alloc_sbuf_tensor_at("work_parts", [P, 7936], F32R, offset=work_at)
        oN_low = part(work_r, 0, 4 * T).rearrange("p (m t) -> p m t", m=4)
        m_low = nc.alloc_sbuf_tensor_at("merged_low", [P, KD * T], F32R, offset=attb_at)[:, :].rearrange(
            "p (k t) -> p k t", k=KD)
        act_r = nc.alloc_sbuf_tensor_at("act_parts", [P, 2 * NJ * T], F32R, offset=mixb_at)
        h_low = nc.alloc_sbuf_tensor_at("h_low", [P, KD * T], F32R, offset=hT_at)[:, :].rearrange(
            "p (k t) -> p k t", k=KD)
        h_high = part(work_r, 1280 + 2 * UNIT_COLS, KD * T).rearrange("p (k t) -> p k t", k=KD)
        oH_low, oH_high, oN_high = (part(act_r, at, 4 * T).rearrange("p (m t) -> p m t", m=4)
                                    for at in (0, 5120, 6400))
        m_high = part(act_r, 2560, KD * T).rearrange("p (k t) -> p k t", k=KD)
        act_high, act_low = (part(act_r, NJ * T * n, NJ * T).rearrange("p (j t) -> p j t", j=NJ) for n in range(2))
        xin = part(mixb, 4096, 3 * D).rearrange("p (i c) -> p i c", i=3)
        yout = part(mixb, 4096, 3 * D).rearrange("p (i c) -> p i c", i=3)
        cmpT = attb[:, :].rearrange("p (v g s t) -> p v g s t", v=2, g=2, s=NCS)
        hid = part(attb, 0, 2 * NCS * NCB).rearrange("p (g s n) -> p g s n", g=2, s=NCS)
        kraw = part(attb, 512, NCS * NCB).rearrange("p (s n) -> p s n", s=NCS)
        kt1, kt2 = (part(attb, 1024 + 256 * n, NCS * NCB).rearrange("p (s n) -> p s n", s=NCS) for n in range(2))
        probs = [part(*at, 4 * 512).rearrange("p (r w k) -> p r w k", r=GRP, w=2) for at in ((attb, 0), (mixb, 11520))]
        probT = part(attb, 2048, 4 * 512).rearrange("p (x c) -> p x c", x=4)
        probTc = part(attb, 4096, 512)
        sprob = part(attb, 1280, 512).rearrange("p (w k) -> p w k", w=2)
        snew = part(attb, 1792, 2 * SMP).rearrange("p (w k) -> p w k", w=2)
        sprobT = part(attb, 1920, 512).rearrange("p (x c) -> p x c", x=4)
        snewT = part(attb, 2560 + 4 * T, 384).rearrange("p (x c) -> p x c", x=3)
        merged = part(attb, 0, KD * T).rearrange("p (k t) -> p k t", k=KD)
        mgs = part(attb, 2560, MGB * T).rearrange("p (b t) -> p b t", b=MGB)
        GX = SEQ + 2 + NSEQ * (STEPS + 2)
        gext = [part(attb, GX * n, GX) for n in range(2)]
        cvt = [part(attb, 680 + T * n, T) for n in range(2)]
        cvo = part(attb, 1320, DFF)
        S1 = CHUNK

        def slot(b):
            s = BNO[b] % NSLOT
            return ring[:, s * SLOT:(s + 1) * SLOT]

        def unit_of(u, buf):
            b, a, n = SPLIT[u]
            s = (BNO[b] % NSLOT) * SLOT
            if b[:2] in ("ff", "mg", "wo"):
                v = buf[:, s:s + SLOT].rearrange("p (k h c) -> p k h c", k=KD, h=4)
                return v[:, :, 2 * a:2 * a + 2, :] if b[:2] == "wo" else v[:, :, a::2, :]
            return buf[:, s + 512 * a:s + 512 * (a + n)].rearrange("p (k h c) -> p k h c", k=n, h=4)

        def unit_high(u):
            b, _, n = SPLIT[u]
            at = 1280 + UNIT_COLS * (u % 2)
            h = 4 if b[:2] in ("dn", "br") else 2
            return work_r[:, at:at + n * h * P].rearrange("p (k h c) -> p k h c", k=n, h=h)

        def kt_of(b, n, width):
            return slot(b)[:, 0:n * width].rearrange("p (k c) -> p k c", k=n)

        mmb = [ctx.enter_context(nc.psum_tensor(f"mm{n}", [P, 512], F32)) for n in range(4)]
        axb = [ctx.enter_context(nc.psum_tensor(f"ax{n}", [P, 512], F32)) for n in range(4)]

        landed = [sem(f"ring_landed{s}") for s in range(NSLOT)]
        arrived, cleared = sem("arrived"), sem("cleared")
        spare = sem("spare")
        first_consts_in, consts_in, copied = sem("first_consts_in"), sem("consts_in"), sem("window_copied")
        first = {}

        def lsem(name):
            s = sem(name)
            first.setdefault("range", []).append(s)
            return s

        down_read = lsem("down_unit_read")
        kv_stored = lsem("keys_and_values_stored")
        on_hi, oh_hi, m_hi, m_lo = lsem("on_high"), lsem("oh_high"), lsem("merged_high"), lsem("merged_low_ready")
        on_ready = lsem("on_parts_ready")
        w_high, w_low, h_hi, h_lo = lsem("weights_high"), lsem("weights_low"), lsem("h_high"), lsem("h_low_ready")
        stored = lsem("outputs_stored")
        state_stored = [lsem("state_stored0"), lsem("state_stored1")]
        mm_full, mm_act, mm_dve = lsem("mm_full"), lsem("mm_emptied_by_act"), lsem("mm_emptied_by_dve")
        ax_full, ax_act, ax_dve = lsem("ax_full"), lsem("ax_emptied_by_act"), lsem("ax_emptied_by_dve")
        dve_step, act_step, pool_step = lsem("dve_step"), lsem("act_step"), lsem("pool_step")
        squares_dve, squares_act, rs_ready, h_ready = (lsem("squares_dve"), lsem("squares_act"), lsem("rs_ready"),
                                                       lsem("h_ready"))
        x_ready, squares_x = lsem("x_ready"), lsem("squares_of_new_x")
        prm_ready = lsem("params_ready")
        k_roped = lsem("k_roped")
        rows_ready = lsem("compressor_rows_ready")
        qraw_ready, q_ready, qs_ready = lsem("qraw_ready"), lsem("q_ready"), lsem("q_sample_ready")
        hid_ready, kraw_ready, kc_ready = lsem("hidden_ready"), lsem("kcmp_raw_ready"), lsem("kcmp_ready")
        sig_ready, mul_ready = lsem("sigmoid_ready"), lsem("hgrn_inputs_ready")
        ql_ready, kl_ready, r_done = lsem("q_level_ready"), lsem("k_level_ready"), lsem("r_updated")
        p_done = lsem("p_updated")
        max_ready, exp_ready, scaled = lsem("max_ready"), lsem("exp_ready"), lsem("probs_scaled")
        vx_ready, s_ready, sn_ready = lsem("vx_ready"), lsem("state_ready"), lsem("new_state")
        sqo_ready, rso_ready, oh_ready = lsem("o_squares"), lsem("o_rs"), lsem("oh_parts_ready")
        oh_raw = lsem("oh_raw")
        merged_ready, pre_ready, conv_ready, gelu_ready, act_ready = (
            lsem("merged_ready"), lsem("prefix_ready"), lsem("conv_ready"), lsem("gelu_ready"), lsem("act_ready"))
        glast_ready, cvo_ready, xin_in, y_ready = lsem("glast_ready"), lsem("cvo_ready"), lsem("x_in"), lsem("y_ready")
        reset = first["range"]
        nums = sorted(s.num for s in reset)
        assert nums == list(range(nums[0], nums[0] + len(nums)))

        MM = Banks(MM_PLAN, mmb, mm_full, {"A": mm_act, "V": mm_dve})
        AXR = Banks(AX_PLAN, axb, ax_full, {"A": ax_act, "V": ax_dve})

        down_units = [u for u, (b, _, _) in enumerate(SPLIT) if b[:2] == "dn"]
        down_inner = [u for u in down_units if u + 1 < len(SPLIT) and SPLIT[u + 1][0][:3] == SPLIT[u][0][:3]]

        def unit_read(u):
            b, a, _ = SPLIT[u]
            n = int(b[2])
            if b[:2] == "mg":
                return MM.filled(f"mgb{2 * n + a}")
            if b[:2] == "br":
                return AXR.filled(f"br{'ab'[a // 4]}{4 * n + 3}")
            if b[:2] == "wo":
                return MM.filled(f"wo{4 * n + 2 * a + 1}")
            if b[:2] == "ff":
                return MM.filled(f"u{u - FFU}")
            if u in down_inner:
                return down_read, down_inner.index(u) + 1
            return (MM if SPLIT[u][0][2] == "0" else AXR).filled(f"{SPLIT[u][0][:3]}_3")

        def landed_at(b, l):
            return landed[BNO[b] % NSLOT], l * SLOT_TOTAL[BNO[b] % NSLOT] + LANDED[b]

        def depart(eng, l):
            eng.sem_inc(arrived, 1)
            eng.wait_ge(cleared, l + 1)

        block = ctx.enter_context(nc.Block())

        @block.sync
        def _(sp):
            def ld(b, out, in_):
                sp.dma_start(out, in_).then_inc(landed[BNO[b] % NSLOT], 16)

            def page(n, lay):
                pg = sp.value_load(pages[0:1, n:n + 1], min_val=0, max_val=POOLN - 1)
                return lay * POOLN + pg

            def lay1(x, lay):
                return x[bass.DynSlice(lay, 1)] if not isinstance(lay, int) else x[lay:lay + 1]

            def load(b, lay):
                s = slot(b)
                if b == "par":
                    for at, x in ((0, norm_mix), (8, norm_ffn), (16, hg_norm), (17, conv_b)):
                        n = x.shape[1] // P
                        ld(b, s[at:at + n, 0:P], lay1(x, lay).rearrange("o (k p) -> (o k) p", p=P))
                    ld(b, s[39:105, 0:P], lay1(conv_w, lay).rearrange("o w (k p) -> (o w k) p", p=P))
                    ld(b, s[0:32, P:2 * P], lay1(cmp_pe, lay).rearrange("o v (j a) d -> (o v j) (a d)", a=2))
                    ld(b, s[0:16, 256:256 + DFF], lay1(state_conv, lay).rearrange("o b w c -> (o b w) c"))
                elif b == "cmp":
                    v = s.rearrange("p (s c) -> p s c", s=NSEQ)
                    pool = cache_cmp.rearrange("l n (p a) v g d -> (l n) p (a v g d)", a=2)
                    for q in range(NSEQ):
                        for k in range(NPAGE):
                            row = page(q * NPAGE + k, lay)
                            ld(b, v[64 * k:64 * k + 64, q, :],
                               pool[bass.DynSlice(row, 1)].rearrange("o p c -> (o p) c"))
                elif b in ("kv0", "kv1"):
                    hb = int(b[2])
                    v = s.rearrange("p (w s c) -> p w s c", w=2, s=4)
                    pool = cache_slc.rearrange("l n (p a) v g d -> (l n) p (a v g d)", a=2)
                    win = cache_win.rearrange("l b (p a) v g d -> (l b) p (a v g d)", a=2)
                    for q in range(4):
                        for k in range(NPAGE):
                            row = page((4 * hb + q) * NPAGE + k, lay)
                            ld(b, v[64 * k:64 * k + 64, 0, q, :],
                               pool[bass.DynSlice(row, 1)].rearrange("o p c -> (o p) c"))
                        ld(b, v[:, 1, q, :],
                           win[bass.DynSlice(lay * NSEQ + 4 * hb + q, 1)].rearrange("o p c -> (o p) c"))
                elif b in ("st0", "st1"):
                    v = s[:, 0:4 * NSEQ * P // 2].rearrange("p (h b v) -> p h b v", h=2, b=NSEQ)
                    for h in range(2):
                        ld(b, v[:, h], lay1(state_hgrn, lay)[:, :, 2 * int(b[2]) + h].rearrange(
                            "o b p v -> p (o b) v"))
                elif b == "w_cmp":
                    for v in range(2):
                        ld(b, s[:, 1024 * v:1024 * (v + 1)].rearrange("p (j e) -> p j e", e=ND),
                           lay1(cmp_w1, lay)[:, v].rearrange("o (j a) d e -> (a d) (o j) e", a=2))
                        ld(b, s[64 * v:64 * v + 64, 2048:2048 + ND],
                           lay1(cmp_w2, lay)[:, v].rearrange("o e f -> (o e) f"))
                elif b in ("br0", "br1"):
                    c = 512 * int(b[2])
                    va, vb = (s[:, 2048 * n:2048 * (n + 1)].rearrange("p (k c) -> p k c", k=4) for n in range(2))
                    wb = lay1(w_branch, lay)[:, :, :, c:c + 512]
                    ld(b, va, wb[:, 0].rearrange("o (k p) c -> p (o k) c", p=P))
                    for g in range(KVH):
                        ld(b, vb[64 * g:64 * g + 64], wb[:, 1, 256 * g:256 * g + 256].rearrange(
                            "o (k p) c -> p (o k) c", p=ND))
                elif b.startswith("mg") or b.startswith("ff"):
                    n = int(b[2:])
                    v = s.rearrange("p (k c) -> p k c", k=KD)
                    w, a0, a1 = ((w_in, C_MG, C_MG + D) if b[0] == "m" else (w_gate_up, 0, DFF))
                    for h, a in enumerate((a0, a1)):
                        ld(b, v[:, :, 256 * h:256 * h + 256], lay1(w, lay)[:, :, a + 256 * n:a + 256 * n + 256]
                           .rearrange("o (k p) c -> p (o k) c", p=P))
                elif b.startswith("dn"):
                    mh, n = int(b[2]), int(b[4:])
                    k0, kn = sum(DOWN[mh][:n]), DOWN[mh][n]
                    ld(b, kt_of(b, kn, 512), lay1(w_down, lay)[:, k0 * P:(k0 + kn) * P, 512 * mh:512 * mh + 512]
                       .rearrange("o (k p) c -> p (o k) c", p=P))
                else:
                    w, c, n = {"w_kvc": (w_in, C_KC, 256), "w_kvn": (w_in, C_KS, 512), "w_nq": (w_in, C_NQ, 512),
                               "w_hf": (w_in, C_HF, 512), "w_hq": (w_in, C_HQ, 512), "w_hi": (w_in, C_HI, 512),
                               "w_hg": (w_in, C_HG, 512), "wo0": (w_out, 0, 512), "wo1": (w_out, 512, 512)}[b]
                    tot = 280 if b == "w_kvc" else n
                    v = kt_of(b, KD, tot)
                    ld(b, v[:, :, 0:n], lay1(w, lay)[:, :, c:c + n].rearrange("o (k p) c -> p (o k) c", p=P))
                    if b == "w_kvc":
                        ld(b, v[:, :, 256:280], lay1(w, lay)[:, :, C_GT:C_GT + 24].rearrange(
                            "o (k p) c -> p (o k) c", p=P))

            def store(out, in_, s=stored):
                sp.dma_start(out, in_).then_inc(s, 16)

            def flat3(x, lay):
                return lay1(x, lay).rearrange("o b s v g d -> (o b s) (v g d)")

            def stores_before(b, lay):
                if b == "w_nq":
                    for q in range(NSEQ):
                        sp.dma_start(lay1(win_s, lay)[:, q, 0:PAST - STEPS].rearrange(
                            "o (a t) v g d -> (o a) (t v g d)", a=8),
                            lay1(cache_win, lay)[:, q, STEPS:PAST].rearrange(
                                "o (a t) v g d -> (o a) (t v g d)", a=8)).then_inc(copied, 16)
                if b == "w_hi":
                    sp.wait_ge(mm_act, 3)
                    store(lay1(cmp_p, lay).rearrange("o b (p a) v g d -> (o b p) a (v g d)", a=2), ctok[:, 0:2, :],
                          kv_stored)
                    store(flat3(cmp_s, lay), ctok[0:SMP, 2, :], kv_stored)
                    sp.wait_ge(k_roped, 3)
                    for w, (op, os) in enumerate(((slc_p, slc_s), (win_p, None))):
                        store(lay1(op, lay).rearrange("o b (i p) v g d -> (o b p) i (v g d)", p=P),
                              stok[:, 0:2, 256 * w:256 * w + 256], kv_stored)
                        if os is not None:
                            store(flat3(os, lay), stok[0:SMP, 2, 256 * w:256 * w + 256], kv_stored)
                    store(lay1(win_s, lay)[:, :, PAST - STEPS:PAST].rearrange("o b s v g d -> (o b) s (v g d)"),
                          stok[0:SMP, 2, 256:512], kv_stored)
                if b == "dn1_0":
                    sp.wait_ge(cvo_ready, 6)
                    store(lay1(cv_p, lay).rearrange("o b w c -> (o b w) c"), cvo[0:2, :])
                    store(lay1(cv_s, lay).rearrange("o b w c -> (o b w) c"), cvo[2:18, :])
                if b == "st0":
                    sp.wait_ge(s_ready, 4)
                    store(lay1(hg_p, lay).rearrange("o b h p v -> p (o b h) v"), sP[:, 3])
                if b in ("st0", "st1"):
                    n = int(b[2])
                    v = slot(b)[:, 0:2048].rearrange("p (h b v) -> p h b v", h=2, b=NSEQ)
                    for h in range(2):
                        sp.wait_ge(sn_ready, 2 * n + h + 1)
                        store(lay1(hg_s, lay)[:, :, 2 * n + h].rearrange("o b p v -> p (o b) v"), v[:, h],
                              state_stored[n])
                    sp.wait_ge(state_stored[n], 32)

            sp.dma_start(cst_all[:, 0:NFIRST], consts[:, 0:NFIRST]).then_inc(first_consts_in, 16)
            sp.dma_start(xin[:, 0:2, :], x_prompt.rearrange("b (i p) c -> p (b i) c", p=P)).then_inc(xin_in, 16)
            sp.dma_start(xin[0:SMP, 2, :], x_sample.rearrange("b s c -> (b s) c")).then_inc(xin_in, 16)
            sp.dma_start(attb[0:8, 0:P], hg_lower.rearrange("l (h p) -> (l h) p", p=P)).then_inc(xin_in, 16)
            sp.dma_start(attb[8:16, 0:P], norm_final.rearrange("(k p) -> k p", p=P)).then_inc(xin_in, 16)
            sp.dma_start(pages[0:1, :], page_table.rearrange("b n -> (b n)").unsqueeze(0)).then_inc(consts_in, 16)
            assert BLOCKS[:NSLOT] == ["par", "cmp", "w_kvc", "w_kvn"]
            load("par", 0)
            load("w_kvc", 0)
            sp.dma_start(cst_all[:, NFIRST:], consts[:, NFIRST:]).then_inc(consts_in, 16)
            load("w_kvn", 0)
            sp.wait_ge(consts_in, 32)
            load("cmp", 0)

            def layer(lay, last):
                for n, b in enumerate(BLOCKS):
                    stores_before(b, lay)
                    if n + NSLOT < NBLK or not last:
                        if b == "cmp":
                            sp.wait_ge(rows_ready, NSEQ)
                        elif b in LAST_USE:
                            R = MM if LAST_USE[b] in MM.no else AXR
                            sp.wait_ge(*R.filled(LAST_USE[b]))
                        elif b.startswith("dn"):
                            sp.wait_ge(*unit_read(max(u for u in down_units if SPLIT[u][0] == b)))
                    if n == NBLK - 1:
                        sp.wait_ge(stored, 16 * NSTORE)
                        sp.sem_inc(arrived, 1)
                    if n + NSLOT < NBLK or not last:
                        load(BLOCKS[(n + NSLOT) % NBLK], lay + (n + NSLOT) // NBLK)
                sp.wait_ge(cleared, lay + 2)

            NSTORE = 1 + 2
            sp.wait_ge(cleared, 1)
            with sp.Fori(0, DEPTH - 1) as lay:
                layer(lay, False)
            layer(DEPTH - 1, True)
            sp.wait_ge(y_ready, 1)
            store(y_p.rearrange("b (i p) c -> p (b i) c", p=P), yout[:, 0:2, :])
            store(y_s.rearrange("b s c -> (b s) c"), yout[0:SMP, 2, :])
            sp.wait_ge(stored, 32)
            sp.wait_ge(copied, 16 * DEPTH * NSEQ)

        @block.tensor
        def _(pe):
            def begin(R, name):
                w = R.vacant(name)
                if w:
                    pe.wait_ge(*w)
                return R.bank(name)

            def mm(out, lhsT, rhs, start, stop):
                return nc.tensor.matmul(out, lhsT, rhs, start=start, stop=stop)

            def tr(out, in_):
                return nc.tensor.transpose(out, in_, ident[0:in_.shape[0], 0:in_.shape[0]])

            pe.wait_ge(first_consts_in, 16)
            pe.wait_ge(xin_in, 64)
            for k in range(KD + 1):
                if k >= 4:
                    pe.wait_ge(x_ready, k - 3)
                if k < KD:
                    for i in range(3):
                        last = tr(axb[k % 4][:, P * i:P * i + TM[i]], xin[0:TM[i], i, P * k:P * k + P])
                else:
                    last = tr(axb[k % 4][:, 0:16], attb[0:16, 0:P])
                last.then_inc(ax_full, 1)
            pe.wait_ge(x_ready, KD + 1)
            pe.wait_ge(consts_in, 32)
            depart(pe, 0)

            def norm(name, l_sq):
                bank = begin(AXR, name)
                for k in range(KD):
                    if k == 0:
                        pe.wait_ge(squares_dve, l_sq)
                    if k == 4:
                        pe.wait_ge(squares_act, l_sq)
                    last = mm(bank[:, 0:T], ones, sq[:, k, :], k == 0, k == KD - 1)
                last.then_inc(ax_full, 1)

            def feature_tile(name, w, cols, need_h=None):
                bank = begin(MM, name)
                for k in range(KD):
                    if need_h is not None:
                        pe.wait_ge(h_ready, need_h + k + 1)
                    last = mm(bank[:, 0:T], cols(w, k), hT[:, k, :], k == 0, k == KD - 1)
                last.then_inc(mm_full, 1)

            def square_sum(bank, k):
                pe.wait_ge(squares_x, k + 1)
                last = mm(bank[:, 0:T], ones, sq[:, k, :], k == 0, k == KD - 1)
                if k == KD - 1:
                    last.then_inc(ax_full, 1)

            def split_products(out, high, low, x_high, x_low, start, stop):
                mm(out, high, x_high, start, False)
                mm(out, high, x_low, False, False)
                return mm(out, low, x_high, False, stop)

            def split_tile(R, name, u, h, x_high, x_low, tile_ready=None):
                bank = begin(R, name)
                kn = SPLIT[u][2]
                for k in range(kn):
                    if tile_ready is not None:
                        pe.wait_ge(tile_ready[0], tile_ready[1] + k + 1)
                    last = split_products(bank[:, 0:T], unit_high(u)[:, k, h, :], unit_of(u, ring_r)[:, k, h, :],
                                          x_high[:, k, :], x_low[:, k, :], k == 0, k == kn - 1)
                last.then_inc(R.full, 1)

            def plain(w, c0):
                return lambda v, k: v[:, k, c0:c0 + P]

            def hgrn_values(i, l):
                if i == 0:
                    pe.wait_ge(*landed_at("w_hi", l))
                w = kt_of("w_hi", KD, 512)
                bank = begin(MM, f"hi{i}")
                for k in range(KD):
                    last = mm(bank[0:TM[i], :], hT[:, k, P * i:P * i + TM[i]], w[:, k, :], k == 0, k == KD - 1)
                last.then_inc(mm_full, 1)

            def out_gate(h, l):
                if h == 0:
                    pe.wait_ge(*landed_at("w_hg", l))
                w = kt_of("w_hg", KD, 512)
                feature_tile(f"hg{h}", w, plain(w, P * h))

            def split_gates(m):
                u = m - 4 if m < 6 else m - 2
                pe.wait_ge(w_low, u + 1)
                for y in range(2):
                    split_tile(MM, f"mg{'ab'[y]}{m}", u, y, h_high, h_low)

            def merge_gate(m, y, l):
                mg = f"mg{m // 2}"
                if m % 2 == 0 and y == 0:
                    pe.wait_ge(*landed_at(mg, l))
                w = kt_of(mg, KD, 512)
                feature_tile(f"mg{'ab'[y]}{m}", w, plain(w, 256 * y + P * (m % 2)))

            def level(kk):
                m = LEVELS[kk]
                pe.wait_ge(ql_ready, kk + 1)
                pe.wait_ge(kl_ready, kk + 1)
                qs, ks = (qH, kH) if m == 0 else (qL, kL)
                if m == 1:
                    ks = kH
                bank = begin(AXR, f"lv{kk}")
                for h in range(HH):
                    for c in range(4):
                        at = (c // 2) * 256 + h * S1
                        last = mm(bank[64 * (c % 2):64 * (c % 2) + 64, at:at + S1], ks[:, h, S1 * c:S1 * c + S1],
                                  qs[:, h, S1 * c:S1 * c + S1], True, True)
                last.then_inc(ax_full, 1)
                if m < STEPS:
                    bank = begin(AXR, f"lvs{kk}")
                    for h in range(HH):
                        last = mm(bank[0:64, h * S1:h * S1 + S1], ks[:, h, SEQ:T], qs[:, h, SEQ:T], True, True)
                    last.then_inc(ax_full, 1)

            def scores(n):
                i, g = UNITS[n]
                gs = slice(64 * g, 64 * g + 64)
                nk = P * (i + 1)
                for r in range(GRP):
                    bank = begin(AXR, f"sc{n}_{r}")
                    for w in range(2):
                        last = mm(bank[:, 256 * w:256 * w + nk], qT[gs, r, P * i:P * i + P], ktn[gs, w, 0:nk], True,
                                  True)
                    last.then_inc(ax_full, 1)
                bank = begin(AXR, f"scc{n}")
                for r in range(GRP):
                    last = mm(bank[:, NCB * r:NCB * r + NCB], qT[gs, r, P * i:P * i + P], kcT[gs, NSEQ, :], True, True)
                last.then_inc(ax_full, 1)

            def values(n):
                i, g = UNITS[n]
                prob, pcs = probs[n % 2], pcb[n % 2]
                pe.wait_ge(scaled, n + 1)
                for x in range(2 * (i + 1)):
                    w, kt = x % 2, x // 2
                    bank = begin(AXR, f"tp{n}_{x}")
                    for r in range(GRP):
                        last = tr(bank[:, P * r:P * r + P], prob[:, r, w, P * kt:P * kt + P])
                    last.then_inc(ax_full, 1)
                bank = begin(AXR, f"tpc{n}")
                for r in range(GRP):
                    last = tr(bank[0:NCB, P * r:P * r + P], pcs[:, NCB * r:NCB * r + NCB])
                last.then_inc(ax_full, 1)
                bank = begin(AXR, f"ov{n}")
                out = bank[64 * g:64 * g + 64, :]
                pe.wait_ge(*AXR.emptied_at(f"tpc{n}"))
                pe.wait_ge(*AXR.emptied_at(f"tp{n}_{2 * i + 1}"))
                mm(out, vc[0:NCB, NSEQ, g, :], probTc[0:NCB, :], True, False)
                for x in range(2 * (i + 1)):
                    w, kt = x % 2, x // 2
                    last = mm(out, stok[:, kt, 256 * w + P + 64 * g:256 * w + P + 64 * g + 64], probT[:, x, :], False,
                              x == 2 * i + 1)
                last.then_inc(ax_full, 1)

            def sample_scores(n, hb, g):
                gs = slice(64 * g, 64 * g + 64)
                bank = begin(AXR, f"ssa{n}")
                for w in range(2):
                    for b in range(4):
                        last = mm(bank[32 * b:32 * b + 32, 256 * w:256 * w + 256],
                                  qS[gs, 4 * hb + b].rearrange("p r s -> p (r s)"), kvT[gs, w, b, :], True, True)
                last.then_inc(ax_full, 1)
                bank = begin(AXR, f"ssb{n}")
                q4 = qS[gs, 4 * hb:4 * hb + 4].rearrange("p b r s -> p (b r s)")
                for w in range(2):
                    mm(bank[:, SMP * w:SMP * w + SMP], q4, ktn[gs, w, SEQ:T], True, True)
                for b in range(4):
                    last = mm(bank[32 * b:32 * b + 32, P:P + NCB], qS[gs, 4 * hb + b].rearrange("p r s -> p (r s)"),
                              kcT[gs, 4 * hb + b, :], True, True)
                last.then_inc(ax_full, 1)

            def sample_values(n, hb, g):
                pe.wait_ge(scaled, n + 1)
                bank = begin(AXR, f"tps{n}")
                for x in range(4):
                    w, kt = x // 2, x % 2
                    last = tr(bank[:, P * x:P * x + P], sprob[:, w, P * kt:P * kt + P])
                last.then_inc(ax_full, 1)
                bank = begin(AXR, f"tpn{n}")
                for w in range(2):
                    tr(bank[0:SMP, P * w:P * w + P], snew[:, w, :])
                tr(bank[0:NCB, 2 * P:3 * P], pcs[:, 0:NCB]).then_inc(ax_full, 1)
                bank = begin(AXR, f"ov{n}")
                pe.wait_ge(*AXR.emptied_at(f"tps{n}"))
                pe.wait_ge(*AXR.emptied_at(f"tpn{n}"))
                kv = slot(f"kv{hb}").rearrange("p (w s a v g d) -> p w s a v g d", w=2, s=4, a=2, v=2, g=2)
                for b in range(4):
                    out = bank[64 * g:64 * g + 64, 32 * b:32 * b + 32]
                    cs = slice(32 * b, 32 * b + 32)
                    mm(out, vc[0:NCB, 4 * hb + b, g, :], snewT[0:NCB, 2, cs], True, False)
                    for w in range(2):
                        mm(out, stok[0:SMP, 2, 256 * w + P + 64 * g:256 * w + P + 64 * g + 64], snewT[0:SMP, w, cs],
                           False, False)
                    for x in range(4):
                        last = mm(out, kv[:, x // 2, b, x % 2, 1, g, :], sprobT[:, x, cs], False, x == 3)
                last.then_inc(ax_full, 1)

            def layer(l):
                pe.wait_ge(*landed_at("par", l))
                s = slot("par")
                bank = begin(AXR, "par")
                tr(bank[:, 0:105], s[0:105, 0:P])
                tr(bank[:, P:P + 32], s[0:32, P:2 * P]).then_inc(ax_full, 1)
                norm("norm1", 1)
                bank = begin(AXR, "cst")
                for j in range(NJ):
                    last = tr(bank[:, 16 * j:16 * j + 16], s[0:16, 256 + P * j:256 + P * j + P])
                last.then_inc(ax_full, 1)
                pe.wait_ge(*landed_at("w_kvc", l))
                w = kt_of("w_kvc", KD, 280)
                for i in range(3):
                    bank = begin(MM, f"kvc{i}")
                    for k in range(KD):
                        if i == 0:
                            pe.wait_ge(h_ready, k + 1)
                        lhs = hT[:, k, i:SEQ:2] if i < 2 else hT[:, k, SEQ:T]
                        n = 256 if i < 2 else 280
                        last = mm(bank[0:TM[i], 0:n], lhs, w[:, k, 0:n], k == 0, k == KD - 1)
                    for k in range(KD if i < 2 else 0):
                        last = mm(bank[0:TM[i], 256:280], hT[:, k, P * i:P * i + TM[i]], w[:, k, 256:280], k == 0,
                                  k == KD - 1)
                    last.then_inc(mm_full, 1)
                pe.wait_ge(*landed_at("w_kvn", l))
                w = kt_of("w_kvn", KD, 512)
                for i in range(3):
                    bank = begin(MM, f"kvn{i}")
                    for k in range(KD):
                        last = mm(bank[0:TM[i], :], hT[:, k, P * i:P * i + TM[i]], w[:, k, :], k == 0, k == KD - 1)
                    last.then_inc(mm_full, 1)
                for q in range(NSEQ):
                    bank = begin(AXR, f"cc{q}")
                    pe.wait_ge(rows_ready, q + 1)
                    for x in range(4):
                        last = tr(bank[:, P * x:P * x + P], craw[:, q, P * x:P * x + P])
                    last.then_inc(ax_full, 1)
                bank = begin(AXR, "cp")
                pe.wait_ge(rows_ready, NCS)
                for x in range(4):
                    last = tr(bank[:, P * x:P * x + P], craw[:, NSEQ, P * x:P * x + P])
                last.then_inc(ax_full, 1)
                pe.wait_ge(*landed_at("w_nq", l))
                w = kt_of("w_nq", KD, 512)
                for m in range(4):
                    bank = begin(MM, f"nq{m}")
                    for k in range(KD):
                        for g in range(KVH):
                            last = mm(bank[64 * g:64 * g + 64, 0:T], w[:, k, 256 * g + 64 * m:256 * g + 64 * m + 64],
                                      hT[:, k, :], k == 0, k == KD - 1)
                    last.then_inc(mm_full, 1)
                pe.wait_ge(*landed_at("w_hf", l))
                w = kt_of("w_hf", KD, 512)
                feature_tile("hf0", w, plain(w, 0))
                for x in range(2):
                    bank = begin(AXR, f"kt{x}")
                    if x == 0:
                        pe.wait_ge(k_roped, 3)
                    for i in range(3):
                        last = tr(bank[:, P * i:P * i + TM[i]], stok[0:TM[i], i, 256 * x:256 * x + P])
                    last.then_inc(ax_full, 1)
                for h in range(1, HH):
                    feature_tile(f"hf{h}", w, plain(w, P * h))
                for m in range(4):
                    bank = begin(AXR, f"nqr{m}")
                    pe.wait_ge(qraw_ready, m + 1)
                    mm(bank[:, 0:T], con("perm"), qraw[:, m, :], True, True).then_inc(ax_full, 1)
                pe.wait_ge(*landed_at("w_hq", l))
                w = kt_of("w_hq", KD, 512)
                for h in range(HH):
                    feature_tile(f"hq{h}", w, plain(w, P * h))
                pe.wait_ge(*landed_at("w_cmp", l))
                w1 = slot("w_cmp")[:, 0:2048].rearrange("p (v j e) -> p v j e", v=2, e=ND)
                banks = [begin(AXR, "hidk"), begin(AXR, "hidv")]
                pe.wait_ge(prm_ready, 1)
                pe.wait_ge(*AXR.emptied_at(f"cc{NSEQ - 1}"))
                pe.wait_ge(*AXR.emptied_at("cp"))
                for j in range(16):
                    for v in range(2):
                        mm(banks[v][64 * v:64 * v + 64, 300:301], w1[:, v, j, :],
                           prm[:, P + 16 * v + j:P + 16 * v + j + 1], j == 0, j == 15)
                for j in range(16):
                    for v in range(2):
                        rows = cmpT[:, v].rearrange("p g s t -> p (g s) t")[:, :, j:j + 8 * NCB - 7:8]
                        last = mm(banks[v][64 * v:64 * v + 64, 0:2 * NCS * NCB], w1[:, v, j, :], rows, j == 0, j == 15)
                        if j == 15:
                            last.then_inc(ax_full, 1)
                hgrn_values(0, l)
                bank = begin(AXR, "kcm")
                pe.wait_ge(hid_ready, 2)
                w2 = slot("w_cmp")
                for g in range(KVH):
                    last = mm(bank[64 * g:64 * g + 64, 0:NCS * NCB], w2[0:64, 2048:2048 + ND],
                              hid[0:64, g].rearrange("p s n -> p (s n)"), True, True)
                last.then_inc(ax_full, 1)
                bank = begin(AXR, "kcr")
                pe.wait_ge(kraw_ready, 1)
                mm(bank[:, 0:NCS * NCB], con("perm"), kraw.rearrange("p s n -> p (s n)"), True, True).then_inc(
                    ax_full, 1)
                for n in range(3):
                    bank = begin(AXR, f"vc{n}")
                    for y in range(6):
                        q, g = (6 * n + y) // 2, (6 * n + y) % 2
                        last = mm(bank[0:NCB, ND * y:ND * y + ND], hid[64:128, g, q, :], w2[64:128, 2048:2048 + ND], True,
                                  True)
                    last.then_inc(ax_full, 1)
                for n in range(4):
                    level(2 * n)
                    if n == 0:
                        pe.wait_ge(q_ready, 4)
                        pe.wait_ge(*AXR.emptied_at("kt1"))
                        pe.wait_ge(*AXR.emptied_at("vc2"))
                        pe.wait_ge(kc_ready, 1)
                    scores(n)
                    if n == 0:
                        hgrn_values(1, l)
                    else:
                        values(n - 1)
                    if n in (1, 2):
                        out_gate(2 * n - 2, l)
                    if 2 * n + 1 < len(LEVELS):
                        level(2 * n + 1)
                    if n == 0:
                        for hb in range(2):
                            bank = begin(AXR, f"gsel{hb}")
                            mm(bank[:, 0:24], con("sel", SMP)[:, P * hb:P * hb + P], gts[0:SMP, 2, :], True,
                               True).then_inc(ax_full, 1)
                        hgrn_values(2, l)
                    if n in (1, 2):
                        out_gate(2 * n - 1, l)
                pe.wait_ge(kl_ready, len(LEVELS) + 1)
                for h in range(HH):
                    bank = begin(AXR, f"krt{h}")
                    for i in range(3):
                        last = tr(bank[0:TM[i], P * i:P * i + P], kL[:, h, P * i:P * i + TM[i]])
                    last.then_inc(ax_full, 1)
                pe.wait_ge(qs_ready, 1)
                for hb in range(2):
                    pe.wait_ge(*landed_at(f"kv{hb}", l))
                    kv = slot(f"kv{hb}").rearrange("p (w s a c) -> p w s a c", w=2, s=4, a=2)
                    for x in range(4):
                        w, bp = x // 2, x % 2
                        bank = begin(AXR, f"skt{hb}_{x}")
                        for y in range(4):
                            last = tr(bank[:, P * y:P * y + P], kv[:, w, 2 * bp + y // 2, y % 2, 0:P])
                        last.then_inc(ax_full, 1)
                    if hb == 0:
                        merge_gate(0, 0, l)
                        values(3)
                    for c in (2 * hb, 2 * hb + 1):
                        bank = begin(AXR, f"ds{c}")
                        if c == 0:
                            pe.wait_ge(*AXR.emptied_at("krt3"))
                            pe.wait_ge(*AXR.emptied_at("krt2"))
                        rows = slice(64 * (c % 2), 64 * (c % 2) + 64)
                        for h in range(HH):
                            last = mm(bank[:, P * h:P * h + P], krP[rows, h, c // 2, :],
                                      vH[rows, c // 2, P * h:P * h + P], True, True)
                        last.then_inc(ax_full, 1)
                    pe.wait_ge(*AXR.emptied_at(f"skt{hb}_3"))
                    pe.wait_ge(*AXR.emptied_at(f"skt{hb}_2"))
                    for g in range(KVH):
                        n = 4 + 2 * hb + g
                        sample_scores(n, hb, g)
                        merge_gate(2 * hb + g, 1, l)
                        if n < 7:
                            merge_gate(2 * hb + g + 1, 0, l)
                        sample_values(n, hb, g)
                pe.wait_ge(s_ready, 3)
                pe.wait_ge(ql_ready, len(LEVELS) + 1)
                for h in range(HH):
                    if h % 2 == 0:
                        pe.wait_ge(*landed_at(f"st{h // 2}", l))
                    s0 = slot(f"st{h // 2}")[:, 0:2048].rearrange("p (h b v) -> p h b v", h=2, b=NSEQ)
                    for c in (0, 2, 4, 1, 3):
                        if c < 2:
                            bank = begin(AXR, ("o", "oo")[c] + str(h))
                        rows = slice(64 * (c % 2), 64 * (c % 2) + 64)
                        cols = slice(S1 * c, S1 * c + S1)
                        last = mm(bank[:, cols], vH[rows, c // 2, P * h:P * h + P], acc[rows, c // 2, h, :], True, c == 0)
                        if 1 <= c <= 3:
                            last = mm(bank[:, cols], sP[:, c - 1, h, :], qL[:, h, cols], False, True)
                        for b in range(NSEQ if c == 4 else 0):
                            cols = slice(SEQ + STEPS * b, SEQ + STEPS * (b + 1))
                            last = mm(bank[:, cols], s0[:, h % 2, b, :], qL[:, h, cols], False, b == NSEQ - 1)
                        if c >= 3:
                            last.then_inc(ax_full, 1)
                    pe.wait_ge(vx_ready, h + 1)
                    for y, name in enumerate((f"dsa{h}", f"dsb{h}")):
                        bank = begin(AXR, name)
                        mm(bank[:, :], krS[0:SMP, h, :], vX[0:SMP, 4 * y:4 * y + 4, :].rearrange("p b v -> p (b v)"),
                           True, True).then_inc(ax_full, 1)
                pe.wait_ge(h_lo, 1)
                split_gates(4)
                for h in range(HH):
                    bank = begin(AXR, f"on{h}")
                    pe.wait_ge(sqo_ready, h + 1)
                    mm(bank[:, 0:T], ones, sqH[:, h, :], True, True).then_inc(ax_full, 1)
                split_gates(5)
                for n in range(2):
                    for y, src, low in ((1, oN_high, oN_low), (0, oH_high, oH_low)):
                        u = 4 * n + 3 - y
                        pe.wait_ge(w_low, u + 1)
                        if n == 0:
                            pe.wait_ge(on_ready if y else oh_ready, 1)
                        for m in range(4):
                            split_tile(AXR, f"br{'ab'[y]}{4 * n + m}", u, m, src, low)
                    if n == 0:
                        split_gates(6)
                        split_gates(7)
                for m in range(KD):
                    u = 8 + m // 2
                    pe.wait_ge(w_low, u + 1)
                    split_tile(MM, f"wo{m}", u, m % 2, m_high, m_low, (m_lo, 0) if m == 0 else None)
                    if m == 2:
                        bank = begin(AXR, "norm2")
                    if m >= 2:
                        square_sum(bank, m - 2)
                for k in (KD - 2, KD - 1):
                    square_sum(bank, k)
                for j in range(NJ):
                    u = FFU + j
                    pe.wait_ge(w_low, u + 1)
                    split_tile(MM, f"g{j}", u, 0, h_high, h_low, (h_lo, 1) if j == 0 else None)
                    split_tile(MM, f"u{j}", u, 1, h_high, h_low)
                for u in down_units:
                    b, a, kn = SPLIT[u]
                    mh, n = int(b[2]), int(b[4:])
                    R = (MM, AXR)[mh]
                    if u == DNU + 2:
                        pe.wait_ge(glast_ready, 1)
                        for c in range(6):
                            bank = begin(AXR, f"cv{c}")
                            for y in range(4 if c < 5 else 2):
                                last = tr(bank[0:18, P * y:P * y + P], glast[:, 4 * c + y, :])
                            last.then_inc(ax_full, 1)
                    pe.wait_ge(w_low, u + 1)
                    for kk in range(kn):
                        k = sum(DOWN[mh][:n]) + a + kk
                        for m in range(4):
                            bank = begin(R, f"dn{mh}_{m}") if k == 0 else R.bank(f"dn{mh}_{m}")
                            if mh == 0 and m == 0:
                                pe.wait_ge(act_ready, k + 1)
                            last = split_products(bank[:, 0:T], unit_high(u)[:, kk, m, :],
                                                  unit_of(u, ring_r)[:, kk, m, :],
                                                  act_high[:, k, :], act_low[:, k, :], k == 0, k == NJ - 1)
                            if k == NJ - 1:
                                last.then_inc(R.full, 1)
                    if u in down_inner:
                        last.then_inc(down_read, 1)
                pe.wait_ge(x_ready, 2 * KD)

            with pe.Fori(0, DEPTH) as l:
                layer(l)
                depart(pe, l + 1)
            for k in range(KD):
                if k == 0:
                    pe.wait_ge(squares_dve, 1)
                if k == 4:
                    pe.wait_ge(squares_act, 1)
                last = mm(axb[0][:, 0:T], ones, sq[:, k, :], k == 0, k == KD - 1)
            last.then_inc(ax_full, 1)
            n = 0
            for k0 in range(0, KD, 4):
                for i in range(3):
                    if n >= 4:
                        pe.wait_ge(mm_dve, n - 3)
                    for k in range(k0, k0 + 4):
                        if i == 0:
                            pe.wait_ge(h_ready, k + 1)
                        last = tr(mmb[n % 4][0:TM[i], P * (k - k0):P * (k - k0) + P], hT[:, k, P * i:P * i + TM[i]])
                    last.then_inc(mm_full, 1)
                    n += 1

        @block.scalar
        def _(sc):
            def A(out, in_, f, **kw):
                return nc.scalar.activation(out, in_, f, **kw)

            sc.wait_ge(mul_ready, 1)
            A(lbs[:, 12:20], lbs[:, 12:20], ACT.Exp).then_inc(exp_ready, 1)
            sc.wait_ge(exp_ready, 1)
            depart(sc, 0)

            def norm(st, bank, squares=True):
                if squares:
                    A(sq[:, 4:8, :], xT[:, 4:8, :], ACT.Square).then_inc(*st.up(squares_act))
                sc.wait_ge(*bank[1])
                A(rs[:, 0:T], bank[0][:, 0:T], ACT.Ln, bias=epsb[:, 0:1], scale=1.0 / D).then_inc(*st.up(ax_act))
                sc.wait_ge(*st.settled())
                A(rs[:, 0:T], rs[:, 0:T], ACT.Exp, scale=-0.5).then_inc(*st.up(rs_ready))

            def layer(l):
                st = Steps(sc)
                AB, MB = AXR.bank, MM.bank

                def take(R, name):
                    sc.wait_ge(*R.filled(name))
                    return R.bank(name)

                norm(st, (AB("norm1"), AXR.filled("norm1")))
                for i in range(3):
                    bank = take(MM, f"kvc{i}")
                    A(gts[0:TM[i], i, :], bank[0:TM[i], 256:280], ACT.Sigmoid)
                    A(ctok[0:TM[i], i, :], bank[0:TM[i], 0:256], ACT.Copy).then_inc(*st.up(mm_act))
                for i in range(3):
                    bank = take(MM, f"kvn{i}")
                    A(stok[0:TM[i], i, :], bank[0:TM[i], :], ACT.Copy).then_inc(*st.up(mm_act))
                for q in range(0, NSEQ, 2):
                    bank = take(AXR, f"cc{q}")
                    A(cmpT[:, :, :, q, :].rearrange("p v g t -> p (v g) t"),
                      bank[:, :].rearrange("p (x t) -> p x t", x=4), ACT.Copy).then_inc(*st.up(ax_act))
                bank = take(AXR, "cp")
                A(cmpT[:, :, :, NSEQ, :].rearrange("p v g t -> p (v g) t"), bank[:, :].rearrange("p (x t) -> p x t", x=4),
                  ACT.Copy).then_inc(*st.up(ax_act))
                for m in range(4):
                    bank = take(MM, f"nq{m}")
                    A(qraw[:, m, :], bank[:, 0:T], ACT.Copy).then_inc(*st.up(qraw_ready))
                    sc.wait_ge(*st.settled())
                    sc.sem_inc(*st.up(mm_act))
                for h in range(HH):
                    bank = take(MM, f"hf{h}")
                    A(pH[:, h, :], bank[:, 0:T], ACT.Sigmoid).then_inc(*st.up(sig_ready))
                    A(kH[:, h, :], bank[:, 0:T], ACT.Sigmoid, scale=-1.0).then_inc(*st.up(mm_act))
                    if h == 0:
                        bank = take(AXR, "kt0")
                        A(ktn[:, 0, :], bank[:, 0:T], ACT.Copy).then_inc(*st.up(ax_act))
                for h in range(HH):
                    bank = take(MM, f"hq{h}")
                    A(sgq[:, h, :], bank[:, 0:T], ACT.Sigmoid).then_inc(*st.up(sig_ready))
                take(AXR, "hidk")
                bank = take(AXR, "hidv")
                for v, name in enumerate(("hidk", "hidv")):
                    rows = slice(64 * v, 64 * v + 64)
                    A(hbias[rows, 0:1], AB(name)[rows, 300:301], ACT.Copy).then_inc(*st.up(act_step))
                sc.wait_ge(*st.settled())
                for v, name in enumerate(("hidk", "hidv")):
                    rows = slice(64 * v, 64 * v + 64)
                    A(hid[rows].rearrange("p g s n -> p (g s n)"), AB(name)[rows, 0:2 * NCS * NCB],
                      ACT.Gelu_apprx_tanh, bias=hbias[rows, 0:1]).then_inc(*st.up(hid_ready))
                sc.wait_ge(*st.settled())
                sc.sem_inc(ax_act, 2)
                st.count[ax_act.name] += 2
                def hgrn_values(i):
                    bank = take(MM, f"hi{i}")
                    A(vH[0:TM[i], i, :], bank[0:TM[i], :], ACT.Copy).then_inc(*st.up(mm_act))

                def out_gate(h):
                    bank = take(MM, f"hg{h}")
                    A(gH[:, h, :], bank[:, 0:T], ACT.Sigmoid).then_inc(*st.up(sig_ready))

                def merge_gate(m, y):
                    bank = take(MM, f"mg{'ab'[y]}{m}")
                    if m >= MGB and y:
                        sc.wait_ge(merged_ready, m - MGB + 1)
                    A(mgs[:, m % MGB, :] if y else merged[:, m, :], bank[:, 0:T], ACT.Sigmoid).then_inc(*st.up(mm_act))

                def merge_gates(m):
                    merge_gate(m, 0)
                    merge_gate(m, 1)

                hgrn_values(0)
                bank = take(AXR, "kcm")
                A(kraw.rearrange("p s n -> p (s n)"), bank[:, 0:NCS * NCB], ACT.Copy).then_inc(*st.up(kraw_ready))
                sc.wait_ge(*st.settled())
                sc.sem_inc(*st.up(ax_act))
                for n in range(3):
                    bank = take(AXR, f"vc{n}")
                    A(vc[0:NCB, 3 * n:3 * n + 3].rearrange("p s g d -> p (s g d)"), bank[0:NCB, 0:6 * ND],
                      ACT.Copy).then_inc(*st.up(ax_act))
                def turned(n):
                    for x in range(0, 2 * (UNITS[n][0] + 1), 2):
                        bank = take(AXR, f"tp{n}_{x}")
                        A(probT[:, x, :], bank[:, :], ACT.Copy).then_inc(*st.up(ax_act))
                    bank = take(AXR, f"tpc{n}")
                    A(probTc[0:NCB, :], bank[0:NCB, :], ACT.Copy).then_inc(*st.up(ax_act))

                for n, (i, g) in enumerate(UNITS):
                    nk = P * (i + 1)
                    prob, pcs, nm, sm = probs[n % 2], pcb[n % 2], nmb[n % 2], smb[n % 2]
                    if n:
                        turned(n - 1)
                    sc.wait_ge(max_ready, n + 1)
                    A(pcs[:, 0:60], pcs[:, 0:60], ACT.Exp, scale=SCALE)
                    for r in range(GRP):
                        for w in range(2):
                            c = 4 * (w + 1) + r
                            last = A(prob[:, r, w, 0:nk], prob[:, r, w, 0:nk], ACT.Exp, bias=nm[:, c:c + 1],
                                     scale=SCALE, accum_out=sm[:, c:c + 1])
                    last.then_inc(*st.up(exp_ready))
                    if n == 0:
                        hgrn_values(1)
                        hgrn_values(2)
                    else:
                        for h in ((0, 1), (2, 3), ())[n - 1]:
                            out_gate(h)
                sc.wait_ge(ql_ready, len(LEVELS) + 1)
                for h in (0, 2):
                    bank = take(AXR, f"krt{h}")
                    A(krP[:, h].rearrange("p i d -> p (i d)"), bank[:, 0:256], ACT.Copy)
                    A(krS[0:SMP, h, :], bank[0:SMP, 256:384], ACT.Copy).then_inc(*st.up(ax_act))
                for hb in range(2):
                    for x in (0, 2):
                        bank = take(AXR, f"skt{hb}_{x}")
                        A(kvT[:, x // 2, 2 * (x % 2):2 * (x % 2) + 2, :].rearrange("p b t -> p (b t)"), bank[:, :],
                          ACT.Copy).then_inc(*st.up(ax_act))
                    if hb == 0:
                        merge_gate(0, 0)
                        turned(3)
                    pcs, nm, sm = pcb[0], nmb[0], smb[0]
                    for g in range(KVH):
                        n = 4 + 2 * hb + g
                        sc.wait_ge(max_ready, n + 1)
                        A(pcs[:, 0:NCB], AB(f"ssb{n}")[:, P:P + NCB], ACT.Exp, bias=nm[:, 0:1], scale=SCALE,
                          accum_out=sm[:, 0:1])
                        for w in range(2):
                            A(snew[:, w, :], snew[:, w, :], ACT.Exp, bias=nm[:, w + 1:w + 2], scale=SCALE,
                              accum_out=sm[:, w + 3:w + 4])
                        for w in range(2):
                            last = A(sprob[:, w, :], AB(f"ssa{n}")[:, 256 * w:256 * w + 256], ACT.Exp,
                                     bias=nm[:, w + 1:w + 2], scale=SCALE, accum_out=sm[:, w + 1:w + 2])
                        last.then_inc(*st.up(exp_ready))
                        sc.wait_ge(*st.settled())
                        sc.sem_inc(ax_act, 2)
                        st.count[ax_act.name] += 2
                        merge_gate(2 * hb + g, 1)
                        if n < 7:
                            merge_gate(2 * hb + g + 1, 0)
                        bank = take(AXR, f"tpn{n}")
                        A(snewT[0:SMP, 0:2, :].rearrange("p x c -> p (x c)"), bank[0:SMP, 0:256], ACT.Copy)
                        A(snewT[0:NCB, 2, :], bank[0:NCB, 256:384], ACT.Copy).then_inc(*st.up(ax_act))
                def split(u):
                    if u == 0 or SPLIT[u][0] != SPLIT[u - 1][0]:
                        sc.wait_ge(*landed_at(SPLIT[u][0], l))
                        sc.sem_inc(spare, 1)
                    if u >= 2:
                        sc.wait_ge(*unit_read(u - 2))
                    A(unit_high(u), unit_of(u, ring), ACT.Copy).then_inc(*st.up(w_high))

                sc.wait_ge(*AXR.filled("ov7"))
                sc.wait_ge(kv_stored, 16 * 6)
                A(h_high, hT, ACT.Copy).then_inc(*st.up(h_hi))
                split(0)
                split(1)
                sc.wait_ge(kl_ready, len(LEVELS) + 1)
                for h in range(HH):
                    sc.wait_ge(*AXR.emptied_at(f"oo{h}"))
                    A(sqH[:, h, :], oS[:, h, :], ACT.Square).then_inc(*st.up(sqo_ready))
                sc.wait_ge(*AXR.filled(f"dsb{HH - 1}"))
                A(oN_high, oN, ACT.Copy).then_inc(*st.up(on_hi))
                merge_gates(4)
                for h in range(HH):
                    bank = take(AXR, f"on{h}")
                    A(rsH[:, h, :], bank[:, 0:T], ACT.Ln, bias=epsb[:, 0:1], scale=1.0 / HD).then_inc(*st.up(ax_act))
                sc.wait_ge(*st.settled())
                A(rsH[:, :, :], rsH[:, :, :], ACT.Exp, scale=-0.5).then_inc(*st.up(rso_ready))
                split(2)
                sc.wait_ge(oh_raw, 1)
                A(oH_high, oH, ACT.Copy).then_inc(*st.up(oh_hi))
                merge_gates(5)

                def merged_high(n):
                    for m in range(4 * n, 4 * n + 4):
                        sc.wait_ge(merged_ready, m + 1)
                        A(m_high[:, m, :], merged[:, m, :], ACT.Copy).then_inc(*st.up(m_hi))

                split(3)
                split(4)
                split(5)
                merged_high(0)
                merge_gates(6)
                split(6)
                merge_gates(7)
                split(7)
                split(8)
                merged_high(1)
                split(9)
                for m in range(KD):
                    sc.wait_ge(x_ready, m + 1)
                    A(sq[:, m, :], xT[:, m, :], ACT.Square).then_inc(*st.up(squares_x))
                    if m in (1, 3, 5):
                        split(10 + m // 2)
                norm(st, (AB("norm2"), AXR.filled("norm2")), False)
                for k in range(KD):
                    sc.wait_ge(h_ready, KD + k + 1)
                    A(h_high[:, k, :], hT[:, k, :], ACT.Copy).then_inc(*st.up(h_hi))
                split(FFU + 1)
                for j in range(NJ):
                    if j:
                        split(FFU + j + 1)
                    bank = take(MM, f"g{j}")
                    gx, cv = gext[j % 2], cvt[j % 2]
                    if j == 0:
                        sc.wait_ge(pre_ready, 1)
                    if j >= 2:
                        sc.wait_ge(conv_ready, j - 1)
                        sc.wait_ge(pre_ready, j + 1)
                        sc.wait_ge(act_ready, j - 1)
                    A(gx[:, 2:2 + SEQ], bank[:, 0:SEQ], ACT.Copy)
                    A(gx[:, 2 + SEQ:GX].rearrange("p (b s) -> p b s", b=NSEQ)[:, :, 2:2 + STEPS],
                      bank[:, SEQ:T].rearrange("p (b s) -> p b s", b=NSEQ), ACT.Copy)
                    A(cv, bank[:, 0:T], ACT.Identity, bias=prm[:, 17 + j:18 + j],
                      scale=prm[:, 39 + 2 * NJ + j:40 + 2 * NJ + j]).then_inc(*st.up(mm_act))
                    sc.wait_ge(conv_ready, j + 1)
                    A(cv, cv, ACT.Gelu_apprx_tanh).then_inc(*st.up(gelu_ready))
                for u in range(DNU + 1, len(SPLIT)):
                    split(u)
                sc.wait_ge(*st.settled())

            with sc.Fori(0, DEPTH) as l:
                layer(l)
                depart(sc, l + 1)
            norm(Steps(sc), (axb[0], (ax_full, 1)))

        @block.vector
        def _(ve):
            V = nc.vector

            st = Steps(ve)
            V.memset(epsb[:, :], EPS)
            for k in range(KD + 1):
                ve.wait_ge(ax_full, k + 1)
                if k < KD:
                    V.tensor_copy(xT[:, k, :], axb[k % 4][:, 0:T]).then_inc(*st.up(x_ready))
                else:
                    V.tensor_copy(pro[:, :], axb[k % 4][:, 0:16]).then_inc(*st.up(x_ready))
            ve.wait_ge(*st.settled())

            def link(ins):
                ins.then_inc(*st.up(dve_step))
                ve.wait_ge(*st.settled())

            big = lbs[:, 0:4]
            link(V.tensor_tensor(big, pro[:, 0:4], pro[:, 4:8], ALU.max))
            link(V.tensor_tensor(lbs[:, 4:12].rearrange("p (l h) -> p l h", l=2),
                                 pro[:, 0:8].rearrange("p (l h) -> p l h", l=2),
                                 big.unsqueeze(1).to_broadcast([P, 2, 4]), ALU.subtract))
            V.tensor_copy(lbs[:, 12:20], lbs[:, 4:12]).then_inc(*st.up(mul_ready))
            ve.wait_ge(exp_ready, 1)
            link(V.tensor_tensor(lbs[:, 20:24], lbs[:, 12:16], lbs[:, 16:20], ALU.add))
            link(V.reciprocal(lbs[:, 24:28], lbs[:, 20:24]))
            link(V.tensor_tensor(lbs[:, 12:20].rearrange("p (l h) -> p l h", l=2),
                                 lbs[:, 12:20].rearrange("p (l h) -> p l h", l=2),
                                 lbs[:, 24:28].unsqueeze(1).to_broadcast([P, 2, 4]), ALU.mult))
            link(V.tensor_tensor(lbs[:, 28:32], lbs[:, 12:16], lbs[:, 16:20], ALU.add))
            link(V.tensor_tensor(lbs[:, 32:36], lbs[:, 12:16], lbs[:, 12:16], ALU.subtract))
            link(V.tensor_tensor(lbs[:, 36:40], lbs[:, 28:32], lbs[:, 12:16], ALU.subtract))
            depart(ve, 0)

            def make_h(st, n, gain):
                ve.wait_ge(rs_ready, n)
                for k in range(KD):
                    V.scalar_tensor_tensor(hT[:, k, :], xT[:, k, :], gain[:, k:k + 1], rs[:, 0:T], ALU.mult,
                                           ALU.mult).then_inc(*st.up(h_ready))

            def layer(l):
                st = Steps(ve)

                def link(ins):
                    ins.then_inc(*st.up(dve_step))
                    ve.wait_ge(*st.settled())

                def take(R, name):
                    ve.wait_ge(*R.filled(name))
                    return R.bank(name)

                V.tensor_tensor(sq[:, 0:4, :], xT[:, 0:4, :], xT[:, 0:4, :], ALU.mult).then_inc(*st.up(squares_dve))
                link(V.tensor_copy(lbl[:, 0:4], lbs[:, bass.DynSlice(32 + 4 * l, 4)]))
                link(V.tensor_scalar(lbl[:, 4:8], lbl[:, 0:4], -1.0, 1.0, ALU.mult, ALU.add))
                link(V.tensor_scalar(lbl[:, 0:4], lbl[:, 0:4], 1e-30, None, ALU.max))
                bank = take(AXR, "par")
                V.tensor_copy(prm[:, 0:105], bank[:, 0:105])
                V.tensor_copy(prm[:, P:P + 32], bank[:, P:P + 32]).then_inc(*st.up(ax_dve))
                ve.wait_ge(*st.settled())
                ve.sem_inc(prm_ready, 1)
                make_h(st, 1, prm[:, 0:8])
                bank = take(AXR, "cst")
                V.tensor_copy(cstT[:, :, :].rearrange("p j c -> p (j c)"), bank[:, 0:16 * NJ]).then_inc(*st.up(ax_dve))
                for q in range(1, NSEQ, 2):
                    bank = take(AXR, f"cc{q}")
                    V.tensor_copy(cmpT[:, :, :, q, :].rearrange("p v g t -> p (v g) t"),
                                  bank[:, :].rearrange("p (x t) -> p x t", x=4)).then_inc(*st.up(ax_dve))
                bank = take(AXR, "kt1")
                V.tensor_copy(ktn[:, 1, :], bank[:, 0:T]).then_inc(*st.up(ax_dve))
                for h in range(HH):
                    ve.wait_ge(mm_act, 10 + h + 1)
                    V.tensor_scalar(pH[:, h, :], pH[:, h, :], lbl[:, 4 + h:5 + h], lbl[:, h:h + 1], ALU.mult, ALU.add)
                    V.tensor_scalar(kH[:, h, :], kH[:, h, :], lbl[:, 4 + h:5 + h], None, ALU.mult).then_inc(
                        *st.up(mul_ready))
                for m in range(4):
                    bank = take(AXR, f"nqr{m}")
                    V.tensor_tensor(qT[:, m, :], bank[:, 0:T], con("sinq"), ALU.mult).then_inc(*st.up(ax_dve))
                    link(V.tensor_tensor(qraw[:, m, :], qraw[:, m, :], con("cosq"), ALU.mult))
                    V.tensor_tensor(qT[:, m, :], qT[:, m, :], qraw[:, m, :], ALU.add).then_inc(*st.up(q_ready))
                for h in range(HH):
                    ve.wait_ge(sig_ready, HH + h + 1)
                    V.scalar_tensor_tensor(qH[:, h, :], MM.bank(f"hq{h}")[:, 0:T], HD ** -0.5, sgq[:, h, :], ALU.mult,
                                           ALU.mult).then_inc(*st.up(mul_ready))
                    ve.wait_ge(*st.settled())
                    ve.sem_inc(*st.up(mm_dve))
                ve.sem_inc(*st.up(ql_ready))
                bank = take(AXR, "kcr")
                rot = bank[:, 0:NCS * NCB].rearrange("p (s n) -> p s n", s=NCS)
                V.tensor_tensor(kt1, rot, con("scmp").unsqueeze(1).to_broadcast([P, NCS, NCB]), ALU.mult).then_inc(
                    *st.up(ax_dve))
                link(V.tensor_tensor(kt2, kraw, con("ccmp").unsqueeze(1).to_broadcast([P, NCS, NCB]), ALU.mult))
                V.tensor_tensor(kcT[:, :, :], kt1, kt2, ALU.add).then_inc(*st.up(kc_ready))

                def level_q(kk):
                    m = LEVELS[kk]
                    if m == 0:
                        return
                    if kk >= 2:
                        ve.wait_ge(*AXR.filled(f"lvs{kk - 1}" if LEVELS[kk - 1] < STEPS else f"lv{kk - 1}"))
                    ts = T if m < STEPS else SEQ
                    V.tensor_tensor(qL[:, :, 0:ts], qH[:, :, 0:ts], pH[:, :, 0:ts], ALU.mult).then_inc(
                        *st.up(ql_ready))
                    ve.wait_ge(r_done, kk)
                    ve.wait_ge(*st.settled())
                    if m < STEPS:
                        v = pH[:, :, :].rearrange("p h t -> p (h t)").rearrange("p (n u m) -> p n u m", u=2, m=m)
                        V.tensor_tensor(v[:, :, 1, :], v[:, :, 1, :],
                                        v[:, :, 0, m - 1:m].to_broadcast([P, HH * T // (2 * m), m]),
                                        ALU.mult).then_inc(*st.up(p_done))
                    else:
                        v = pH[:, :, 0:SEQ].rearrange("p h (n u m) -> p h n u m", u=2, m=m)
                        V.tensor_tensor(v[:, :, :, 1, :], v[:, :, :, 1, :],
                                        v[:, :, :, 0, m - 1:m].to_broadcast([P, HH, SEQ // (2 * m), m]),
                                        ALU.mult).then_inc(*st.up(p_done))
                    ve.wait_ge(*st.settled())

                def level_take(kk):
                    bank = take(AXR, f"lv{kk}")
                    a, b = CONST["level"]
                    mask = cst_all[:, a + S1 * kk:a + S1 * kk + S1].bitcast(I32)
                    V.copy_predicated(acc[:, 0:2].rearrange("p i h t -> p (i h) t"),
                                      mask.unsqueeze(1).to_broadcast([P, 8, S1]),
                                      bank[:, :].rearrange("p (x t) -> p x t", t=S1)).then_inc(*st.up(ax_dve))
                    if LEVELS[kk] < STEPS:
                        bank = take(AXR, f"lvs{kk}")
                        V.copy_predicated(acc[0:64, 2], mask[0:64].unsqueeze(1).to_broadcast([64, HH, S1]),
                                          bank[0:64, 0:256].rearrange("p (x t) -> p x t", t=S1)).then_inc(
                                              *st.up(ax_dve))
                    ve.wait_ge(*st.settled())

                def normalise(sm, cols):
                    link(V.tensor_scalar(sm[:, cols], sm[:, cols], 1e-30, None, ALU.max))
                    link(V.reciprocal(sm[:, cols], sm[:, cols]))

                def out_gate(h):
                    ve.wait_ge(sig_ready, 2 * HH + h + 1)
                    V.tensor_tensor(gH[:, h, :], MM.bank(f"hg{h}")[:, 0:T], gH[:, h, :], ALU.mult).then_inc(
                        *st.up(mul_ready))
                    ve.wait_ge(*st.settled())
                    ve.sem_inc(*st.up(mm_dve))

                link(V.memset(acc[:, :, :, :], 0.0))
                def unit_scale(n):
                    i, g = UNITS[n]
                    nk = P * (i + 1)
                    prob, sm = probs[n % 2], smb[n % 2]
                    pc = pcb[n % 2][:, 0:60].rearrange("p (r n) -> p r n", r=GRP)
                    a, b = CONST["c01"]
                    one = cst_all[:, a + NCB * i:a + NCB * i + NCB]
                    ve.wait_ge(exp_ready, n + 1)
                    link(V.tensor_tensor(pc, pc, one.unsqueeze(1).to_broadcast([P, GRP, NCB]), ALU.mult))
                    link(V.tensor_reduce(sm[:, 0:4], pc, AX.X, ALU.add))
                    normalise(sm, slice(0, 12))
                    gate = gts[:, i, :].rearrange("p (b h) -> p b h", b=3)[:, :, 4 * g:4 * g + 4]
                    link(V.tensor_tensor(wt[:, 0:12].rearrange("p (b r) -> p b r", b=3), gate,
                                         sm[:, 0:12].rearrange("p (b r) -> p b r", b=3), ALU.mult))
                    V.tensor_tensor(pc, pc, wt[:, 0:4].unsqueeze(2).to_broadcast([P, GRP, NCB]), ALU.mult)
                    w8 = wt[:, 4:12].rearrange("p (w r) -> p r w", w=2).unsqueeze(3).to_broadcast([P, GRP, 2, nk])
                    V.tensor_tensor(prob[:, :, :, 0:nk], prob[:, :, :, 0:nk], w8, ALU.mult).then_inc(*st.up(scaled))

                def unit_reduce(n):
                    i, g = UNITS[n]
                    nk = P * (i + 1)
                    prob, mx, nm = probs[n % 2], mxb[n % 2], nmb[n % 2]
                    pc = pcb[n % 2][:, 0:60].rearrange("p (r n) -> p r n", r=GRP)
                    if n == 0:
                        ve.wait_ge(*AXR.filled("vc2"))
                    a, b = CONST["causal"]
                    mask = cst_all[:, b - nk:b]
                    for r in range(GRP):
                        bank = take(AXR, f"sc{n}_{r}")
                        for w in range(2):
                            c = 4 * (w + 1) + r
                            last = V.tensor_tensor_reduce(prob[:, r, w, 0:nk], bank[:, 256 * w:256 * w + nk], mask, 1.0,
                                                          -3e38, ALU.add, ALU.max, mx[:, c:c + 1])
                        last.then_inc(*st.up(ax_dve))
                    bank = take(AXR, f"scc{n}")
                    a, b = CONST["cneg"]
                    neg = cst_all[:, a + NCB * i:a + NCB * i + NCB]
                    V.tensor_tensor(pc, bank[:, 0:60].rearrange("p (r n) -> p r n", r=GRP),
                                    neg.unsqueeze(1).to_broadcast([P, GRP, NCB]), ALU.add).then_inc(*st.up(ax_dve))
                    ve.wait_ge(*st.settled())
                    link(V.tensor_reduce(mx[:, 0:4], pc, AX.X, ALU.max))
                    V.tensor_tensor(pc, pc, mx[:, 0:4].unsqueeze(2).to_broadcast([P, GRP, NCB]), ALU.subtract)
                    V.tensor_scalar(nm[:, 0:12], mx[:, 0:12], -SCALE, None, ALU.mult).then_inc(*st.up(max_ready))

                def unit_turned(n):
                    i, g = UNITS[n]
                    for x in range(1, 2 * (i + 1), 2):
                        bank = take(AXR, f"tp{n}_{x}")
                        V.tensor_copy(probT[:, x, :], bank[:, :]).then_inc(*st.up(ax_dve))

                def unit_out(n):
                    i, g = UNITS[n]
                    bank = take(AXR, f"ov{n}")
                    V.tensor_copy(oN[64 * g:64 * g + 64, :, P * i:P * i + P],
                                  bank[64 * g:64 * g + 64, :].rearrange("p (r q) -> p r q", r=GRP)).then_inc(
                                      *st.up(ax_dve))

                def gates_by_row():
                    for hb in range(2):
                        bank = take(AXR, f"gsel{hb}")
                        t3 = gtmp[:, 0:24].rearrange("p (x r) -> p x r", r=GRP)
                        V.tensor_tensor(t3, bank[:, 0:24].rearrange("p (x r) -> p x r", r=GRP),
                                        con("rrow").unsqueeze(1).to_broadcast([P, 6, GRP]), ALU.mult).then_inc(
                                            *st.up(ax_dve))
                        ve.wait_ge(*st.settled())
                        link(V.tensor_reduce(gsel[:, hb, :], t3, AX.X, ALU.add))

                for n in range(4):
                    if n:
                        unit_scale(n - 1)
                    level_take(2 * n)
                    unit_reduce(n)
                    if n:
                        unit_turned(n - 1)
                    if 2 * n + 1 < len(LEVELS):
                        level_q(2 * n + 1)
                    else:
                        link(V.tensor_tensor(qL[:, :, :], qH[:, :, :], pH[:, :, :], ALU.mult))
                        ve.sem_inc(*st.up(ql_ready))
                    if n:
                        unit_out(n - 1)
                        out_gate(n - 1)
                    if 2 * n + 1 < len(LEVELS):
                        level_take(2 * n + 1)
                        level_q(2 * n + 2)
                    if n == 0:
                        gates_by_row()
                    if n == 2:
                        out_gate(3)
                for h in (1, 3):
                    bank = take(AXR, f"krt{h}")
                    V.tensor_copy(krP[:, h].rearrange("p i d -> p (i d)"), bank[:, 0:256])
                    V.tensor_copy(krS[0:SMP, h, :], bank[0:SMP, 256:384]).then_inc(*st.up(ax_dve))
                unit_scale(3)
                for hb in range(2):
                    for x in (1, 3):
                        bank = take(AXR, f"skt{hb}_{x}")
                        V.tensor_copy(kvT[:, x // 2, 2 * (x % 2):2 * (x % 2) + 2, :].rearrange("p b t -> p (b t)"),
                                      bank[:, :]).then_inc(*st.up(ax_dve))
                    if hb == 0:
                        unit_turned(3)
                        unit_out(3)
                    for c in (2 * hb, 2 * hb + 1):
                        bank = take(AXR, f"ds{c}")
                        if c == 0:
                            V.tensor_copy(sP[:, 0].rearrange("p h v -> p (h v)"), bank[:, :]).then_inc(*st.up(s_ready))
                        else:
                            for h in range(HH):
                                end = pH[:, h, S1 * c + S1 - 1:S1 * c + S1]
                                last = V.scalar_tensor_tensor(sP[:, c, h, :], sP[:, c - 1, h, :], end,
                                                              bank[:, P * h:P * h + P], ALU.mult, ALU.add)
                            last.then_inc(*st.up(s_ready))
                        ve.wait_ge(*st.settled())
                        ve.sem_inc(*st.up(ax_dve))
                    for g in range(KVH):
                        n = 4 + 2 * hb + g
                        a, b = CONST["newneg"]
                        mask = cst_all[:, a + SMP * hb:a + SMP * hb + SMP]
                        bank = take(AXR, f"ssb{n}")
                        m1 = mx[:, 4:6]
                        V.tensor_reduce(m1, AXR.bank(f"ssa{n}")[:, :].rearrange("p (w k) -> p w k", w=2), AX.X, ALU.max)
                        for w in range(2):
                            V.tensor_tensor_reduce(snew[:, w, :], bank[:, SMP * w:SMP * w + SMP], mask, 1.0, -3e38,
                                                   ALU.add, ALU.max, mx[:, 6 + w:7 + w])
                        link(V.tensor_reduce(mx[:, 0:1], bank[:, P:P + NCB], AX.X, ALU.max))
                        link(V.tensor_tensor(mx[:, 1:3], mx[:, 4:6], mx[:, 6:8], ALU.max))
                        V.tensor_scalar(nm[:, 0:3], mx[:, 0:3], -SCALE, None, ALU.mult).then_inc(*st.up(max_ready))
                        ve.wait_ge(exp_ready, n + 1)
                        link(V.tensor_tensor(sm[:, 1:3], sm[:, 1:3], sm[:, 3:5], ALU.add))
                        normalise(sm, slice(0, 3))
                        gate = gsel[:, hb, :].rearrange("p (b g) -> p b g", b=3)[:, :, g]
                        link(V.tensor_tensor(wt[:, 0:3], gate, sm[:, 0:3], ALU.mult))
                        V.tensor_scalar(pcs[:, 0:NCB], pcs[:, 0:NCB], wt[:, 0:1], None, ALU.mult)
                        for w in range(2):
                            V.tensor_scalar(snew[:, w, :], snew[:, w, :], wt[:, w + 1:w + 2], None, ALU.mult)
                            last = V.tensor_scalar(sprob[:, w, :], sprob[:, w, :], wt[:, w + 1:w + 2], None, ALU.mult)
                        last.then_inc(*st.up(scaled))
                        bank = take(AXR, f"tps{n}")
                        V.tensor_copy(sprobT[:, :, :].rearrange("p x c -> p (x c)"), bank[:, :]).then_inc(
                            *st.up(ax_dve))
                        bank = take(AXR, f"ov{n}")
                        for b in range(4):
                            t0 = SEQ + STEPS * (4 * hb + b)
                            last = V.tensor_copy(oN[64 * g:64 * g + 64, :, t0:t0 + STEPS],
                                                 bank[64 * g:64 * g + 64, 32 * b:32 * b + 32].rearrange(
                                                     "p (r s) -> p r s", r=GRP))
                        last.then_inc(*st.up(ax_dve))
                def split(u):
                    ve.wait_ge(w_high, u + 1)
                    V.tensor_tensor(unit_of(u, ring_r), unit_of(u, ring), unit_high(u).bitcast(F32),
                                    ALU.subtract).then_inc(*st.up(w_low))

                def low(out, in_, high, sem):
                    V.tensor_tensor(out, in_, high.bitcast(F32), ALU.subtract).then_inc(*st.up(sem))

                ve.wait_ge(r_done, len(LEVELS) + 1)
                for h in range(HH):
                    s0 = slot(f"st{h // 2}")[:, 0:2048].rearrange("p (h b v) -> p h b v", h=2, b=NSEQ)
                    bank = take(AXR, f"o{h}")
                    for c in (0, 2):
                        V.tensor_copy(oS[:, h, S1 * c:S1 * c + S1], bank[:, S1 * c:S1 * c + S1])
                    V.tensor_copy(oS[:, h, SEQ:T], bank[:, SEQ:T]).then_inc(*st.up(ax_dve))
                    bank = take(AXR, f"oo{h}")
                    for c in (1, 3):
                        last = V.tensor_copy(oS[:, h, S1 * c:S1 * c + S1], bank[:, S1 * c:S1 * c + S1])
                    last.then_inc(*st.up(ax_dve))
                    for y, name in enumerate((f"dsa{h}", f"dsb{h}")):
                        bank = take(AXR, name)
                        for b in range(4):
                            q = 4 * y + b
                            end = pH[:, h, SEQ + STEPS * q + STEPS - 1:SEQ + STEPS * q + STEPS]
                            last = V.scalar_tensor_tensor(s0[:, h % 2, q, :], s0[:, h % 2, q, :], end,
                                                          bank[:, P * b:P * b + P], ALU.mult, ALU.add)
                        last.then_inc(*st.up(ax_dve))
                    ve.wait_ge(*st.settled())
                    ve.sem_inc(*st.up(sn_ready))
                    if h == 0:
                        ve.wait_ge(h_hi, 1)
                        ve.wait_ge(*MM.filled("mgb3"))
                        low(h_low, hT, h_high, h_lo)
                    elif h < 3:
                        split(h - 1)
                    else:
                        ve.wait_ge(on_hi, 1)
                        low(oN_low, oN, oN_high, on_ready)
                ve.wait_ge(rso_ready, 1)
                link(V.scalar_tensor_tensor(oS[:, :, :].rearrange("p h t -> p (h t)"),
                                            oS[:, :, :].rearrange("p h t -> p (h t)"), prm[:, 16:17],
                                            rsH[:, :, :].rearrange("p h t -> p (h t)"), ALU.mult, ALU.mult))
                link(V.tensor_tensor(oH[:, :, :], oS[:, :, :], gH[:, :, :], ALU.mult))
                ve.sem_inc(*st.up(oh_raw))
                split(2)
                ve.wait_ge(oh_hi, 1)
                low(oH_low, oH, oH_high, oh_ready)
                split(3)
                def gated(y, n):
                    for m in range(4 * n, 4 * n + 4):
                        ve.wait_ge(mm_act, 17 + 2 * m + 2)
                        bank = take(AXR, f"br{'ab'[y]}{m}")
                        buf = mgs[:, m % MGB, :] if y else merged[:, m, :]
                        V.tensor_tensor(buf, bank[:, 0:T], buf, ALU.mult).then_inc(*st.up(ax_dve))

                def merged_low(n):
                    for m in range(4 * n, 4 * n + 4):
                        ve.wait_ge(m_hi, m + 1)
                        low(m_low[:, m, :], merged[:, m, :], m_high[:, m, :], m_lo)

                gated(1, 0)
                split(4)
                gated(0, 0)
                split(5)
                merged_low(0)
                split(6)
                split(7)
                gated(1, 1)
                split(8)
                gated(0, 1)
                merged_low(1)
                split(9)
                for m in range(KD):
                    bank = take(MM, f"wo{m}")
                    V.tensor_tensor(xT[:, m, :], xT[:, m, :], bank[:, 0:T], ALU.add).then_inc(*st.up(x_ready))
                    ve.wait_ge(*st.settled())
                    ve.sem_inc(*st.up(mm_dve))
                    if m in (1, 3, 5):
                        split(10 + m // 2)
                ve.wait_ge(rs_ready, 2)
                for k in range(KD + 2):
                    if k < KD:
                        V.scalar_tensor_tensor(hT[:, k, :], xT[:, k, :], prm[:, 8 + k:9 + k], rs[:, 0:T], ALU.mult,
                                               ALU.mult).then_inc(*st.up(h_ready))
                    if k >= 2:
                        ve.wait_ge(h_hi, k)
                        low(h_low[:, k - 2, :], hT[:, k - 2, :], h_high[:, k - 2, :], h_lo)
                split(FFU + 1)
                for j in range(NJ):
                    if j:
                        split(FFU + j + 1)
                    gx, cv = gext[j % 2], cvt[j % 2]
                    ve.wait_ge(mm_act, 33 + j + 1)
                    ve.wait_ge(pre_ready, j + 1)
                    gs3 = gx[:, 2 + SEQ:GX].rearrange("p (b s) -> p b s", b=NSEQ)
                    cs3 = cv[:, SEQ:T].rearrange("p (b s) -> p b s", b=NSEQ)
                    for tap in (1, 0):
                        c = 39 + NJ * tap + j
                        V.scalar_tensor_tensor(cv[:, 0:SEQ], gx[:, tap:tap + SEQ], prm[:, c:c + 1], cv[:, 0:SEQ],
                                               ALU.mult, ALU.add)
                        last = V.scalar_tensor_tensor(cs3, gs3[:, :, tap:tap + STEPS], prm[:, c:c + 1], cs3, ALU.mult,
                                                      ALU.add)
                        if tap:
                            link(last)
                    last.then_inc(*st.up(conv_ready))
                    ve.wait_ge(gelu_ready, j + 1)
                    bank = take(MM, f"u{j}")
                    V.tensor_tensor(cv, cv, bank[:, 0:T], ALU.mult).then_inc(*st.up(mm_dve))
                    ve.wait_ge(*st.settled())
                    link(V.tensor_copy(act_high[:, j, :], cv))
                    V.tensor_tensor(act_low[:, j, :], cv, act_high[:, j, :].bitcast(F32), ALU.subtract).then_inc(
                        *st.up(act_ready))
                for u in range(DNU + 1, len(SPLIT)):
                    if u == DNU + 3:
                        for n in range(6):
                            bank = take(AXR, f"cv{n}")
                            w = P * (4 if n < 5 else 2)
                            V.tensor_copy(cvo[0:18, 512 * n:512 * n + w], bank[0:18, 0:w]).then_inc(*st.up(cvo_ready))
                            ve.wait_ge(*st.settled())
                            ve.sem_inc(*st.up(ax_dve))
                    split(u)
                    if u == DNU + 10:
                        for m in range(4):
                            bank = take(MM, f"dn0_{m}")
                            V.tensor_tensor(xT[:, m, :], xT[:, m, :], bank[:, 0:T], ALU.add).then_inc(*st.up(x_ready))
                for m in range(4):
                    bank = take(AXR, f"dn1_{m}")
                    V.tensor_tensor(xT[:, 4 + m, :], xT[:, 4 + m, :], bank[:, 0:T], ALU.add).then_inc(*st.up(x_ready))
                ve.wait_ge(*st.settled())

            with ve.Fori(0, DEPTH) as l:
                layer(l)
                depart(ve, l + 1)
            st = Steps(ve)
            V.tensor_tensor(sq[:, 0:4, :], xT[:, 0:4, :], xT[:, 0:4, :], ALU.mult).then_inc(*st.up(squares_dve))
            make_h(st, 1, pro[:, 8:16])
            n = 0
            for k0 in range(0, KD, 4):
                for i in range(3):
                    ve.wait_ge(mm_full, n + 1)
                    last = V.tensor_copy(yout[0:TM[i], i, P * k0:P * k0 + 512], mmb[n % 4][0:TM[i], :])
                    last.then_inc(*st.up(mm_dve))
                    n += 1
            ve.wait_ge(*st.settled())
            ve.sem_inc(y_ready, 1)

        @block.gpsimd
        def _(po):
            G = nc.gpsimd
            def clear(count):
                po.wait_ge(arrived, count)
                po.sem_inc(spare, 1)
                po.sem_clear(range(nums[0], nums[-1] + 1))
                po.sem_inc(cleared, 1)

            po.wait_ge(consts_in, 32)
            clear(3)

            def layer(l):
                st = Steps(po)

                def link(ins):
                    ins.then_inc(*st.up(pool_step))
                    po.wait_ge(*st.settled())

                def pair_rows(q, src):
                    G.tensor_copy(craw[:, q, :].rearrange("p (x a d) -> p x a d", x=4, a=2),
                                  src.rearrange("p a (x d) -> p x a d", x=4)).then_inc(*st.up(rows_ready))

                po.wait_ge(*landed_at("cmp", l))
                po.sem_inc(spare, 1)
                for q in range(NSEQ):
                    pair_rows(q, slot("cmp").rearrange("p (s a c) -> p s a c", s=NSEQ, a=2)[:, q])
                po.wait_ge(mm_act, 3)
                pair_rows(NSEQ, ctok[:, 0:2, :])
                for i in range(3):
                    n = TM[i]
                    po.wait_ge(mm_act, 3 + i + 1)
                    for w in range(2):
                        x = stok[0:n, i, 256 * w:256 * w + P].rearrange("p (g d) -> p g d", g=2)[:, :, 0:16]
                        tc, ts = (rtmp[0:n, 64 * y:64 * y + 32].rearrange("p (g d) -> p g d", g=2) for y in range(2))
                        a, b = CONST["cosk"]
                        link(G.tensor_tensor(tc, x, cst_all[0:n, a + 16 * i:a + 16 * i + 16].unsqueeze(1).to_broadcast(
                            [n, 2, 16]), ALU.mult))
                        a, b = CONST["sink"]
                        link(G.tensor_tensor(ts, x, cst_all[0:n, a + 16 * i:a + 16 * i + 16].unsqueeze(1).to_broadcast(
                            [n, 2, 16]), ALU.mult))
                        link(G.tensor_tensor(x[:, :, 0:8], tc[:, :, 0:8], ts[:, :, 8:16], ALU.subtract))
                        link(G.tensor_tensor(x[:, :, 8:16], ts[:, :, 0:8], tc[:, :, 8:16], ALU.add))
                    po.sem_inc(*st.up(k_roped))
                po.wait_ge(squares_dve, 1)
                po.wait_ge(*AXR.filled("norm1"))
                link(G.memset(rH[:, :, :], 1.0))
                po.wait_ge(q_ready, 4)
                for b in range(NSEQ):
                    last = G.tensor_copy(qS[:, b], qT[:, :, SEQ + STEPS * b:SEQ + STEPS * (b + 1)])
                last.then_inc(*st.up(qs_ready))
                po.wait_ge(mul_ready, 2 * HH)
                po.sem_inc(*st.up(kl_ready))
                for kk in range(1, len(LEVELS)):
                    m = LEVELS[kk]
                    if m == 1:
                        po.sem_inc(*st.up(kl_ready))
                    else:
                        if m > 2:
                            po.wait_ge(*AXR.filled(f"lvs{kk - 1}" if LEVELS[kk - 1] < STEPS else f"lv{kk - 1}"))
                        ts = T if m < STEPS else SEQ
                        G.tensor_tensor(kL[:, :, 0:ts], kH[:, :, 0:ts], rH[:, :, 0:ts], ALU.mult).then_inc(
                            *st.up(kl_ready))
                    po.wait_ge(*st.settled())
                    if kk > 1:
                        po.wait_ge(p_done, kk - 1)
                    if m < STEPS:
                        r = rH[:, :, :].rearrange("p h t -> p (h t)").rearrange("p (n u m) -> p n u m", u=2, m=m)
                        p_ = pH[:, :, :].rearrange("p h t -> p (h t)").rearrange("p (n u m) -> p n u m", u=2, m=m)
                        link(G.tensor_tensor(r[:, :, 0, :], r[:, :, 0, :],
                                             p_[:, :, 1, m - 1:m].to_broadcast([P, HH * T // (2 * m), m]), ALU.mult))
                    else:
                        for h in range(HH):
                            r = rH[:, h, 0:SEQ].rearrange("p (n u m) -> p n u m", u=2, m=m)
                            p_ = pH[:, h, 0:SEQ].rearrange("p (n u m) -> p n u m", u=2, m=m)
                            last = G.tensor_tensor(r[:, :, 0, :], r[:, :, 0, :],
                                                   p_[:, :, 1, m - 1:m].to_broadcast([P, SEQ // (2 * m), m]), ALU.mult)
                        link(last)
                    po.sem_inc(*st.up(r_done))
                po.wait_ge(*AXR.filled(f"lv{len(LEVELS) - 1}"))
                G.tensor_tensor(kL[:, :, :], kH[:, :, :], rH[:, :, :], ALU.mult).then_inc(*st.up(kl_ready))
                po.wait_ge(*st.settled())
                po.sem_inc(*st.up(r_done))
                po.sem_inc(*st.up(r_done))
                po.wait_ge(mm_act, 17)
                for h in range(HH):
                    if h:
                        po.wait_ge(*AXR.filled(f"dsb{h - 1}"))
                    v = vH[0:SMP, 2, P * h:P * h + P].unsqueeze(1).to_broadcast([SMP, NSEQ, P])
                    G.tensor_tensor(vX[0:SMP], v, con("seqrow", SMP).unsqueeze(2).to_broadcast([SMP, NSEQ, P]),
                                    ALU.mult).then_inc(*st.up(vx_ready))
                for m in range(KD):
                    po.wait_ge(*AXR.emptied_at(f"bra{m}"))
                    G.tensor_tensor(merged[:, m, :], merged[:, m, :], mgs[:, m % MGB, :], ALU.add).then_inc(
                        *st.up(merged_ready))
                po.wait_ge(*MM.filled("wo7"))
                for n in range(2):
                    G.memset(gext[n][:, 0:2], 0.0)
                for j in range(NJ + 1):
                    gx = gext[j % 2]
                    if j < NJ:
                        if j >= 2:
                            po.wait_ge(conv_ready, j - 1)
                        G.tensor_copy(gx[:, 2 + SEQ:GX].rearrange("p (b s) -> p b s", b=NSEQ)[:, :, 0:2],
                                      cstT[:, j, :].rearrange("p (b w) -> p b w", b=NSEQ)).then_inc(*st.up(pre_ready))
                    if j:
                        gp = gext[(j - 1) % 2]
                        po.wait_ge(mm_act, 33 + j)
                        G.tensor_copy(glast[:, j - 1, 0:2], gp[:, SEQ:SEQ + 2])
                        link(G.tensor_copy(glast[:, j - 1, 2:18].rearrange("p (b w) -> p b w", b=NSEQ),
                                           gp[:, 2 + SEQ:GX].rearrange("p (b s) -> p b s", b=NSEQ)[:, :,
                                                                                                STEPS:STEPS + 2]))
                po.sem_inc(glast_ready, 1)

            with po.Fori(0, DEPTH) as l:
                layer(l)
                clear(4 * l + 7)


def shape_constants(np):
    out = np.zeros((P, NCONST), np.float32)

    def put(name, v):
        a, b = CONST[name]
        v = np.asarray(v, np.float32)
        out[:v.shape[0], a:b] = v.reshape(v.shape[0], -1)

    put("ident", np.eye(P))
    put("ones", np.ones((P, P)))
    half = ND // 8
    perm = np.zeros((P, P))
    for g in range(2):
        for d in range(half):
            perm[64 * g + half + d, 64 * g + d] = -1
            perm[64 * g + d, 64 * g + half + d] = 1
    put("perm", perm)
    inv = np.float32(500000.0) ** (-np.arange(half, dtype=np.float32) * np.float32(2.0) / np.float32(2 * half))

    def angles(pos):
        return pos.astype(np.float32)[:, None] * inv[None, :].astype(np.float32)

    pos = np.concatenate([np.arange(SEQ), PAST + np.tile(np.arange(STEPS), NSEQ)])

    def table(pos):
        ang = angles(pos)
        c, s = np.ones((ND, len(pos)), np.float32), np.zeros((ND, len(pos)), np.float32)
        c[:half] = c[half:2 * half] = np.cos(ang).T
        s[:half] = s[half:2 * half] = np.sin(ang).T
        return np.tile(c, (2, 1)), np.tile(s, (2, 1))

    for (cn, sn), ps in ((("cosq", "sinq"), pos), (("ccmp", "scmp"), np.arange(NCB) * 16 + 31)):
        c, s = table(ps)
        put(cn, c)
        put(sn, s)
    ang = angles(np.concatenate([pos, np.zeros(64)])).reshape(3, P, half).transpose(1, 0, 2)
    put("cosk", np.concatenate([np.cos(ang), np.cos(ang)], 2))
    put("sink", np.concatenate([np.sin(ang), np.sin(ang)], 2))
    q = np.arange(P)
    put("causal", np.concatenate([np.zeros((P, P)), np.where(q[None, :] <= q[:, None], 0, NEG)], 1))
    end = np.arange(NCB) * 16 + 31
    ok = np.stack([end[None, :] <= (q[:, None] + P * i) for i in range(2)], 1)
    put("cneg", np.where(ok, 0, NEG))
    put("c01", ok)
    b4, s = q // 32, q % 8
    key = np.arange(SMP)
    put("newneg", np.stack([np.where((key[None, :] // 8 == 4 * hb + b4[:, None]) & (key[None, :] % 8 <= s[:, None]), 0,
                                     NEG) for hb in range(2)], 1))
    ks, qs = np.arange(P)[:, None] % CHUNK, np.arange(CHUNK)[None, :]
    lev = []
    for m in LEVELS:
        if m == 0:
            lev.append(ks == qs)
        else:
            lev.append((ks // (2 * m) == qs // (2 * m)) & (ks % (2 * m) < m) & (qs % (2 * m) >= m))
    put("level", np.stack(lev, 1))
    tok = np.arange(SMP)[:, None]
    put("sel", np.stack([(tok == (4 * hb + b4[None, :]) * 8 + s[None, :]) for hb in range(2)], 1))
    put("seqrow", tok // 8 == np.arange(NSEQ)[None, :])
    put("rrow", (q[:, None] % 32) // 8 == np.arange(GRP)[None, :])
    return out


_INS = ["x_prompt", "x_sample", "cache_cmp_kv", "cache_slc_kv", "cache_win_kv", "state_hgrn", "state_conv", "page_table",
        "norm_mix", "w_in", "hg_lower", "hg_norm", "cmp_pe", "cmp_w1", "cmp_w2", "w_branch", "w_out", "norm_ffn",
        "w_gate_up", "conv_w", "conv_b", "w_down", "norm_final"]
_KV = (2, KVH, ND)
_OUTS = [(1, SEQ, D), (NSEQ, STEPS, D), (DEPTH, 1, SEQ) + _KV, (DEPTH, NSEQ, STEPS) + _KV, (DEPTH, 1, SEQ) + _KV,
         (DEPTH, NSEQ, STEPS) + _KV, (DEPTH, 1, SEQ) + _KV, (DEPTH, NSEQ, PAST) + _KV, (DEPTH, 1, HH, HD, HD),
         (DEPTH, NSEQ, HH, HD, HD), (DEPTH, 1, 2, DFF), (DEPTH, NSEQ, 2, DFF)]


def kernel(**inputs):
    import numpy as np
    import concourse.bacc as bacc
    from concourse.bass_utils import run_bass_kernel_spmd

    nc = bacc.Bacc("TRN2", target_bir_lowering=False, num_devices=1)
    arrays, args = {}, []
    for name in _INS:
        a = np.ascontiguousarray(inputs[name])
        arrays[f"in_{name}"] = a
        args.append(nc.dram_tensor(f"in_{name}", a.shape, mybir.dt.from_np(a.dtype), kind="ExternalInput").ap())
    a = shape_constants(np)
    arrays["in_constants"] = a
    args.append(nc.dram_tensor("in_constants", a.shape, F32, kind="ExternalInput").ap())
    for i, shape in enumerate(_OUTS):
        args.append(nc.dram_tensor(f"out_{i}", shape, F32, kind="ExternalOutput").ap())
    hybrid_step(nc, *args)
    r = run_bass_kernel_spmd(nc, [arrays], core_ids=[0])
    return tuple(r.results[0][f"out_{i}"] for i in range(len(_OUTS)))
```
